# Optimizing a Trainium2 kernel written in Bass

```python
import math
import jax, jax.numpy as jnp
from jax import lax
import numpy as np

D_MODEL = 1024
BATCH = 1
SEQ = 1024
DEPTH = 1

SSM_GROUP = 16
SSM_GROUPS = 32
SSM_WIDTH = SSM_GROUP * SSM_GROUPS
SSM_STATE = 64
HEAD_DIM = 64
HEADS_PER_GROUP = 8
ATTN_PATTERNS = ((128, 1), (512, 4), (2048, 16))
N_ATTN_GROUPS = 3
ATTN_WIDTH = HEADS_PER_GROUP * HEAD_DIM
QKV_WIDTH = N_ATTN_GROUPS * ATTN_WIDTH
QBLK = 128
IN_WIDTH = SSM_WIDTH + 3 * QKV_WIDTH + 2 * D_MODEL
SPLIT_POINTS = (SSM_WIDTH, SSM_WIDTH + QKV_WIDTH, SSM_WIDTH + 2 * QKV_WIDTH,
                SSM_WIDTH + 3 * QKV_WIDTH, SSM_WIDTH + 3 * QKV_WIDTH + D_MODEL)
N_EXPERTS = 64
TOP_K = 8
N_EXPERT_GROUPS = 8
TOPK_GROUPS = 4
EXPERT_HIDDEN = 256
SHARED_HIDDEN = 256
ROUTED_SCALE = 2.5
DISPATCH_BLK = 128
LN_EPS = 1e-5
DEEPNORM_ALPHA = (2 * DEPTH) ** 0.25
DEEPNORM_BETA = (8 * DEPTH) ** -0.25

kernel_name = "s5_dilated_attn_gated_moe_deepnorm"

def layer_norm(x, g, b):
    xf = x.astype(jnp.float32)
    mu = jnp.mean(xf, axis=-1, keepdims=True)
    var = jnp.mean(jnp.square(xf - mu), axis=-1, keepdims=True)
    y = (xf - mu) * lax.rsqrt(var + LN_EPS) * g.astype(jnp.float32) + b.astype(jnp.float32)
    return y.astype(x.dtype)

def swiglu(x, w_gate, w_up, w_down):
    return (jax.nn.silu(x @ w_gate) * (x @ w_up)) @ w_down

def s5_branch(u, lam_re, lam_im, log_dt, b_re, b_im, c_re, c_im, d_skip, w_glu):
    B, L, _ = u.shape
    f32 = jnp.float32
    lam = lax.complex(lam_re.astype(f32), lam_im.astype(f32))
    dt = jnp.exp(log_dt.astype(f32))[:, None]
    lam_bar = jnp.exp(lam * dt)
    b_bar = ((lam_bar - 1.0) / lam)[:, :, None] * lax.complex(b_re.astype(f32), b_im.astype(f32))
    c = lax.complex(c_re.astype(f32), c_im.astype(f32))
    ug = u.astype(f32).reshape(B, L, SSM_GROUPS, SSM_GROUP)
    bu = jnp.einsum('blgc,gpc->blgp', ug.astype(jnp.complex64), b_bar)
    a = jnp.broadcast_to(lam_bar, (1, L) + lam_bar.shape)

    def combine(e1, e2):
        a1, s1 = e1
        a2, s2 = e2
        return a1 * a2, a2 * s1 + s2

    _, states = lax.associative_scan(combine, (a, bu), axis=1)
    y = jnp.real(jnp.einsum('blgp,gcp->blgc', states, c)) + d_skip.astype(f32) * ug
    y = jax.nn.gelu(y.reshape(B, L, SSM_WIDTH))
    y = y * jax.nn.sigmoid(y @ w_glu.astype(f32))
    return y.astype(u.dtype)

def dilated_window_attention(q, k, v, window, dilation):
    B, L, H, Dh = q.shape
    steps = window // dilation
    n = L // dilation
    nb = -(-n // QBLK)
    pad = nb * QBLK - n

    def to_blocks(t):
        t = t.reshape(B, n, dilation, H, Dh).transpose(0, 2, 3, 1, 4)
        t = jnp.pad(t, ((0, 0), (0, 0), (0, 0), (0, pad), (0, 0)))
        return t.reshape(B, dilation, H, nb, QBLK, Dh)

    def with_prev(t):
        prev = jnp.pad(t, ((0, 0), (0, 0), (0, 0), (1, 0), (0, 0), (0, 0)))[:, :, :, :-1]
        return jnp.concatenate([prev, t], axis=4)

    qb = to_blocks(q)
    kc = with_prev(to_blocks(k))
    vc = with_prev(to_blocks(v))
    s = jnp.einsum('bdhnqc,bdhnkc->bdhnqk', qb, kc).astype(jnp.float32) * (HEAD_DIM ** -0.5)
    qi = jnp.arange(QBLK)[:, None]
    kj = jnp.arange(2 * QBLK)[None, :]
    dist = qi + QBLK - kj
    blk = jnp.arange(nb)[:, None, None]
    allowed = (dist >= 0) & (dist <= steps) & (blk * QBLK + kj - QBLK >= 0)
    s = jnp.where(allowed, s, -jnp.inf)
    m = jnp.max(s, axis=-1, keepdims=True)
    p = jnp.exp(s - m)
    denom = jnp.sum(p, axis=-1)
    o = jnp.einsum('bdhnqk,bdhnkc->bdhnqc', p, vc.astype(jnp.float32)) / denom[..., None]
    lse = m[..., 0] + jnp.log(denom)

    def from_blocks(t):
        t = t.reshape((B, dilation, H, nb * QBLK) + t.shape[5:])[:, :, :, :n]
        t = jnp.moveaxis(t, 3, 1)
        return t.reshape((B, L, H) + t.shape[4:])

    return from_blocks(o), from_blocks(lse)

def token_mixer(x, w_in, b_in, lam_re, lam_im, log_dt, b_re, b_im, c_re, c_im, d_skip,
                w_glu, w_br_ssm, w_br_attn, w_out):
    B, L, _ = x.shape
    proj = x @ w_in + b_in
    u, q, k, v, g_ssm, g_attn = jnp.split(proj, SPLIT_POINTS, axis=-1)
    y_ssm = s5_branch(u, lam_re, lam_im, log_dt, b_re, b_im, c_re, c_im, d_skip, w_glu) @ w_br_ssm
    q = q.reshape(B, L, N_ATTN_GROUPS, HEADS_PER_GROUP, HEAD_DIM)
    k = k.reshape(B, L, N_ATTN_GROUPS, HEADS_PER_GROUP, HEAD_DIM)
    v = v.reshape(B, L, N_ATTN_GROUPS, HEADS_PER_GROUP, HEAD_DIM)
    outs, lses = [], []
    for g, (window, dilation) in enumerate(ATTN_PATTERNS):
        o_g, lse_g = dilated_window_attention(q[:, :, g], k[:, :, g], v[:, :, g], window, dilation)
        outs.append(o_g)
        lses.append(lse_g)
    wts = jax.nn.softmax(jnp.stack(lses, axis=0), axis=0)
    y_attn = jnp.einsum('gblh,gblhc->blhc', wts, jnp.stack(outs, axis=0))
    y_attn = y_attn.reshape(B, L, ATTN_WIDTH).astype(x.dtype) @ w_br_attn
    merged = jax.nn.sigmoid(g_ssm) * y_ssm + jax.nn.sigmoid(g_attn) * y_attn
    return merged @ w_out

def moe_ffn(x, router_w, router_bias, w_gate, w_up, w_down, sh_gate, sh_up, sh_down):
    B, L, D = x.shape
    N = B * L
    x2 = x.reshape(N, D)
    scores = jax.nn.sigmoid((x2 @ router_w).astype(jnp.float32))
    sel = scores + router_bias.astype(jnp.float32)
    grp_score = lax.top_k(sel.reshape(N, N_EXPERT_GROUPS, N_EXPERTS // N_EXPERT_GROUPS), 2)[0].sum(-1)
    _, top_grp = lax.top_k(grp_score, TOPK_GROUPS)
    grp_mask = jax.nn.one_hot(top_grp, N_EXPERT_GROUPS).sum(axis=1) > 0
    expert_mask = jnp.repeat(grp_mask, N_EXPERTS // N_EXPERT_GROUPS, axis=1)
    _, idx = lax.top_k(jnp.where(expert_mask, sel, -jnp.inf), TOP_K)
    gates = jnp.take_along_axis(scores, idx, axis=1)
    gates = gates / jnp.sum(gates, axis=-1, keepdims=True) * ROUTED_SCALE
    nk = N * TOP_K
    flat_e = idx.reshape(nk)
    order = jnp.argsort(flat_e)
    sorted_e = flat_e[order]
    tok = (order // TOP_K).astype(jnp.int32)
    gate_sorted = gates.reshape(nk)[order]
    counts = jnp.bincount(flat_e, length=N_EXPERTS)
    start = jnp.cumsum(counts) - counts
    pad_counts = (counts + DISPATCH_BLK - 1) // DISPATCH_BLK * DISPATCH_BLK
    pad_end = jnp.cumsum(pad_counts)
    pad_start = pad_end - pad_counts
    dest = pad_start[sorted_e] + jnp.arange(nk, dtype=jnp.int32) - start[sorted_e]
    n_rows = nk + N_EXPERTS * DISPATCH_BLK
    n_blocks = n_rows // DISPATCH_BLK
    row_tok = jnp.zeros((n_rows,), jnp.int32).at[dest].set(tok)
    row_gate = jnp.zeros((n_rows,), jnp.float32).at[dest].set(gate_sorted)
    blk_e = jnp.minimum(jnp.searchsorted(pad_end, jnp.arange(n_blocks, dtype=jnp.int32) * DISPATCH_BLK,
                                         side='right'), N_EXPERTS - 1)

    def expert_block(acc, blk):
        e, rows, g = blk
        yb = swiglu(x2[rows], w_gate[e], w_up[e], w_down[e])
        return acc.at[rows].add(yb * g[:, None].astype(x2.dtype)), None

    routed, _ = lax.scan(expert_block, jnp.zeros_like(x2),
                         (blk_e, row_tok.reshape(n_blocks, DISPATCH_BLK),
                          row_gate.reshape(n_blocks, DISPATCH_BLK)))
    shared = swiglu(x2, sh_gate, sh_up, sh_down)
    return (routed + shared).reshape(B, L, D)

def setup_inputs(seed: int = 0) -> dict:
    key = jax.random.key(seed)
    ks = jax.random.split(key, 32)
    f32 = jnp.float32
    nrm = lambda k, shape, scale: jax.random.normal(k, shape, f32) * scale
    Dl = DEPTH
    lam_re = -0.5 + nrm(ks[3], (Dl, SSM_GROUPS, SSM_STATE), 0.01)
    lam_im = math.pi * jnp.arange(SSM_STATE, dtype=f32) + nrm(ks[4], (Dl, SSM_GROUPS, SSM_STATE), 0.01)
    log_dt = jax.random.uniform(ks[5], (Dl, SSM_GROUPS), f32, math.log(1e-3), math.log(1e-1))
    return {
        "x": nrm(ks[0], (BATCH, SEQ, D_MODEL), 1.0),
        "w_in": nrm(ks[1], (Dl, D_MODEL, IN_WIDTH), D_MODEL ** -0.5),
        "b_in": nrm(ks[2], (Dl, IN_WIDTH), 0.02),
        "ssm_lam_re": lam_re,
        "ssm_lam_im": lam_im,
        "ssm_log_dt": log_dt,
        "ssm_b_re": nrm(ks[6], (Dl, SSM_GROUPS, SSM_STATE, SSM_GROUP), (2 * SSM_GROUP) ** -0.5),
        "ssm_b_im": nrm(ks[7], (Dl, SSM_GROUPS, SSM_STATE, SSM_GROUP), (2 * SSM_GROUP) ** -0.5),
        "ssm_c_re": nrm(ks[8], (Dl, SSM_GROUPS, SSM_GROUP, SSM_STATE), (2 * SSM_STATE) ** -0.5),
        "ssm_c_im": nrm(ks[9], (Dl, SSM_GROUPS, SSM_GROUP, SSM_STATE), (2 * SSM_STATE) ** -0.5),
        "ssm_d": nrm(ks[10], (Dl, SSM_GROUPS, SSM_GROUP), 1.0),
        "w_glu": nrm(ks[11], (Dl, SSM_WIDTH, SSM_WIDTH), SSM_WIDTH ** -0.5),
        "w_br_ssm": nrm(ks[12], (Dl, SSM_WIDTH, D_MODEL), SSM_WIDTH ** -0.5 * DEEPNORM_BETA),
        "w_br_attn": nrm(ks[13], (Dl, ATTN_WIDTH, D_MODEL), ATTN_WIDTH ** -0.5 * DEEPNORM_BETA),
        "w_out": nrm(ks[14], (Dl, D_MODEL, D_MODEL), D_MODEL ** -0.5 * DEEPNORM_BETA),
        "ln1_g": 1.0 + nrm(ks[15], (Dl, D_MODEL), 0.02),
        "ln1_b": nrm(ks[16], (Dl, D_MODEL), 0.02),
        "router_w": nrm(ks[17], (Dl, D_MODEL, N_EXPERTS), D_MODEL ** -0.5),
        "router_bias": nrm(ks[18], (Dl, N_EXPERTS), 0.01),
        "exp_w_gate": nrm(ks[19], (Dl, N_EXPERTS, D_MODEL, EXPERT_HIDDEN), D_MODEL ** -0.5),
        "exp_w_up": nrm(ks[20], (Dl, N_EXPERTS, D_MODEL, EXPERT_HIDDEN), D_MODEL ** -0.5),
        "exp_w_down": nrm(ks[21], (Dl, N_EXPERTS, EXPERT_HIDDEN, D_MODEL), EXPERT_HIDDEN ** -0.5 * DEEPNORM_BETA),
        "sh_w_gate": nrm(ks[22], (Dl, D_MODEL, SHARED_HIDDEN), D_MODEL ** -0.5),
        "sh_w_up": nrm(ks[23], (Dl, D_MODEL, SHARED_HIDDEN), D_MODEL ** -0.5),
        "sh_w_down": nrm(ks[24], (Dl, SHARED_HIDDEN, D_MODEL), SHARED_HIDDEN ** -0.5 * DEEPNORM_BETA),
        "ln2_g": 1.0 + nrm(ks[25], (Dl, D_MODEL), 0.02),
        "ln2_b": nrm(ks[26], (Dl, D_MODEL), 0.02),
    }

def reference(x, w_in, b_in, ssm_lam_re, ssm_lam_im, ssm_log_dt, ssm_b_re, ssm_b_im, ssm_c_re, ssm_c_im,
              ssm_d, w_glu, w_br_ssm, w_br_attn, w_out, ln1_g, ln1_b, router_w, router_bias,
              exp_w_gate, exp_w_up, exp_w_down, sh_w_gate, sh_w_up, sh_w_down, ln2_g, ln2_b):
    for l in range(DEPTH):
        mix = token_mixer(x, w_in[l], b_in[l], ssm_lam_re[l], ssm_lam_im[l], ssm_log_dt[l],
                          ssm_b_re[l], ssm_b_im[l], ssm_c_re[l], ssm_c_im[l], ssm_d[l],
                          w_glu[l], w_br_ssm[l], w_br_attn[l], w_out[l])
        x = layer_norm(DEEPNORM_ALPHA * x + mix, ln1_g[l], ln1_b[l])
        ffn = moe_ffn(x, router_w[l], router_bias[l], exp_w_gate[l], exp_w_up[l], exp_w_down[l],
                      sh_w_gate[l], sh_w_up[l], sh_w_down[l])
        x = layer_norm(DEEPNORM_ALPHA * x + ffn, ln2_g[l], ln2_b[l])
    return x


_drawn_inputs = setup_inputs


def setup_inputs(seed=0):
    import zlib

    import numpy as np

    out = dict(_drawn_inputs(seed))
    spreads = {}
    factors = {'b_in': 3.845,
     'ssm_lam_re': 64.0,
     'ssm_lam_im': 25.8,
     'ssm_log_dt': 29.304,
     'ssm_b_re': 33.632,
     'ssm_b_im': 36.944,
     'ssm_c_re': 36.496,
     'ssm_c_im': 34.4,
     'ln2_g': 7.869,
     'ln2_b': 7.862}
    for name, (base, spread) in spreads.items():
        noise = np.random.default_rng([zlib.crc32(name.encode()), seed]).standard_normal(out[name].shape)
        drawn = base * np.exp(spread * noise) if base else spread * noise
        out[name] = __import__('jax').numpy.asarray(drawn.astype(out[name].dtype))
    for name, factor in factors.items():
        out[name] = (out[name] * factor).astype(out[name].dtype)
    return out
```

```python
from contextlib import ExitStack

import numpy as np
import concourse.bass as bass
from concourse import mybir

F32 = mybir.dt.float32
F32R = mybir.dt.float32r
BF16 = mybir.dt.bfloat16
FP16 = mybir.dt.float16
I32 = mybir.dt.int32
ALU = mybir.AluOpType
ACT = mybir.ActivationFunctionType
AX = mybir.AxisListType

P = 128
D = 1024
L = 1024
KD = D // P
NT = L // P
SSM_W, SSM_C, SSM_G, SSM_N = 512, 16, 32, 64
PAIRS = SSM_G // 2
T = 8
NCH = L // T
KP0 = (T - 1) * SSM_C
NG, NH, DH = 3, 8, 64
HP = NH // 2
QKV = NG * NH * DH
IN_W = SSM_W + 3 * QKV + 2 * D
C_Q, C_K, C_V, C_GS, C_GA = SSM_W, SSM_W + QKV, SSM_W + 2 * QKV, SSM_W + 3 * QKV, SSM_W + 3 * QKV + D
NB_COL = IN_W // P
ROW = DH + 2
NE, EH = 64, 256
TOPK = 8
CAP = 160
REST = CAP - P
NEG = -1.0e30
ROUND = 1.5 * 2.0 ** 23
ALPHA = 2.0 ** 0.25
LN_EPS = 1e-5


class Chain:

    def __init__(self, eng, sem):
        self.eng, self.sem, self.base, self.n = eng, sem, 0, 0

    def __call__(self, ins):
        ins.then_inc(self.sem, 1)
        self.n += 1

    def sync(self):
        self.eng.wait_ge(self.sem, self.base + self.n)

    def do(self, ins):
        self(ins)
        self.sync()

    def loop(self, i, per_turn):
        self.before, self.n, self.per_turn = self.base + self.n, 0, per_turn
        self.base = self.before + i * per_turn

    def end_loop(self, turns):
        assert self.n == self.per_turn, (self.n, self.per_turn)
        self.base, self.n = self.before + turns * self.per_turn, 0


def mm3(eng, out, lh, ll, rh, rl, first, last):
    eng.matmul(out, lh, rh, start=first, stop=False, skip_group_check=True)
    eng.matmul(out, lh, rl, start=False, stop=False, skip_group_check=True)
    return eng.matmul(out, ll, rh, start=False, stop=last, skip_group_check=True)


class Memory:

    def __init__(self, nc, stack):
        self.nc, self.stack, self.sems = nc, stack, []
        stack.callback(self.clear)

    def clear(self):
        if self.sems:
            self.nc.clear_and_free_semaphores(self.sems)
            self.nc.all_engine_barrier()

    def sb(self, name, shape, dt=F32):
        return self.stack.enter_context(self.nc.sbuf_tensor(name, shape, dt))

    def ps(self, name, shape, dt=F32):
        return self.stack.enter_context(self.nc.psum_tensor(name, shape, dt))

    def sem(self, name):
        self.sems.append(self.nc.alloc_semaphore(name))
        return self.sems[-1]


def constants(nc, m):
    c = {}
    c["ident"] = m.sb("ident", [P, P])
    c["identb"] = m.sb("identb", [P, P], BF16)
    c["mask_band"] = m.sb("mask_band", [P, 2 * P], BF16)
    c["mask_pair"] = m.sb("mask_pair", [P, P], BF16)
    parity = m.sb("parity", [P, 2, P])
    c["ready"] = m.sem("const_ready")
    chain_sem = m.sem("const_chain")

    def write(pool):
        ch = Chain(pool, chain_sem)
        ident, identb, band, pair = (c[n][:, :] for n in ("ident", "identb", "mask_band", "mask_pair"))
        for t in (ident, identb):
            ch(pool.memset(t, 0.0))
        ch(pool.memset(band, 0.0))
        odd, near = parity[:, 0, :], parity[:, 1, :]
        ch(pool.iota(odd, pattern=[[-1, P]], base=0, channel_multiplier=1, allow_small_or_imprecise_dtypes=True))
        ch.sync()
        ch.do(pool.tensor_scalar(odd, odd, 0.5, 0.0, ALU.mult, ALU.add))
        ch.do(pool.tensor_scalar(near, odd, ROUND, -ROUND, ALU.add, ALU.add))
        ch.do(pool.tensor_tensor(odd, odd, near, ALU.subtract))
        ch.do(pool.tensor_tensor(odd, odd, odd, ALU.mult))
        ch.do(pool.tensor_scalar(pair, odd, 4.0 * NEG, 0.0, ALU.mult, ALU.add))
        for t in (ident, identb):
            ch(pool.affine_select(out=t, in_=t, compare_op=ALU.not_equal, fill=1.0, base=0,
                                  pattern=[[-1, P]], channel_multiplier=1))
        ch(pool.affine_select(out=band, in_=band, compare_op=ALU.is_ge, fill=NEG, base=0,
                              pattern=[[1, 2 * P]], channel_multiplier=-1))
        ch(pool.affine_select(out=pair, in_=pair, compare_op=ALU.is_ge, fill=NEG, base=0,
                              pattern=[[-1, P]], channel_multiplier=1))
        ch.sync()
        ch(pool.affine_select(out=band, in_=band, compare_op=ALU.is_ge, fill=NEG, base=P,
                              pattern=[[-1, 2 * P]], channel_multiplier=1))
        ch.sync()
        pool.sem_inc(c["ready"], 1)

    return c, write


def s5_parameters(pool, sem, t, out):
    ch = Chain(pool, sem)
    free = iter(range(24))
    new = lambda: t["scratch"][:, next(free), :]
    dt, er, ph, a, b, c2, n = (new() for _ in range(7))
    bits = t["bits"][:, :]

    def ts(o, i, s1, s2, op0, op1):
        ch.do(pool.tensor_scalar(o, i, s1, s2, op0, op1))

    def tt(o, i, j, op):
        ch.do(pool.tensor_tensor(o, i, j, op))

    def poly(o, x, coefs):
        ts(o, x, coefs[0], coefs[1], ALU.mult, ALU.add)
        for c in coefs[2:]:
            tt(o, o, x, ALU.mult)
            ts(o, o, c, 0.0, ALU.add, ALU.add)

    def exp(o, x):
        ts(a, x, -87.0, 88.0, ALU.max, ALU.min)
        ts(b, a, 1.0 / float(np.log(2.0)), 0.0, ALU.mult, ALU.add)
        ts(n, b, ROUND, -ROUND, ALU.add, ALU.add)
        ts(b, n, -0.693359375, 0.0, ALU.mult, ALU.add)
        tt(a, a, b, ALU.add)
        ts(b, n, 2.12194440e-4, 0.0, ALU.mult, ALU.add)
        tt(a, a, b, ALU.add)
        poly(b, a, [1 / 5040, 1 / 720, 1 / 120, 1 / 24, 1 / 6, 0.5, 1.0, 1.0])
        ts(c2, n, 127.0, 8388608.0, ALU.add, ALU.mult)
        ch.do(pool.tensor_copy(bits, c2))
        tt(o, b, bits.bitcast(F32), ALU.mult)

    lre, lim, ldt = (t["raw"][:, j, :] for j in range(3))
    exp(dt, ldt)
    tt(er, lre, dt, ALU.mult)
    exp(er, er)
    tt(ph, lim, dt, ALU.mult)
    ts(n, ph, 1.0 / (2 * float(np.pi)), 0.0, ALU.mult, ALU.add)
    ts(n, n, ROUND, -ROUND, ALU.add, ALU.add)
    for part in (6.28125, 1.9350051879882812e-3, 3.0199159819e-7):
        ts(b, n, -part, 0.0, ALU.mult, ALU.add)
        tt(ph, ph, b, ALU.add)
    ts(ph, ph, 0.5, 0.0, ALU.mult, ALU.add)
    tt(a, ph, ph, ALU.mult)
    f = float
    from_fact = lambda k: f(1.0 / np.prod(np.arange(1.0, k + 1)))
    poly(b, a, [from_fact(13), -from_fact(11), from_fact(9), -from_fact(7), from_fact(5), -from_fact(3), 1.0])
    tt(b, b, ph, ALU.mult)
    poly(c2, a, [from_fact(12), -from_fact(10), from_fact(8), -from_fact(6), from_fact(4), -0.5, 1.0])
    sn, cs, lbr, lbi, den, m1 = (new() for _ in range(6))
    tt(sn, b, c2, ALU.mult)
    ts(sn, sn, 2.0, 0.0, ALU.mult, ALU.add)
    tt(cs, b, b, ALU.mult)
    ts(cs, cs, -2.0, 1.0, ALU.mult, ALU.add)
    tt(lbr, er, cs, ALU.mult)
    tt(lbi, er, sn, ALU.mult)
    ts(m1, lbr, -1.0, 0.0, ALU.add, ALU.add)
    tt(a, lre, lre, ALU.mult)
    tt(b, lim, lim, ALU.mult)
    tt(den, a, b, ALU.add)
    pool.sem_inc(t["den_ready"], 1)
    pool.wait_ge(t["rden_ready"], 1)
    rden = t["rden"][:, :]
    for o, x, y, op in ((out["fac_re"], m1, lbi, ALU.add), (out["fac_im"], lbi, m1, ALU.subtract)):
        tt(a, x, lre, ALU.mult)
        tt(b, y, lim, ALU.mult)
        tt(a, a, b, op)
        tt(o[:, :], a, rden, ALU.mult)
    pr, pi = out["pow_re"], out["pow_im"]
    ch(pool.memset(pr[:, :, 0], 1.0))
    ch(pool.memset(pi[:, :, 0], 0.0))
    ch(pool.tensor_copy(pr[:, :, 1], lbr))
    ch.do(pool.tensor_copy(pi[:, :, 1], lbi))
    for j in range(2, T + 1):
        tt(a, pr[:, :, j - 1], lbr, ALU.mult)
        tt(b, pi[:, :, j - 1], lbi, ALU.mult)
        tt(pr[:, :, j], a, b, ALU.subtract)
        tt(a, pr[:, :, j - 1], lbi, ALU.mult)
        tt(b, pi[:, :, j - 1], lbr, ALU.mult)
        tt(pi[:, :, j], a, b, ALU.add)
    for j in range(T):
        ch(pool.tensor_copy(out["rpow_re"][:, :, j], pr[:, :, T - 1 - j]))
        ch(pool.tensor_copy(out["rpow_im"][:, :, j], pi[:, :, T - 1 - j]))
    for j, (src, sign) in enumerate(((pr, 1.0), (pr, 1.0), (pi, 1.0), (pi, -1.0))):
        ch(pool.tensor_scalar(out["scan_fac"][:, j // 2, (j % 2) * PAIRS:(j % 2 + 1) * PAIRS],
                              src[:, :, T], sign, 0.0, ALU.mult, ALU.add))
    ch.sync()


def mixer_input(nc, m, cst, io, xT_hi, xT_lo, keep, scr):
    with ExitStack() as stack:
        a = Memory(nc, stack)
        XR = 2
        x_tok = a.sb("x_tok", [P, XR, D])
        w_raw = a.sb("u_w_raw", [P, KD, 256])
        WR = 4
        w_hi = a.sb("u_w_hi", [P, WR, 256], F32R)
        w_lo = a.sb("u_w_lo", [P, WR, 256], F32R)
        bias_u = a.sb("bias_u", [P, SSM_W])
        bias_rows = a.sb("bias_rows", [NB_COL, P])
        u_tok = keep["u_tok"]
        lam_rows = a.sb("lam_rows", [PAIRS, 3, P])
        dt_rows = a.sb("dt_rows", [PAIRS, 2])
        lam_raw = a.sb("lam_raw", [P, 3, PAIRS])
        b_raw = a.sb("b_raw", [P, 2, PAIRS, SSM_C])
        b_bar = a.sb("b_bar", [P, 2, PAIRS, SSM_C])
        c_rows = a.sb("c_rows", [P, 2, 2, P])
        c_col = a.sb("c_col", [P, 2, PAIRS, SSM_C])
        c_pow = a.sb("c_pow", [P, 2, PAIRS, T + 1, SSM_C])
        prod = [keep["ut_all"][:, :], keep["states"][:, :, :, :].rearrange("p r a k -> p (r a k)")]
        scratch = a.sb("lam_scratch", [P, 24, PAIRS])
        bits = a.sb("lam_bits", [P, PAIRS], I32)
        rden = a.sb("rden", [P, PAIRS])
        par = {n: a.sb("s5_" + n, [P, PAIRS, w]) for n, w in
               (("pow_re", T + 1), ("pow_im", T + 1), ("rpow_re", T), ("rpow_im", T))}
        par |= {n: a.sb("s5_" + n, [P, PAIRS]) for n in ("fac_re", "fac_im")}
        par["scan_fac"] = keep["scan_fac"]
        u_stage = a.sb("u_stage", [P, 4, P])
        w_stage = a.sb("w_stage", [P, 2, 2, P])
        w_prod = a.sb("w_prod", [P, 4, 2, P])
        b_pad = a.sb("b_pad", [P, 4, 2, SSM_C])
        ut_stage = a.sb("ut_stage", [P, 4, P])
        wt_stage = a.sb("wt_stage", [P, 2, 2, P])
        k_resp = a.sb("k_resp", [SSM_C, SSM_G, P])
        zeros = a.sb("k_zeros", [SSM_C, (T - 1) * SSM_C])
        d_row = a.sb("d_row", [SSM_C, SSM_G, SSM_C])

        ps_x = a.ps("ps_x", [P, 4, 512])
        ps_u = a.ps("ps_u", [P, NT // 2, 2, 256])
        ld_x = [a.sem(f"ld_x{j}") for j in range(XR)]
        ld_dt, dt_ready = a.sem("ld_dt"), a.sem("dt_ready")
        ld_w, ld_par, ld_bias = a.sem("ld_uw"), a.sem("ld_par"), a.sem("ld_bias")
        x_turned, x_hi_made, x_lo_made = a.sem("x_turned"), a.sem("x_hi_made"), a.sem("x_lo_made")
        p_turned, p_copied = a.sem("p_turned"), a.sem("p_copied")
        w_hi_made, w_lo_made, w_used = a.sem("uw_hi_made"), a.sem("uw_lo_made"), a.sem("uw_used")
        u_evac = a.sem("u_evac")
        den_ready, rden_ready, par_ready = a.sem("den_ready"), a.sem("rden_ready"), a.sem("par_ready")
        pool_ch, dve_ch = a.sem("mi_pool_ch"), a.sem("mi_dve_ch")
        cpow_ready, zero_ready = a.sem("cpow_ready"), a.sem("zero_ready")
        staged, turned, copied_u, copied_w = a.sem("s5_staged"), a.sem("s5_turned"), a.sem("s5_ut"), a.sem("s5_wt")
        k_done, k_copied, v_done, v_copied = a.sem("s5_k"), a.sem("s5_kc"), a.sem("s5_v"), a.sem("s5_vc")
        ut_kept, stored, kd_ready = a.sem("s5_ut_kept"), a.sem("mi_stored"), a.sem("kd_ready")
        ident = cst["ident"]
        x_d = io["x"][0].rearrange("(p s) d -> p s d", s=NT)
        w_d = io["w_in"][0].rearrange("(q k) n -> q k n", k=KD)
        b_row = io["b_in"]
        TURNS = SSM_G // 4
        ps_ut = ps_u[:, 0].rearrange("p a (b c) -> p (a b) c", b=2)
        ps_wt = ps_u[:, 1].rearrange("p a (b c) -> p a b c", b=2)
        ps_k = ps_u[:, 2].rearrange("p a (b c) -> p (a b) c", b=2)
        ps_v = ps_u[:, 3].rearrange("p a (b c) -> p a b c", b=2)
        N_PAR = 1 + 3 + 4

        def split_hi(act, n):
            act.wait_ge(ld_w, 16 * (n // KD + 1))
            if n >= WR:
                act.wait_ge(w_used, n - WR + 1)
            act.activation(w_hi[:, n % WR, :], w_raw[:, n % KD, :], ACT.Copy).then_inc(w_hi_made, 1)

        def s5_operators(dve, ch):
            dve.wait_ge(par_ready, 1)
            fr, fi = (par[n][:, :].unsqueeze(2).broadcast_to((P, PAIRS, SSM_C)) for n in ("fac_re", "fac_im"))
            pb = [prod[j][:, 0:PAIRS * SSM_C].rearrange("p (a c) -> p a c", c=SSM_C) for j in range(2)]
            for part, (o, op) in enumerate(((0, ALU.subtract), (1, ALU.add))):
                ch(dve.tensor_tensor(pb[0], b_raw[:, part, :, :], fr, ALU.mult))
                ch.do(dve.tensor_tensor(pb[1], b_raw[:, 1 - part, :, :], fi, ALU.mult))
                ch.do(dve.tensor_tensor(b_bar[:, part, :, :], pb[0], pb[1], op))
            W4 = (P, PAIRS, T + 1, SSM_C)
            pp = [prod[j][:, 0:PAIRS * (T + 1) * SSM_C].rearrange("p (a t c) -> p a t c", t=T + 1, c=SSM_C) for j in range(2)]
            cc = [c_col[:, j, :, :].unsqueeze(2).broadcast_to(W4) for j in range(2)]
            lr, li = (par[n][:, :, :].unsqueeze(3).broadcast_to(W4) for n in ("pow_re", "pow_im"))
            ch(dve.tensor_tensor(pp[0], cc[0], lr, ALU.mult))
            ch.do(dve.tensor_tensor(pp[1], cc[1], li, ALU.mult))
            ch.do(dve.tensor_tensor(c_pow[:, 0], pp[0], pp[1], ALU.subtract))
            ch(dve.tensor_tensor(pp[0], cc[0], li, ALU.mult))
            ch.do(dve.tensor_tensor(pp[1], cc[1], lr, ALU.mult))
            ch.do(dve.scalar_tensor_tensor(out=c_pow[:, 1], in0=pp[0], scalar=-1.0, in1=pp[1],
                                           op0=ALU.mult, op1=ALU.subtract))
            ch.sync()
            dve.sem_inc(cpow_ready, 1)

        with nc.Block() as block:
            @block.sync
            def _(sp):
                for s in range(NT):
                    if s >= XR:
                        sp.wait_ge(x_turned, 2 * (s - XR + 1))
                    sp.dma_start(x_tok[:, s % XR, :], x_d[:, s, :]).then_inc(ld_x[s % XR], 16)
                    if s == 0:
                        sp.dma_start(w_raw[:, :, :], w_d[:, :, 0:256]).then_inc(ld_w, 16)
                sp.wait_ge(w_hi_made, KD)
                sp.wait_ge(w_lo_made, KD)
                sp.dma_start(w_raw[:, :, :], w_d[:, :, 256:512]).then_inc(ld_w, 16)

                sp.wait_ge(cpow_ready, 1)
                sp.dma_start(scr["c_pow"], c_pow[:, :, :, :, :].rearrange("p a b c d -> p (a b c d)")).then_inc(stored, 16)
                sp.wait_ge(zero_ready, 1)
                sp.dma_start(scr["k_pad"][:, :, 0:KP0], zeros[:, :].unsqueeze(1).broadcast_to((SSM_C, SSM_G, KP0))).then_inc(stored, 16)
                sp.wait_ge(kd_ready, 1)
                sp.dma_start(scr["k_pad"][:, :, KP0:KP0 + P], k_resp[:, :, :]).then_inc(stored, 16)
                sp.wait_ge(stored, 48)

            @block.gpsimd
            def _(pool):
                cst["write"](pool)
                pool.memset(zeros[:, :], 0.0).then_inc(zero_ready, 1)
                pool.memset(b_pad[:, :, :, :], 0.0).then_inc(zero_ready, 1)
                pool.wait_ge(p_copied, N_PAR)
                t = {"raw": lam_raw, "scratch": scratch, "bits": bits, "rden": rden,
                     "den": None, "den_ready": den_ready, "rden_ready": rden_ready}
                s5_parameters(pool, pool_ch, t, par)
                pool.sem_inc(par_ready, 1)
                with pool.Fori(0, TURNS) as it:
                    pool.wait_ge(copied_u, it + 1)
                    pool.tensor_copy(keep["ut_all"][:, bass.ds(it * 512, 512)],
                                     ut_stage[:, :, :].rearrange("p a b -> p (a b)")).then_inc(ut_kept, 1)

            @block.tensor
            def _(pe):
                pe.wait_ge(cst["ready"], 1)
                for s in range(NT):
                    pe.wait_ge(ld_x[s % XR], 16 * (s // XR + 1))
                    for h in range(2):
                        n = 2 * s + h
                        if n >= 4:
                            pe.wait_ge(x_hi_made, n - 3)
                            pe.wait_ge(x_lo_made, n - 3)
                        for j in range(4):
                            ins = pe.transpose(ps_x[:, n % 4, P * j:P * j + P],
                                               x_tok[:, s % XR, 4 * h + j:D:KD], ident[:, :])
                        ins.then_inc(x_turned, 1)
                pe.wait_ge(x_hi_made, 2 * NT)
                pe.wait_ge(x_lo_made, 2 * NT)
                pe.wait_ge(ld_par, 16 * (1 + 2 + 2 + 32 + 1))
                pe.wait_ge(dt_ready, 1)
                pe.transpose(ps_x[:, 0, 0:NB_COL], bias_rows[:, :], ident[0:NB_COL, 0:NB_COL])
                for j in range(3):
                    pe.transpose(ps_x[:, 1, 32 * j:32 * j + PAIRS], lam_rows[:, j, :], ident[0:PAIRS, 0:PAIRS])
                for j in range(4):
                    ins = pe.transpose(ps_x[:, 2, P * j:P * j + P], c_rows[:, j // 2, j % 2, :], ident[:, :])
                ins.then_inc(p_turned, 1)
                for half in range(2):
                    if half:
                        pe.wait_ge(u_evac, NT)
                    for k in range(KD):
                        n = half * KD + k
                        pe.wait_ge(w_hi_made, n + 1)
                        pe.wait_ge(w_lo_made, n + 1)
                        for s in range(NT):
                            ins = mm3(pe, ps_u[:, s // 2, s % 2, :], xT_hi[:, k, s:L:NT], xT_lo[:, k, s:L:NT],
                                      w_hi[:, n % WR, :], w_lo[:, n % WR, :], k == 0 and s % 2 == 0, k == KD - 1)
                        ins.then_inc(w_used, 1)
                pe.wait_ge(u_evac, 2 * NT)
                pe.wait_ge(cpow_ready, 1)
                with pe.Fori(0, TURNS) as it:
                    pe.wait_ge(staged, it + 1)
                    for g in range(4):
                        pe.transpose(ps_ut[:, g, :], u_stage[:, g, :], ident[:, :])
                    for j in range(4):
                        ins = pe.transpose(ps_wt[:, j // 2, j % 2, :], w_stage[:, j // 2, j % 2, :], ident[:, :])
                    ins.then_inc(turned, 1)
                    pe.wait_ge(k_copied, it)
                    for g in range(4):
                        for part in range(2):
                            rhs = c_pow[:, part, bass.ds(2 * it + g // 2, 1), 0:T, :]
                            ins = pe.matmul(ps_k[0:SSM_C, g, :], b_pad[:, g, part, :],
                                            rhs.rearrange("p o t c -> p (o t c)"),
                                            start=(part == 0), stop=(part == 1))
                    ins.then_inc(k_done, 1)
                    pe.wait_ge(copied_u, it + 1)
                    pe.wait_ge(copied_w, it + 1)
                    pe.wait_ge(v_copied, it)
                    for j in range(2):
                        for part in range(2):
                            for g2 in range(2):
                                ins = pe.matmul(ps_v[64 * g2:64 * g2 + 64, j, part, :],
                                                wt_stage[:, j, part, 64 * g2:64 * g2 + 64],
                                                ut_stage[:, 2 * j + g2, :],
                                                start=True, stop=True)
                    ins.then_inc(v_done, 1)

            @block.scalar
            def _(act):
                act.dma_start(bias_u[:, :], b_row[:, 0:SSM_W].broadcast_to((P, SSM_W))).then_inc(ld_bias, 16)
                act.dma_start(bias_rows[:, :], b_row[0].rearrange("(c p) -> c p", p=P)).then_inc(ld_par, 16)
                act.dma_start(lam_rows[:, 0, :], io["ssm_lam_re"][0].rearrange("(a g) n -> a (g n)", g=2)).then_inc(ld_par, 16)
                act.dma_start(lam_rows[:, 1, :], io["ssm_lam_im"][0].rearrange("(a g) n -> a (g n)", g=2)).then_inc(ld_par, 16)
                act.dma_start(dt_rows[:, :], io["ssm_log_dt"][0].rearrange("(a g) -> a g", g=2)).then_inc(ld_dt, 16)
                for j, n in enumerate(("ssm_b_re", "ssm_b_im")):
                    act.dma_start(b_raw[:, j, :, :], io[n][0].rearrange("(a g) n c -> (g n) a c", g=2)).then_inc(ld_par, 16)
                for j, n in enumerate(("ssm_c_re", "ssm_c_im")):
                    for half in range(2):
                        for a8 in range(8):
                            g0 = 2 * (8 * half + a8)
                            act.dma_start(c_rows[16 * a8:16 * a8 + 16, j, half, :].rearrange("c (g n) -> c g n", g=2),
                                          io[n][0, g0:g0 + 2].rearrange("g c n -> c g n")).then_inc(ld_par, 16)
                act.dma_start(d_row[:, :, :], io["ssm_d"].rearrange("o g c -> o (g c)").broadcast_to((SSM_C, SSM_G * SSM_C))
                              .rearrange("p (g c) -> p g c", c=SSM_C)).then_inc(ld_par, 16)
                for n in range(2 * NT):
                    act.wait_ge(x_turned, n + 1)
                    s, h = n // 2, n % 2
                    act.activation(xT_hi[:, 4 * h:4 * h + 4, s:L:NT],
                                   ps_x[:, n % 4, :].rearrange("p (k t) -> p k t", k=4), ACT.Copy).then_inc(x_hi_made, 1)
                    if n == 1:
                        act.wait_ge(ld_dt, 16)
                        act.activation(lam_rows[:, 2, :].rearrange("a (g n) -> a g n", g=2),
                                       dt_rows[:, :].unsqueeze(2).broadcast_to((PAIRS, 2, SSM_N)), ACT.Copy).then_inc(dt_ready, 1)
                        for k in range(WR):
                            split_hi(act, k)
                act.wait_ge(p_turned, 1)
                act.activation(keep["bias_T"][:, :], ps_x[:, 0, 0:NB_COL], ACT.Copy).then_inc(p_copied, 1)
                for j in range(3):
                    act.activation(lam_raw[:, j, :], ps_x[:, 1, 32 * j:32 * j + PAIRS], ACT.Copy).then_inc(p_copied, 1)
                for j in range(4):
                    act.activation(c_col[:, j // 2, 8 * (j % 2):8 * (j % 2) + 8, :],
                                   ps_x[:, 2, P * j:P * j + P].rearrange("p (a c) -> p a c", c=SSM_C), ACT.Copy).then_inc(p_copied, 1)
                for n in range(WR, 2 * KD):
                    split_hi(act, n)
                with act.Fori(0, TURNS) as it:
                    act.wait_ge(turned, it + 1)
                    act.wait_ge(ut_kept, it)
                    act.wait_ge(v_done, it)
                    act.activation(ut_stage[:, :, :], ps_ut, ACT.Copy).then_inc(copied_u, 1)
                    act.activation(wt_stage[:, :, :, :], ps_wt, ACT.Copy).then_inc(copied_w, 1)
                    act.wait_ge(k_done, it + 1)
                    act.activation(k_resp[:, bass.ds(4 * it, 4), :], ps_k[0:SSM_C, :, :], ACT.Copy).then_inc(k_copied, 1)

            @block.vector
            def _(dve):
                ch = Chain(dve, dve_ch)

                def split_lo(n):
                    dve.wait_ge(w_hi_made, n + 1)
                    dve.tensor_tensor(w_lo[:, n % WR, :], w_raw[:, n % KD, :], w_hi[:, n % WR, :].bitcast(F32),
                                      ALU.subtract).then_inc(w_lo_made, 1)

                for n in range(2 * NT):
                    dve.wait_ge(x_hi_made, n + 1)
                    s, h = n // 2, n % 2
                    dve.tensor_tensor(xT_lo[:, 4 * h:4 * h + 4, s:L:NT], ps_x[:, n % 4, :].rearrange("p (k t) -> p k t", k=4),
                                      xT_hi[:, 4 * h:4 * h + 4, s:L:NT].bitcast(F32), ALU.subtract).then_inc(x_lo_made, 1)
                    if n == 4:
                        for k in range(WR):
                            split_lo(k)
                for n in range(WR, KD):
                    split_lo(n)
                dve.wait_ge(den_ready, 1)
                dve.reciprocal(rden[:, :], scratch[:, 11, :]).then_inc(rden_ready, 1)
                dve.wait_ge(ld_bias, 16)
                for half in range(2):
                    dve.wait_ge(w_used, KD * (half + 1))
                    for s in range(NT):
                        dve.tensor_tensor(u_tok[:, s, 256 * half:256 * half + 256], ps_u[:, s // 2, s % 2, :],
                                          bias_u[:, 256 * half:256 * half + 256], ALU.add).then_inc(u_evac, 1)
                    if half == 0:
                        for n in range(KD, 2 * KD):
                            split_lo(n)
                        s5_operators(dve, ch)
                dve.wait_ge(u_evac, 2 * NT)
                dve.wait_ge(zero_ready, 2)
                with dve.Fori(0, TURNS) as it:
                    ch.loop(it, 6)
                    dve.wait_ge(turned, it)
                    dve.wait_ge(k_done, it)
                    for g in range(4):
                        ch(dve.tensor_copy(u_stage[:, g, :].rearrange("p (s c) -> p s c", s=T),
                                           u_tok[:, :, bass.ds(64 * it + 16 * g, 16)]))
                    for j in range(2):
                        for n, (w, part) in enumerate((("re", 0), ("im", 1), ("re", 1), ("im", 0))):
                            ins = dve.tensor_tensor(w_prod[:, n, j, :].rearrange("p (s c) -> p s c", s=T),
                                                    par["rpow_" + w][:, bass.ds(2 * it + j, 1), :].rearrange("p o s -> p (o s)").unsqueeze(2).broadcast_to((P, T, SSM_C)),
                                                    b_bar[:, part, bass.ds(2 * it + j, 1), :].broadcast_to((P, T, SSM_C)), ALU.mult)
                    ch(ins)
                    for g in range(4):
                        for part in range(2):
                            rows = slice(64 * (g % 2), 64 * (g % 2) + 64)
                            ins = dve.tensor_copy(b_pad[rows, g, part, :],
                                                  b_bar[rows, part, bass.ds(2 * it + g // 2, 1), :].rearrange("p o c -> p (o c)"))
                    ch(ins)
                    ch.sync()
                    dve.tensor_tensor(w_stage[:, :, 0, :], w_prod[:, 0, :, :], w_prod[:, 1, :, :], ALU.subtract)
                    dve.tensor_tensor(w_stage[:, :, 1, :], w_prod[:, 2, :, :], w_prod[:, 3, :, :], ALU.add).then_inc(staged, 1)
                    dve.wait_ge(v_done, it + 1)
                    dve.tensor_copy(keep["states"][:, :, bass.ds(2 * it, 2), 1:NCH + 1],
                                    ps_v.rearrange("p a r k -> p r a k")).then_inc(v_copied, 1)
                ch.end_loop(TURNS)
                dve.wait_ge(k_copied, TURNS)
                eye = ident[0:SSM_C, 0:SSM_C].unsqueeze(1).broadcast_to((SSM_C, SSM_G, SSM_C))
                ch.do(dve.tensor_tensor(d_row[:, :, :], d_row[:, :, :], eye, ALU.mult))
                dve.tensor_tensor(k_resp[:, :, 0:SSM_C], k_resp[:, :, 0:SSM_C], d_row[:, :, :],
                                  ALU.add).then_inc(kd_ready, 1)


def attention(nc, m, cst, io, xT_hi, xT_lo, keep, scr):
    with ExitStack() as stack:
        a = Memory(nc, stack)
        WR = 4
        NBLK, NU = 8, 16
        w_raw = a.sb("v_w_raw", [P, KD, 256])
        w_hi = a.sb("v_w_hi", [P, WR, 256], F32R)
        w_lo = a.sb("v_w_lo", [P, WR, 256], F32R)
        bias_v = a.sb("bias_v", [P, 512])
        v_cur = a.sb("v_cur", [P, NBLK, 512])
        qk_raw = [a.sb(n + "_w_raw", [P, KD, P]) for n in "qk"]
        qk_hi = [a.sb(n + "_w_hi", [P, KD, P], F32R) for n in "qk"]
        qk_lo = [a.sb(n + "_w_lo", [P, KD, P], F32R) for n in "qk"]
        nxt = [a.sb(n + "_next", [P, L]) for n in "qk"]
        cur = [a.sb(n + "_cur", [P, L]) for n in "qk"]
        probs = a.sb("probs", [P, 2, 256])
        probs_T = a.sb("probs_T", [P, 2, 256])
        o_stage = a.sb("o_stage", [P, NBLK, 2 * ROW])
        scan_prod = a.sb("scan_prod", [P, 2, 2 * PAIRS])
        ps_st = a.ps("ps_st", [P, 4, 512])
        ps_o = a.ps("ps_o", [P, 2, 512])
        ps_p = a.ps("ps_p", [P, 2, 512])
        ld_vw, ld_bv = a.sem("ld_vw"), a.sem("ld_bv")
        ld_qk = [a.sem("ld_qw"), a.sem("ld_kw")]
        vw_hi_made, vw_lo_made, vw_used, v_evac = a.sem("vw_hi_made"), a.sem("vw_lo_made"), a.sem("vw_used"), a.sem("v_evac")
        qk_hi_made = [a.sem("qw_hi_made"), a.sem("kw_hi_made")]
        qk_lo_made = [a.sem("qw_lo_made"), a.sem("kw_lo_made")]
        proj_done, proj_q_evac, proj_k_evac = a.sem("proj_done"), a.sem("proj_q_evac"), a.sem("proj_k_evac")
        cur_ready = a.sem("cur_ready")
        s_ready, m_ready, p_ready = a.sem("scores_ready"), a.sem("max_ready"), a.sem("probs_ready")
        t_ready = a.sem("turned_ready")
        tc_even, tc_odd = a.sem("probs_T_even"), a.sem("probs_T_odd")
        o_ready, o_evac = a.sem("o_ready"), a.sem("o_evac")
        stored = [a.sem("o_stored_0"), a.sem("o_stored_1")]
        scan_sem = a.sem("scan_chain")
        identb, ident = cst["identb"], cst["ident"]
        w_d = io["w_in"][0].rearrange("(q k) n -> q k n", k=KD)
        b_d = io["b_in"]
        QW = 2

        def has_before(g, blk):
            return (blk > 0, blk >= 4, False)[g]

        def block_before(g, blk):
            return (blk - 1, blk - 4, None)[g]

        def tokens(rows, g, blk, before=False):
            n = 2 * P if before else P
            if g == 0:
                at = P * blk - (P if before else 0)
                return rows[:, at:at + n]
            if g == 1:
                nb, r = divmod(blk, 4)
                at = 512 * nb + r - (512 if before else 0)
                return rows[:, at:at + 4 * (n - 1) + 1:4]
            return rows[:, blk:L:8]


        def unit(u):
            return u // 2, u % 2

        def sp_load_v(sp, g, half):
            sp.dma_start(w_raw[:, :, :], w_d[:, :, C_V + 512 * g + 256 * half:C_V + 512 * g + 256 * half + 256]).then_inc(ld_vw, 16)

        def sp_load_qk(sp, which, h):
            sp.dma_start(qk_raw[which][:, :, :], w_d[:, :, bass.ds((C_Q, C_K)[which] + P * h, P)]).then_inc(ld_qk[which], 16)

        def sp_store(sp, g, hp, half):
            cols = bass.ds(2 * ROW * hp, 2 * ROW)
            rows = scr["att"][g]
            src = o_stage[:, 4 * half:4 * half + 4, :]
            if g == 0:
                dst = rows.rearrange("(b p) c -> p b c", p=P)[:, 4 * half:4 * half + 4, cols]
            elif g == 1:
                dst = rows.rearrange("(b p r) c -> b p r c", b=2, r=4)[half, :, :, cols]
            else:
                dst = rows.rearrange("(p b) c -> p b c", b=8)[:, 4 * half:4 * half + 4, cols]
            sp.dma_start(dst, src).then_inc(stored[half], 16)

        def sp_turn(sp, g, hp, h, ahead):
            for half in range(2):
                if ahead:
                    which = 1 - half
                    sp.wait_ge(qk_lo_made[which], h + 2 + half)
                    sp_load_qk(sp, which, h + 2 + half)
                sp.wait_ge(o_evac, NU * h + 8 * (half + 1))
                sp.wait_ge(p_ready, NU * h + 8 * (half + 1))
                sp_store(sp, g, hp, half)

        def act_split(act, which, n):
            act.wait_ge(ld_qk[which], 16 * n)
            act.wait_ge(proj_done, 4 * (n - 1) - (0 if which else 2)) if not (isinstance(n, int) and n == 1) else None
            act.activation(qk_hi[which][:, :, :], qk_raw[which][:, :, :], ACT.Copy).then_inc(qk_hi_made[which], 1)

        def dve_split(dve, which, n):
            dve.wait_ge(qk_hi_made[which], n)
            dve.tensor_tensor(qk_lo[which][:, :, :], qk_raw[which][:, :, :], qk_hi[which][:, :, :].bitcast(F32),
                              ALU.subtract).then_inc(qk_lo_made[which], 1)

        def pe_project(pe, step, h, steps_per=6):
            quarter, part = divmod(step, 4)
            which, half = divmod(quarter, 2)
            if part == 0:
                if half == 0:
                    pe.wait_ge(qk_lo_made[which], h + 1)
                if which == 0:
                    pe.wait_ge(proj_k_evac, 2 * h)
                else:
                    pe.wait_ge(proj_q_evac, 2 * h + half + 1)
            for k in (2 * part, 2 * part + 1):
                ins = mm3(pe, ps_p[:, quarter % 2, :], qk_hi[which][:, k, :], qk_lo[which][:, k, :],
                          xT_hi[:, k, 512 * half:512 * half + 512], xT_lo[:, k, 512 * half:512 * half + 512],
                          k == 0, k == KD - 1)
            if part == 3:
                ins.then_inc(proj_done, 1)

        def dve_q_evac(dve, half, h):
            dve.wait_ge(proj_done, 4 * h + half + 1)
            dve.tensor_scalar(nxt[0][:, 512 * half:512 * half + 512], ps_p[:, half, :],
                              keep["bias_T"][:, bass.ds(C_Q // P + h, 1)], DH ** -0.5, ALU.add, ALU.mult).then_inc(proj_q_evac, 1)

        def dve_k_evac(dve, half, h):
            dve.wait_ge(proj_done, 4 * h + half + 3)
            dve.tensor_scalar(nxt[1][:, 512 * half:512 * half + 512], ps_p[:, half, :],
                              keep["bias_T"][:, bass.ds(C_K // P + h, 1)], 0.0, ALU.add, ALU.add).then_inc(proj_k_evac, 1)

        def pe_turn(pe, g, hp, h, ahead):
            pe.wait_ge(cur_ready, 2 * h + 2)
            for u in range(NU + 2):
                if u < NU:
                    blk, h2 = unit(u)
                    rows = slice(64 * h2, 64 * h2 + 64)
                    before = has_before(g, blk)
                    out = ps_st[:, u % 2, 0:256 if before else P]
                    if u >= 2:
                        pe.wait_ge(p_ready, NU * h + u - 1)
                    mask = cst["mask_pair"][:, :] if g == 2 else cst["mask_band"][:, 0 if before else P:2 * P]
                    pe.matmul(out, identb[:, :], mask, start=True, stop=False, skip_group_check=True)
                    pe.matmul(out, tokens(cur[0][rows, :], g, blk), tokens(cur[1][rows, :], g, blk, before),
                              start=False, stop=True, skip_group_check=True).then_inc(s_ready, 1)
                    if ahead:
                        pe_project(pe, u, h + 1)
                if 1 <= u <= NU:
                    v = u - 1
                    blk, h2 = unit(v)
                    pe.wait_ge(p_ready, NU * h + v + 1)
                    if v >= 2:
                        pe.wait_ge((tc_even, tc_odd)[v % 2], 8 * h + v // 2)
                    for j in range(2 if has_before(g, blk) else 1):
                        ins = pe.transpose(ps_st[:, 2 + v % 2, P * j:P * j + P], probs[:, v % 2, P * j:P * j + P], ident[:, :])
                    ins.then_inc(t_ready, 1)
                if u >= 2:
                    v = u - 2
                    blk, h2 = unit(v)
                    pe.wait_ge((tc_even, tc_odd)[v % 2], 8 * h + v // 2 + 1)
                    pe.wait_ge(o_evac, NU * h + max(0, v - 1))
                    blocks = [block_before(g, blk), blk] if has_before(g, blk) else [blk]
                    for j, kb in enumerate(blocks):
                        ins = pe.matmul(ps_o[:, v % 2, 0:DH], probs_T[:, v % 2, P * j:P * j + P],
                                        v_cur[:, kb, bass.ds(P * hp + DH * h2, DH)],
                                        start=(j == 0), stop=(j == len(blocks) - 1))
                    ins.then_inc(o_ready, 1)

        def dve_turn(dve, g, hp, h, ahead):
            dve.wait_ge(s_ready, NU * h)
            dve.wait_ge(proj_q_evac, 2 * h + 2)
            dve.tensor_copy(cur[0][:, :], nxt[0][:, :]).then_inc(cur_ready, 1)
            for u in range(NU + 2):
                if u < NU:
                    blk, h2 = unit(u)
                    n = 256 if has_before(g, blk) else P
                    if u % 8 == 0:
                        dve.wait_ge(stored[u // 8], 16 * h)
                    dve.wait_ge(s_ready, NU * h + u + 1)
                    dve.tensor_reduce(o_stage[:, blk, ROW * h2 + DH + 1:ROW * h2 + DH + 2], ps_st[:, u % 2, 0:n],
                                      AX.X, ALU.max, negate=True).then_inc(m_ready, 1)
                if 1 <= u <= NU and (u - 1) % 2:
                    v = u - 1
                    n = 256 if has_before(g, unit(v)[0]) else P
                    dve.wait_ge(t_ready, NU * h + v + 1)
                    if v >= 2:
                        dve.wait_ge(o_ready, NU * h + v - 1)
                    dve.tensor_copy(probs_T[:, 1, 0:n], ps_st[:, 3, 0:n]).then_inc(tc_odd, 1)
                if u >= 2:
                    v = u - 2
                    blk, h2 = unit(v)
                    dve.wait_ge(o_ready, NU * h + v + 1)
                    dve.tensor_copy(o_stage[:, blk, ROW * h2:ROW * h2 + DH], ps_o[:, v % 2, 0:DH]).then_inc(o_evac, 1)
                if ahead:
                    if u == 1:
                        dve_split(dve, 1, h + 2)
                    if u == 10:
                        dve_split(dve, 0, h + 3)
                    if u in (4, 8):
                        dve_q_evac(dve, u // 4 - 1, h + 1)
                    if u in (12, 16):
                        dve_k_evac(dve, u // 4 - 3, h + 1)

        def act_turn(act, g, hp, h, ahead):
            act.wait_ge(s_ready, NU * h)
            act.wait_ge(proj_k_evac, 2 * h + 2)
            act.activation(cur[1][:, :], nxt[1][:, :], ACT.Copy).then_inc(cur_ready, 1)
            for u in range(NU + 1):
                if u < NU:
                    blk, h2 = unit(u)
                    n = 256 if has_before(g, blk) else P
                    act.wait_ge(m_ready, NU * h + u + 1)
                    if u >= 2:
                        act.wait_ge(t_ready, NU * h + u - 1)
                    at = ROW * h2 + DH
                    act.activation(probs[:, u % 2, 0:n], ps_st[:, u % 2, 0:n], ACT.Exp,
                                   bias=o_stage[:, blk, at + 1:at + 2],
                                   accum_out=o_stage[:, blk, at:at + 1]).then_inc(p_ready, 1)
                if u >= 1 and (u - 1) % 2 == 0:
                    v = u - 1
                    n = 256 if has_before(g, unit(v)[0]) else P
                    act.wait_ge(t_ready, NU * h + v + 1)
                    if v >= 2:
                        act.wait_ge(o_ready, NU * h + v - 1)
                    act.activation(probs_T[:, 0, 0:n], ps_st[:, 2, 0:n], ACT.Copy).then_inc(tc_even, 1)
                if ahead:
                    if u == 0:
                        act_split(act, 1, h + 2)
                    if u == 9:
                        act_split(act, 0, h + 3)

        def turns(eng, g, turn):
            n = HP if g < NG - 1 else HP - 1
            with eng.Fori(0, n) as hp:
                turn(eng, g, hp, HP * g + hp, True)
            if n < HP:
                turn(eng, g, n, HP * g + n, False)

        with nc.Block() as block:
            @block.sync
            def _(sp):
                sp_load_qk(sp, 0, 0)
                sp_load_qk(sp, 1, 0)
                sp_load_v(sp, 0, 0)
                for which, n in ((0, 1), (1, 1), (0, 2)):
                    sp.wait_ge(qk_lo_made[which], n)
                    sp_load_qk(sp, which, n)
                for g in range(NG):
                    sp.wait_ge(vw_lo_made, 2 * KD * g + KD)
                    sp_load_v(sp, g, 1)
                    sp.wait_ge(v_evac, 8 * g + 4)
                    if g + 1 < NG:
                        sp.wait_ge(vw_lo_made, 2 * KD * (g + 1))
                        sp_load_v(sp, g + 1, 0)
                    turns(sp, g, sp_turn)
                for half in range(2):
                    sp.wait_ge(stored[half], 16 * NG * HP)

            @block.tensor
            def _(pe):
                for step in range(16):
                    pe_project(pe, step, 0)
                for g in range(NG):
                    for half in range(2):
                        if g or half:
                            pe.wait_ge(v_evac, 8 * g + 4 * half)
                        if g and not half:
                            pe.wait_ge(o_evac, NU * HP * g)
                            pe.wait_ge(tc_odd, 8 * HP * g)
                        for k in range(KD):
                            n = 2 * KD * g + KD * half + k
                            pe.wait_ge(vw_lo_made, n + 1)
                            for blk in range(NBLK):
                                lhs = [tokens(x[:, k, :], g, blk) for x in (xT_hi, xT_lo)]
                                ins = mm3(pe, ps_st[:, blk // 2, 256 * (blk % 2):256 * (blk % 2) + 256], lhs[0], lhs[1],
                                          w_hi[:, n % WR, :], w_lo[:, n % WR, :], k == 0 and blk % 2 == 0, k == KD - 1)
                            ins.then_inc(vw_used, 1)
                    pe.wait_ge(v_evac, 8 * (g + 1))
                    turns(pe, g, pe_turn)

            @block.scalar
            def _(act):
                act_split(act, 0, 1)
                act_split(act, 1, 1)
                act_split(act, 0, 2)
                for g in range(NG):
                    if g:
                        act.wait_ge(v_evac, 8 * g)
                    act.dma_start(bias_v[:, :], b_d[:, C_V + 512 * g:C_V + 512 * g + 512].broadcast_to((P, 512))).then_inc(ld_bv, 16)
                    for n in range(2 * KD * g, 2 * KD * (g + 1)):
                        act.wait_ge(ld_vw, 16 * (n // KD + 1))
                        if n >= WR:
                            act.wait_ge(vw_used, n - WR + 1)
                        act.activation(w_hi[:, n % WR, :], w_raw[:, n % KD, :], ACT.Copy).then_inc(vw_hi_made, 1)
                    turns(act, g, act_turn)

            @block.vector
            def _(dve):
                dve_split(dve, 0, 1)
                dve_split(dve, 1, 1)
                for half in range(2):
                    dve_q_evac(dve, half, 0)
                for half in range(2):
                    dve_k_evac(dve, half, 0)
                dve_split(dve, 0, 2)
                for g in range(NG):
                    for half in range(2):
                        for n in range(2 * KD * g + KD * half, 2 * KD * g + KD * half + KD):
                            dve.wait_ge(vw_hi_made, n + 1)
                            dve.tensor_tensor(w_lo[:, n % WR, :], w_raw[:, n % KD, :], w_hi[:, n % WR, :].bitcast(F32),
                                              ALU.subtract).then_inc(vw_lo_made, 1)
                        dve.wait_ge(vw_used, 2 * KD * g + KD * (half + 1))
                        dve.wait_ge(ld_bv, 16 * (g + 1))
                        bias = bias_v[:, 256 * half:256 * half + 256].unsqueeze(1).broadcast_to((P, 2, 256))
                        for j in range(4):
                            dve.tensor_tensor(v_cur[:, 2 * j:2 * j + 2, 256 * half:256 * half + 256],
                                              ps_st[:, j, :].rearrange("p (b c) -> p b c", b=2), bias, ALU.add).then_inc(v_evac, 1)
                    turns(dve, g, dve_turn)

            @block.gpsimd
            def _(pool):
                ch = Chain(pool, scan_sem)
                st = keep["states"][:, :, :, :].rearrange("p r a k -> p (r a) k")
                fac = keep["scan_fac"]
                ch.do(pool.memset(st[:, :, 0:1], 0.0))
                with pool.Fori(2, NCH + 1) as k:
                    ch.loop(k - 2, 4)
                    now = lambda lo, hi: st[:, lo:hi, bass.ds(k, 1)]
                    before = st[:, :, bass.ds(k - 1, 1)].rearrange("p a o -> p (a o)").unsqueeze(1).broadcast_to((P, 2, 2 * PAIRS))
                    col = lambda j, lo, hi: scan_prod[:, j, lo:hi].unsqueeze(2)
                    ch.do(pool.tensor_tensor(scan_prod[:, :, :], fac[:, :, :], before, ALU.mult))
                    ch.do(pool.tensor_tensor(now(0, 2 * PAIRS), now(0, 2 * PAIRS), col(0, 0, 2 * PAIRS), ALU.add))
                    ch(pool.tensor_tensor(now(PAIRS, 2 * PAIRS), now(PAIRS, 2 * PAIRS), col(1, 0, PAIRS), ALU.add))
                    ch.do(pool.tensor_tensor(now(0, PAIRS), now(0, PAIRS), col(1, PAIRS, 2 * PAIRS), ALU.add))
                ch.end_loop(NCH - 1)


def branch_outputs(nc, m, cst, io, keep, scr, ya_hi, ya_lo, y_tok):
    with ExitStack() as stack:
        a = Memory(nc, stack)
        c_pow = a.sb("c_pow_in", [P, 2, PAIRS, T + 1, SSM_C])
        k_op = a.sb("k_op", [P, SSM_G, P])
        att = a.sb("att_in", [P, 2, NG, NH * ROW])
        wts = a.sb("att_wts", [P, 2, 4, NG, NH])
        low = a.sb("att_low", [P, 2, NH])
        den = a.sb("att_den", [P, 2, 2, NH])
        y_att = a.sb("y_att", [P, 2, NH * DH])
        ps_y = a.ps("ps_y", [P, 2, 2, 512])
        ps_a = a.ps("ps_a", [P, 2, 512])
        ld_c, ld_k, ld_att = a.sem("ld_cpow"), a.sem("ld_kop"), [a.sem("ld_att0"), a.sem("ld_att1")]
        y_done, y_evac = a.sem("y_done"), a.sem("y_evac")
        shift_ready, exp_ready, wts_ready, parts_ready = a.sem("shift_ready"), a.sem("exp_ready"), a.sem("wts_ready"), a.sem("parts_ready")
        ya_ready, ya_turned, ya_hi_made, ya_lo_made = a.sem("ya_ready"), a.sem("ya_turned"), a.sem("ya_hi_made"), a.sem("ya_lo_made")
        dve_sem = a.sem("bo_dve_ch")
        ident = cst["ident"]
        att_d = scr["att"].rearrange("g (p s) c -> p s g c", s=NT)
        ut, st = keep["ut_all"], keep["states"]
        TURNS = SSM_G // 4

        with nc.Block() as block:
            @block.sync
            def _(sp):
                sp.dma_start(c_pow[:, :, :, :, :].rearrange("p a b c d -> p (a b c d)"), scr["c_pow"]).then_inc(ld_c, 16)
                for s in range(T):
                    sp.dma_start(k_op[SSM_C * s:SSM_C * s + SSM_C, :, :],
                                 scr["k_pad"][:, :, KP0 - SSM_C * s:KP0 - SSM_C * s + P]).then_inc(ld_k, 16)
                for s in range(NT):
                    if s >= 2:
                        sp.wait_ge(ya_ready, s - 1)
                    sp.dma_start(att[:, s % 2, :, :], att_d[:, s, :, :]).then_inc(ld_att[s % 2], 16)

            @block.tensor
            def _(pe):
                pe.wait_ge(ld_c, 16)
                pe.wait_ge(ld_k, 16 * T)
                def merged(s):
                    pe.wait_ge(ya_ready, s + 1)
                    if s >= 2:
                        pe.wait_ge(ya_hi_made, s - 1)
                        pe.wait_ge(ya_lo_made, s - 1)
                    for c in range(4):
                        ins = pe.transpose(ps_a[:, s % 2, P * c:P * c + P], y_att[:, s % 2, P * c:P * c + P], ident[:, :])
                    ins.then_inc(ya_turned, 1)
                for it in range(TURNS):
                    if it == 2:
                        for s in range(NT):
                            merged(s)
                    if it >= 2:
                        pe.wait_ge(y_evac, it - 1)
                    for j in range(4):
                        g = 4 * it + j
                        pair, rows = g // 2, slice(64 * (g % 2), 64 * (g % 2) + 64)
                        out = ps_y[:, it % 2, j % 2, P * (j // 2):P * (j // 2) + P]
                        pe.matmul(out, ut[:, P * g:P * g + P], k_op[:, g, :], start=True, stop=False)
                        for part in range(2):
                            ins = pe.matmul(out, st[rows, part, pair, 0:NCH],
                                            c_pow[rows, part, pair, 1:T + 1, :].rearrange("p t c -> p (t c)"),
                                            start=False, stop=(part == 1))
                    ins.then_inc(y_done, 1)

            @block.scalar
            def _(act):
                for s in range(NT + 2):
                    if s < NT:
                        act.wait_ge(shift_ready, s + 1)
                        if s >= 2:
                            act.wait_ge(wts_ready, s - 1)
                        act.activation(wts[:, s % 2, 1, :, :], wts[:, s % 2, 0, :, :], ACT.Exp, scale=-1.0).then_inc(exp_ready, 1)
                    if s >= 2:
                        n = s - 2
                        act.wait_ge(ya_turned, n + 1)
                        act.activation(ya_hi[:, :, n:L:NT], ps_a[:, n % 2, :].rearrange("p (c t) -> p c t", c=4), ACT.Copy).then_inc(ya_hi_made, 1)
                for it in range(TURNS):
                    act.wait_ge(y_done, it + 1)
                    for g2 in range(2):
                        out = y_tok[:, :, 64 * it:64 * it + 64].rearrange("p t (a g c) -> p g a t c", a=2, g=2)[:, g2]
                        ins = act.activation(out, ps_y[:, it % 2, g2, 0:2 * P].rearrange("p (a t c) -> p a t c", a=2, t=T),
                                             ACT.Gelu_apprx_tanh)
                    ins.then_inc(y_evac, 1)

            @block.vector
            def _(dve):
                ch = Chain(dve, dve_sem)

                def weigh(s):
                    b = s % 2
                    tile = att[:, b, :, :].rearrange("p g (h c) -> p g h c", c=ROW)
                    dve.wait_ge(ld_att[b], 16 * (s // 2 + 1))
                    neg = tile[:, :, :, DH + 1]
                    ch.do(dve.tensor_tensor(low[:, b, :], neg[:, 0], neg[:, 1], ALU.min))
                    ch.do(dve.tensor_tensor(low[:, b, :], low[:, b, :], neg[:, 2], ALU.min))
                    dve.tensor_tensor(wts[:, b, 0, :, :], neg, low[:, b, :].unsqueeze(1).broadcast_to((P, NG, NH)),
                                      ALU.subtract).then_inc(shift_ready, 1)
                    dve.wait_ge(exp_ready, s + 1)
                    ch.do(dve.tensor_tensor(wts[:, b, 2, :, :], wts[:, b, 1, :, :], tile[:, :, :, DH], ALU.mult))
                    ch.do(dve.tensor_tensor(den[:, b, 0, :], wts[:, b, 2, 0, :], wts[:, b, 2, 1, :], ALU.add))
                    ch.do(dve.tensor_tensor(den[:, b, 0, :], den[:, b, 0, :], wts[:, b, 2, 2, :], ALU.add))
                    ch.do(dve.reciprocal(den[:, b, 1, :], den[:, b, 0, :]))
                    if s >= 2:
                        dve.wait_ge(parts_ready, s - 1)
                    dve.tensor_tensor(wts[:, b, 3, :, :], wts[:, b, 1, :, :],
                                      den[:, b, 1, :].unsqueeze(1).broadcast_to((P, NG, NH)), ALU.mult).then_inc(wts_ready, 1)

                def add(s):
                    b = s % 2
                    dve.wait_ge(parts_ready, s + 1)
                    v = att[:, b, :, :].rearrange("p g (h c) -> p g h c", c=ROW)[:, :, :, 0:DH]
                    out = y_att[:, b, :].rearrange("p (h c) -> p h c", c=DH)
                    if s >= 2:
                        dve.wait_ge(ya_turned, s - 1)
                    ch.do(dve.tensor_tensor(out, v[:, 0], v[:, 1], ALU.add))
                    dve.tensor_tensor(out, out, v[:, 2], ALU.add).then_inc(ya_ready, 1)

                def split(s):
                    dve.wait_ge(ya_hi_made, s + 1)
                    dve.tensor_tensor(ya_lo[:, :, s:L:NT], ps_a[:, s % 2, :].rearrange("p (c t) -> p c t", c=4),
                                      ya_hi[:, :, s:L:NT].bitcast(F32), ALU.subtract).then_inc(ya_lo_made, 1)

                for s in range(NT + 2):
                    if s < NT:
                        weigh(s)
                    if 1 <= s <= NT:
                        add(s - 1)
                    if s >= 2:
                        split(s - 2)

            @block.gpsimd
            def _(pool):
                for s in range(NT):
                    b = s % 2
                    pool.wait_ge(wts_ready, s + 1)
                    tile = att[:, b, :, :].rearrange("p g (h c) -> p g h c", c=ROW)
                    for g in range(NG):
                        ins = pool.tensor_tensor(tile[:, g, :, 0:DH], tile[:, g, :, 0:DH],
                                                 wts[:, b, 3, g, :].unsqueeze(2).broadcast_to((P, NH, DH)), ALU.mult)
                    ins.then_inc(parts_ready, 1)


def gated_ssm(nc, m, cst, io, y_tok, y_T, y_hi, y_lo):
    with ExitStack() as stack:
        a = Memory(nc, stack)
        sig = y_tok.rearrange("p s c -> p (s c)").rearrange("p (k t) -> p k t", k=4)
        w_raw = a.sb("glu_raw", [P, 4, SSM_W])
        w_hi, w_lo = a.sb("glu_hi", [P, 4, SSM_W], F32R), a.sb("glu_lo", [P, 4, SSM_W], F32R)
        ps = a.ps("ps_glu", [P, 4, 512])
        ps_z = a.ps("ps_z", [P, 2, 512])
        ld, w_hi_made, w_lo_made = a.sem("ld_glu"), a.sem("glu_hi_made"), a.sem("glu_lo_made")
        turned, y_hi_made, y_lo_made = a.sem("glu_turned"), a.sem("glu_y_hi"), a.sem("glu_y_lo")
        z_done, sig_made, y2_made, y2_split = a.sem("glu_z"), a.sem("glu_sig_made"), a.sem("glu_y2_made"), a.sem("glu_y2_split")
        y2_hi_made = a.sem("glu_y2_hi")
        ident = cst["ident"]
        tile = lambda t, s: t[:, :, s:L:NT]
        bank = lambda s: ps[:, s % 4, :].rearrange("p (c t) -> p c t", c=4)
        part = lambda t, n: t[:, n // 2, 512 * (n % 2):512 * (n % 2) + 512]
        with nc.Block() as block:
            @block.sync
            def _(sp):
                sp.dma_start(w_raw[:, :, :], io["w_glu"][0].rearrange("(c p) n -> p c n", p=P)).then_inc(ld, 16)

            @block.tensor
            def _(pe):
                for s in range(NT):
                    if s >= 4:
                        pe.wait_ge(y_lo_made, s - 3)
                    for c in range(4):
                        ins = pe.transpose(ps[:, s % 4, P * c:P * c + P], y_tok[:, s, P * c:P * c + P], ident[:, :])
                    ins.then_inc(turned, 1)
                pe.wait_ge(w_lo_made, 1)
                pe.wait_ge(y_lo_made, NT)
                for n in range(8):
                    if n >= 2:
                        pe.wait_ge(sig_made, n - 1)
                    c, half = n // 2, slice(512 * (n % 2), 512 * (n % 2) + 512)
                    for k in range(4):
                        ins = mm3(pe, ps_z[:, n % 2, :], w_hi[:, k, P * c:P * c + P], w_lo[:, k, P * c:P * c + P],
                                  y_hi[:, k, half], y_lo[:, k, half], k == 0, k == 3)
                    ins.then_inc(z_done, 1)

            @block.scalar
            def _(act):
                act.wait_ge(ld, 16)
                act.activation(w_hi[:, :, :], w_raw[:, :, :], ACT.Copy).then_inc(w_hi_made, 1)
                for s in range(NT):
                    act.wait_ge(turned, s + 1)
                    act.activation(tile(y_hi, s), bank(s), ACT.Copy).then_inc(y_hi_made, 1)
                for n in range(8):
                    act.wait_ge(z_done, n + 1)
                    act.activation(part(sig, n), ps_z[:, n % 2, :], ACT.Sigmoid).then_inc(sig_made, 1)
                act.wait_ge(z_done, 8)
                for n in range(8):
                    act.wait_ge(y2_made, n + 1)
                    act.activation(part(y_hi, n), part(y_T, n), ACT.Copy).then_inc(y2_hi_made, 1)

            @block.vector
            def _(dve):
                for s in range(NT):
                    dve.wait_ge(y_hi_made, s + 1)
                    dve.tensor_copy(tile(y_T, s), bank(s))
                    dve.tensor_tensor(tile(y_lo, s), bank(s), tile(y_hi, s).bitcast(F32), ALU.subtract).then_inc(y_lo_made, 1)
                    if s == 3:
                        dve.wait_ge(w_hi_made, 1)
                        dve.tensor_tensor(w_lo[:, :, :], w_raw[:, :, :], w_hi[:, :, :].bitcast(F32), ALU.subtract).then_inc(w_lo_made, 1)
                dve.wait_ge(y_lo_made, NT)
                for n in range(8):
                    dve.wait_ge(sig_made, n + 1)
                    dve.tensor_tensor(part(y_T, n), part(y_T, n), part(sig, n), ALU.mult).then_inc(y2_made, 1)
                for n in range(8):
                    dve.wait_ge(y2_hi_made, n + 1)
                    dve.tensor_tensor(part(y_lo, n), part(y_T, n), part(y_hi, n).bitcast(F32), ALU.subtract).then_inc(y2_split, 1)


def merge(nc, m, cst, io, xT_hi, xT_lo, y2, ya, keep, merged):
    with ExitStack() as stack:
        a = Memory(nc, stack)
        NAMES = ("gs", "ga", "bs", "ba")
        KS = (KD, KD, 4, 4)
        free = keep["states"][:, :, :, :].rearrange("p r a k -> p (r a k)")
        sig = free[:, 0:2 * L].rearrange("p (w t) -> p w t", w=2)
        raw = [free[:, (2 + w) * L:(3 + w) * L].rearrange("p (k n) -> p k n", k=KD) for w in range(2)]
        raw += [a.sb(f"m_{n}_raw", [P, k, P]) for n, k in zip(NAMES[2:], KS[2:])]
        hi = [a.sb(f"m_{n}_hi", [P, k, P], F32R) for n, k in zip(NAMES, KS)]
        lo = [a.sb(f"m_{n}_lo", [P, k, P], F32R) for n, k in zip(NAMES, KS)]
        bias = a.sb("m_bias", [P, 2])
        added = a.sem("m_added")
        ps = a.ps("ps_merge", [P, 4, 2, 512])
        ld = [a.sem(f"ld_m_{n}") for n in NAMES]
        hi_made = [a.sem(f"m_{n}_hi_made") for n in NAMES]
        lo_made = [a.sem(f"m_{n}_lo_made") for n in NAMES]
        done = [a.sem(f"m_{n}_done") for n in NAMES]
        bias_ready, sig_made, prod_made, out_made = a.sem("m_bias_ready"), [a.sem("m_sig0"), a.sem("m_sig1")], a.sem("m_prod_made"), a.sem("m_out")
        w_in = io["w_in"][0].rearrange("(q k) n -> q k n", k=KD)
        src = (lambda j: w_in[:, :, bass.ds(C_GS + P * j, P)], lambda j: w_in[:, :, bass.ds(C_GA + P * j, P)],
               lambda j: io["w_br_ssm"][0].rearrange("(c p) n -> p c n", p=P)[:, :, bass.ds(P * j, P)],
               lambda j: io["w_br_attn"][0].rearrange("(c p) n -> p c n", p=P)[:, :, bass.ds(P * j, P)])
        rhs = ((xT_hi, xT_lo), (xT_hi, xT_lo), y2, ya)
        half = lambda h: slice(512 * h, 512 * h + 512)

        def split_hi(act, w, n):
            act.wait_ge(ld[w], 16 * n)
            act.activation(hi[w][:, :, :], raw[w][:, :, :], ACT.Copy).then_inc(hi_made[w], 1)

        def split_lo(dve, w, n):
            dve.wait_ge(hi_made[w], n)
            dve.tensor_tensor(lo[w][:, :, :], raw[w][:, :, :], hi[w][:, :, :].bitcast(F32), ALU.subtract).then_inc(lo_made[w], 1)

        def load(sp, w, j):
            sp.dma_start(raw[w][:, :, :], src[w](j)).then_inc(ld[w], 16)

        def turns(eng, turn):
            with eng.Fori(0, KD - 1) as j:
                turn(eng, j, True)
            turn(eng, KD - 1, False)

        def pe_turn(pe, j, more):
            for w in range(4):
                pe.wait_ge(lo_made[w], j + 1)
                pe.wait_ge(sig_made[w] if w < 2 else (prod_made, out_made)[w - 2], 2 * j)
                for h in range(2):
                    for k in range(KS[w]):
                        ins = mm3(pe, ps[:, w, h, :], hi[w][:, k, :], lo[w][:, k, :],
                                  rhs[w][0][:, k, half(h)], rhs[w][1][:, k, half(h)], k == 0, k == KS[w] - 1)
                    ins.then_inc(done[w], 1)

        def act_turn(act, j, more):
            act.wait_ge(bias_ready, j + 1)
            for w in range(4):
                if w < 2:
                    for h in range(2):
                        act.wait_ge(done[w], 2 * j + h + 1)
                        act.wait_ge(prod_made if w == 0 else added, 2 * j if w == 0 else j)
                        act.activation(sig[:, w, half(h)], ps[:, w, h, :], ACT.Sigmoid, bias=bias[:, w:w + 1]).then_inc(sig_made[w], 1)
                if more:
                    act.wait_ge(done[w], 2 * j + 2)
                    split_hi(act, w, j + 2)

        def dve_turn(dve, j, more):
            for w in range(2):
                if more:
                    split_lo(dve, w, j + 2)
            whole = merged[:, bass.ds(j, 1), :].rearrange("p o t -> p (o t)")
            out = lambda h: merged[:, bass.ds(j, 1), half(h)].rearrange("p o t -> p (o t)")
            for h in range(2):
                dve.wait_ge(done[2], 2 * j + h + 1)
                dve.wait_ge(sig_made[0], 2 * j + h + 1)
                dve.tensor_tensor(out(h), ps[:, 2, h, :], sig[:, 0, half(h)], ALU.mult).then_inc(prod_made, 1)
            if more:
                split_lo(dve, 2, j + 2)
            for h in range(2):
                dve.wait_ge(done[3], 2 * j + h + 1)
                dve.wait_ge(sig_made[1], 2 * j + h + 1)
                dve.tensor_tensor(sig[:, 1, half(h)], ps[:, 3, h, :], sig[:, 1, half(h)], ALU.mult).then_inc(out_made, 1)
            dve.wait_ge(out_made, 2 * j + 2)
            dve.wait_ge(prod_made, 2 * j + 2)
            dve.tensor_tensor(whole, whole, sig[:, 1, :], ALU.add).then_inc(added, 1)
            if more:
                split_lo(dve, 3, j + 2)

        with nc.Block() as block:
            @block.sync
            def _(sp):
                for w in range(4):
                    load(sp, w, 0)
                for w in range(4):
                    sp.wait_ge(lo_made[w], 1)
                    load(sp, w, 1)
                for j in range(KD - 2):
                    for w in range(4):
                        sp.wait_ge(lo_made[w], j + 2)
                        load(sp, w, j + 2)

            @block.tensor
            def _(pe):
                turns(pe, pe_turn)

            @block.scalar
            def _(act):
                for w in range(4):
                    split_hi(act, w, 1)
                turns(act, act_turn)

            @block.vector
            def _(dve):
                for w in range(4):
                    split_lo(dve, w, 1)
                turns(dve, dve_turn)

            @block.gpsimd
            def _(pool):
                with pool.Fori(0, KD) as j:
                    pool.wait_ge(sig_made[0], 2 * j)
                    pool.wait_ge(sig_made[1], 2 * j)
                    pool.tensor_copy(bias[:, 0:1], keep["bias_T"][:, bass.ds(C_GS // P + j, 1)])
                    pool.tensor_copy(bias[:, 1:2], keep["bias_T"][:, bass.ds(C_GA // P + j, 1)]).then_inc(bias_ready, 1)


def layer_norm(dve, ch, act_sqrt, row, buf, gain, shift, out):
    stats, agg = buf["stats"], buf["agg"]
    for h in range(2):
        ch(dve.bn_stats(stats[:, h, :], row[:, 512 * h:512 * h + 512]))
    ch.sync()
    ch.do(dve.bn_aggr(agg[:, 0:2], stats[:, :, :]))
    dve.tensor_scalar(agg[:, 2:3], agg[:, 1:2], LN_EPS, 0.0, ALU.add, ALU.add).then_inc(*act_sqrt["var"])
    act_sqrt["wait"]()
    ch.do(dve.reciprocal(agg[:, 4:5], agg[:, 3:4]))
    ch.do(dve.tensor_scalar(row, row, agg[:, 0:1], agg[:, 4:5], ALU.subtract, ALU.mult))
    ch.do(dve.tensor_tensor(row, row, gain, ALU.mult))
    return dve.tensor_tensor(out, row, shift, ALU.add)


def output_projection(nc, m, cst, io, merged, scr):
    with ExitStack() as stack:
        a = Memory(nc, stack)
        m_hi, m_lo = a.sb("m_hi", [P, KD, L], F32R), a.sb("m_lo", [P, KD, L], F32R)
        w_raw = a.sb("wo_raw", [P, 2, D])
        w_hi, w_lo = a.sb("wo_hi", [P, KD, D], F32R), a.sb("wo_lo", [P, KD, D], F32R)
        x_in = a.sb("wo_x", [P, 2, D])
        gain, shift = a.sb("ln1_gain", [P, D]), a.sb("ln1_shift", [P, D])
        buf = {"stats": a.sb("ln1_stats", [P, 2, 6]), "agg": a.sb("ln1_agg", [P, 8])}
        ps = a.ps("ps_wo", [P, 4, 2, 512])
        ld_w, ld_x, ld_g = [a.sem("ld_wo0"), a.sem("ld_wo1")], [a.sem("ld_wox0"), a.sem("ld_wox1")], a.sem("ld_ln1")
        mh, ml, wh, wl = a.sem("m_hi_made"), a.sem("m_lo_made"), a.sem("wo_hi_made"), a.sem("wo_lo_made")
        done, read, var, root, x1_ready, stored, dve_sem = (a.sem("wo_" + n) for n in
                                                           ("done", "read", "var", "root", "x1", "stored", "dve_ch"))
        x_d = io["x"][0].rearrange("(p s) d -> p s d", s=NT)
        x1_d = scr["x1"][0:L, 0:D].rearrange("(p s) d -> p s d", s=NT)
        w_d = io["w_out"][0].rearrange("(j p) n -> p j n", p=P)
        with nc.Block() as block:
            @block.sync
            def _(sp):
                for j in range(KD):
                    if j >= 2:
                        sp.wait_ge(wl, j - 1)
                    sp.dma_start(w_raw[:, j % 2, :], w_d[:, j, :]).then_inc(ld_w[j % 2], 16)
                for n, t in (("ln1_g", gain), ("ln1_b", shift)):
                    sp.dma_start(t[:, :], io[n].broadcast_to((P, D))).then_inc(ld_g, 16)
                for s in range(NT):
                    if s >= 2:
                        sp.wait_ge(stored, 16 * (s - 1))
                    sp.dma_start(x_in[:, s % 2, :], x_d[:, s, :]).then_inc(ld_x[s % 2], 16)
                    if s >= 1:
                        sp.wait_ge(x1_ready, s)
                        sp.dma_start(x1_d[:, s - 1, :], x_in[:, (s - 1) % 2, :]).then_inc(stored, 16)
                sp.wait_ge(x1_ready, NT)
                sp.dma_start(x1_d[:, NT - 1, :], x_in[:, (NT - 1) % 2, :]).then_inc(stored, 16)
                sp.wait_ge(stored, 16 * NT)

            @block.tensor
            def _(pe):
                for first in (0, 4):
                    for j in range(KD):
                        pe.wait_ge(ml, j + 1)
                        pe.wait_ge(wl, j + 1)
                        for s in range(first, first + 4):
                            if first and j == 0:
                                pe.wait_ge(read, s - 3)
                            for h in range(2):
                                ins = mm3(pe, ps[:, s % 4, h, :], m_hi[:, j, s:L:NT], m_lo[:, j, s:L:NT],
                                          w_hi[:, j, 512 * h:512 * h + 512], w_lo[:, j, 512 * h:512 * h + 512], j == 0, j == KD - 1)
                            if j == KD - 1:
                                ins.then_inc(done, 1)

            @block.scalar
            def _(act):
                for j in range(KD):
                    act.activation(m_hi[:, j, :], merged[:, j, :], ACT.Copy).then_inc(mh, 1)
                    act.wait_ge(ld_w[j % 2], 16 * (j // 2 + 1))
                    act.activation(w_hi[:, j, :], w_raw[:, j % 2, :], ACT.Copy).then_inc(wh, 1)
                for s in range(NT):
                    act.wait_ge(var, s + 1)
                    act.activation(buf["agg"][:, 3:4], buf["agg"][:, 2:3], ACT.Sqrt).then_inc(root, 1)

            @block.vector
            def _(dve):
                ch = Chain(dve, dve_sem)
                for j in range(KD):
                    dve.wait_ge(mh, j + 1)
                    dve.tensor_tensor(m_lo[:, j, :], merged[:, j, :], m_hi[:, j, :].bitcast(F32), ALU.subtract).then_inc(ml, 1)
                    dve.wait_ge(wh, j + 1)
                    dve.tensor_tensor(w_lo[:, j, :], w_raw[:, j % 2, :], w_hi[:, j, :].bitcast(F32), ALU.subtract).then_inc(wl, 1)
                dve.wait_ge(ld_g, 32)
                for s in range(NT):
                    dve.wait_ge(ld_x[s % 2], 16 * (s // 2 + 1))
                    dve.wait_ge(done, s + 1)
                    row = x_in[:, s % 2, :]
                    dve.scalar_tensor_tensor(out=row, in0=row, scalar=ALPHA, in1=ps[:, s % 4, :, :].rearrange("p h n -> p (h n)"),
                                             op0=ALU.mult, op1=ALU.add).then_inc(read, 1)
                    dve.wait_ge(read, s + 1)
                    root_wait = lambda: dve.wait_ge(root, s + 1)
                    layer_norm(dve, ch, {"var": (var, 1), "wait": root_wait}, row, buf, gain[:, :], shift[:, :], row).then_inc(x1_ready, 1)


def route_and_share(nc, m, cst, io, scr, tab):
    with ExitStack() as stack:
        a = Memory(nc, stack)
        xT_hi, xT_lo = a.sb("x1T_hi", [P, KD, L], F32R), a.sb("x1T_lo", [P, KD, L], F32R)
        x_in = a.sb("x1_in", [P, 2, D])
        NAMES = ("gate", "up")
        raw = [a.sb(f"sh_{n}_raw", [P, KD, EH]) for n in NAMES]
        hi = [a.sb(f"sh_{n}_hi", [P, KD, EH], F32R) for n in NAMES]
        lo = [a.sb(f"sh_{n}_lo", [P, KD, EH], F32R) for n in NAMES]
        d_hi, d_lo = a.sb("sh_down_hi", [P, 2, D], F32R), a.sb("sh_down_lo", [P, 2, D], F32R)
        r_raw, r_hi, r_lo = a.sb("router_raw", [P, KD, NE]), a.sb("router_hi", [P, KD, NE], F32R), a.sb("router_lo", [P, KD, NE], F32R)
        h = a.sb("sh_h", [P, L // 2])
        h_hi, h_lo = a.sb("sh_h_hi", [P, 2, L], F32R), a.sb("sh_h_lo", [P, 2, L], F32R)
        silu = a.sb("sh_silu", [P, L // 2])
        acc = a.sb("sh_acc", [P, D])
        W = (P, NT, NE)
        score, sel, key, gates = (a.sb("rt_" + n, [P, NT, NE]) for n in ("score", "sel", "key", "gates"))
        t64 = a.sb("rt_t64", [P, 2, NT, NE])
        bias = a.sb("rt_bias", [P, NE])
        top2 = a.sb("rt_top2", [P, NT, 8, 8])
        grp = a.sb("rt_grp", [P, 4, NT, 8])
        top8 = a.sb("rt_top8", [P, NT, 8])
        low8 = a.sb("rt_low8", [P, 8, 8])
        tot = a.sb("rt_tot", [P, 2, NT])
        mask = a.sb("rt_mask", [P, NT, NE], BF16)
        tri = a.sb("rt_tri", [P, P], BF16)
        ones = a.sb("rt_ones", [P, P], BF16)
        onesf = a.sb("rt_onesf", [NE, P])
        trif = a.sb("rt_trif", [NE, NE])
        slot_n = a.sb("rt_slot", [P, P])
        ecol = a.sb("rt_ecol", [NE, P])
        cnt = a.sb("rt_cnt", [NE, 4])
        NX = (L - 1) // CAP
        over = a.sb("rt_over", [NE, NX])
        place = a.sb("rt_place", [NE, NX])
        onehot = a.sb("rt_onehot", [NE, NX + 1, P])
        base_w = a.sb("rt_base_w", [NE, NX, P])
        small = a.sb("rt_small", [P, 4])
        zero = a.sb("rt_zero", [P, D + NE])

        ps_t = a.ps("ps_rt", [P, 2, 512])
        ps_r = a.ps("ps_router", [P, NT, NE])
        ps_pos = a.ps("ps_pos", [P, 512])
        ps_s = a.ps("ps_share", [P, 4, 512])
        (ld_x0, ld_x1, ld_w, ld_dn, ld_r, ld_b, turned, x_hi_made, x_lo_made, w_hi_made, w_lo_made, zeros_ready, zeros_out,
         r_done, score_ready, mask_ready, pos_done, cnt_done, over_ready, tab_done, gates_ready, gu_done, silu_made, h_made,
         h_hi_made, h_lo_made, dn_done, acc_ready, acc_out, gates_out, dve_sem, pool_sem, pat_ready, place_done, place_w, d_hi_made) = (
            a.sem("rs_" + n) for n in
            ("ld_x0", "ld_x1", "ld_w", "ld_dn", "ld_r", "ld_b", "turned", "x_hi", "x_lo", "w_hi", "w_lo", "zeros", "zeros_out",
             "r_done", "score", "mask", "pos_done", "cnt_done", "over", "tab_done", "gates", "gu_done", "silu", "h",
             "h_hi", "h_lo", "dn_done", "acc", "acc_out", "gates_out", "dve_ch", "pool_ch", "patterns", "place_done", "place_w", "d_hi"))
        ld_x = (ld_x0, ld_x1)
        x1_d = scr["x1"][0:L, 0:D].rearrange("(p s) d -> p s d", s=NT)
        acc_d = scr["acc"][0:L, :].rearrange("(p s) d -> p s d", s=NT)
        ident = cst["ident"]
        d_raw = raw[0][:, :, :].rearrange("p k n -> p (k n)").rearrange("p (c n) -> p c n", c=2)

        with nc.Block() as block:
            @block.sync
            def _(sp):
                for s in range(NT):
                    if s >= 2:
                        sp.wait_ge(turned, 2 * (s - 1))
                    sp.dma_start(x_in[:, s % 2, :], x1_d[:, s, :]).then_inc(ld_x[s % 2], 16)
                    if s == 1:
                        sp.dma_start(r_raw[:, :, :], io["router_w"][0].rearrange("(q k) n -> q k n", k=KD)).then_inc(ld_r, 16)
                        sp.dma_start(bias[:, :], io["router_bias"].broadcast_to((P, NE))).then_inc(ld_b, 16)
                        for n, t in zip(NAMES, raw):
                            sp.dma_start(t[:, :, :], io[f"sh_w_{n}"][0].rearrange("(q k) n -> q k n", k=KD)).then_inc(ld_w, 16)
                sp.wait_ge(zeros_ready, 1)
                for lo_row, n in ((L, P), (L + P, REST)):
                    sp.dma_start(scr["x1"][lo_row:lo_row + n, :], zero[0:n, :]).then_inc(zeros_out, 16)
                    sp.dma_start(scr["acc"][lo_row:lo_row + n, :], zero[0:n, 0:D]).then_inc(zeros_out, 16)
                sp.wait_ge(w_lo_made, 2)
                sp.dma_start(d_raw, io["sh_w_down"][0].rearrange("(c p) n -> p c n", p=P)).then_inc(ld_dn, 16)
                for s in range(NT):
                    if s < 2:
                        sp.wait_ge(turned, 2 * NT)
                    else:
                        sp.wait_ge(acc_ready, s - 1)
                    sp.dma_start(x_in[:, s % 2, :], x1_d[:, s, :]).then_inc(ld_x[s % 2], 16)
                    if s == 0:
                        sp.wait_ge(gates_ready, 1)
                        sp.dma_start(scr["x1"][0:L, D:D + NE].rearrange("(p s) e -> p s e", s=NT), gates[:, :, :]).then_inc(gates_out, 16)
                    if s >= 1:
                        sp.wait_ge(acc_ready, s)
                        sp.dma_start(acc_d[:, s - 1, :], acc[:, :]).then_inc(acc_out, 16)
                sp.wait_ge(acc_ready, NT)
                sp.dma_start(acc_d[:, NT - 1, :], acc[:, :]).then_inc(acc_out, 16)
                sp.wait_ge(acc_out, 16 * NT)
                sp.wait_ge(zeros_out, 64)
                sp.wait_ge(gates_out, 16)

            @block.gpsimd
            def _(pool):
                ch = Chain(pool, pool_sem)
                ch(pool.memset(zero[:, :], 0.0))
                ch.sync()
                pool.sem_inc(zeros_ready, 1)
                ch(pool.memset(low8[:, :, :], 1.0))
                ch(pool.memset(tri[:, :], 1.0))
                ch(pool.memset(ones[:, :], 1.0))
                ch(pool.memset(onesf[:, :], 1.0))
                ch(pool.memset(trif[:, :], 1.0))
                ch(pool.iota(slot_n[:, :], pattern=[[1, P]], base=0, channel_multiplier=0, allow_small_or_imprecise_dtypes=True))
                ch(pool.iota(ecol[:, :], pattern=[[0, P]], base=0, channel_multiplier=1, allow_small_or_imprecise_dtypes=True))
                ch.sync()
                for j in range(NX):
                    ch.do(pool.memset(base_w[:, j, :], float(CAP * (j + 1))))
                ch.do(pool.affine_select(out=low8[:, :, :], in_=low8[:, :, :], compare_op=ALU.is_gt, fill=0.0, base=0,
                                         pattern=[[1, 8], [-1, 8]], channel_multiplier=0))
                ch.do(pool.affine_select(out=tri[:, :], in_=tri[:, :], compare_op=ALU.is_gt, fill=0.0, base=0,
                                         pattern=[[1, P]], channel_multiplier=-1))
                ch.do(pool.affine_select(out=trif[:, :], in_=trif[:, :], compare_op=ALU.is_gt, fill=0.0, base=0,
                                         pattern=[[1, NE]], channel_multiplier=-1))
                pool.sem_inc(pat_ready, 1)

            @block.tensor
            def _(pe):
                for s in range(NT):
                    pe.wait_ge(ld_x[s % 2], 16 * (s // 2 + 1))
                    for half in range(2):
                        n = 2 * s + half
                        if n >= 2:
                            pe.wait_ge(x_lo_made, n - 1)
                        for j in range(4):
                            ins = pe.transpose(ps_t[:, n % 2, P * j:P * j + P], x_in[:, s % 2, 4 * half + j:D:KD], ident[:, :])
                        ins.then_inc(turned, 1)
                pe.wait_ge(x_lo_made, 2 * NT)
                pe.wait_ge(w_lo_made, 1)
                for s in range(NT):
                    for k in range(KD):
                        ins = mm3(pe, ps_r[:, s, :], xT_hi[:, k, s:L:NT], xT_lo[:, k, s:L:NT], r_hi[:, k, :], r_lo[:, k, :],
                                  k == 0, k == KD - 1)
                ins.then_inc(r_done, 1)
                for n in range(4):
                    c, half = n // 2, slice(512 * (n % 2), 512 * (n % 2) + 512)
                    if n >= 2:
                        pe.wait_ge(h_made, n - 1)
                    for w in range(2):
                        pe.wait_ge(w_lo_made, w + 2)
                        for k in range(KD):
                            ins = mm3(pe, ps_s[:, 2 * (n % 2) + w, :], hi[w][:, k, P * c:P * c + P], lo[w][:, k, P * c:P * c + P],
                                      xT_hi[:, k, half], xT_lo[:, k, half], k == 0, k == KD - 1)
                    ins.then_inc(gu_done, 1)
                pe.wait_ge(mask_ready, 1)
                pe.wait_ge(pat_ready, 1)
                for s in range(NT):
                    ins = pe.matmul(ps_pos[:, NE * s:NE * s + NE], tri[:, :], mask[:, s, :], start=(s == 0), stop=(s == NT - 1),
                                    skip_group_check=True)
                    if s + 1 < NT:
                        later = mask[:, s, :].unsqueeze(1).broadcast_to((P, NT - 1 - s, NE))
                        ins = pe.matmul(ps_pos[:, NE * (s + 1):NE * NT], ones[:, :], later, start=False, stop=False, skip_group_check=True)
                ins.then_inc(pos_done, 1)
                pe.wait_ge(x_lo_made, 2 * NT)
                for s in range(NT):
                    ins = pe.matmul(ps_t[0:NE, 0, 0:1], mask[:, s, :], ones[:, 0:1], start=(s == 0), stop=(s == NT - 1))
                ins.then_inc(cnt_done, 1)
                pe.wait_ge(over_ready, 1)
                pe.matmul(ps_t[0:NE, 0, 4:5], trif[:, :], cnt[:, 1:2], start=True, stop=True)
                pe.matmul(ps_t[:, 0, 8:9], onesf[:, :], cnt[:, 1:2], start=True, stop=True).then_inc(place_done, 1)
                pe.wait_ge(place_w, 1)
                for n, w in ((0, None), (1, base_w)):
                    cols = slice(P * n, P * n + P)
                    js = range(NX + 1) if w is None else range(1, NX + 1)
                    for j in js:
                        ins = pe.matmul(ps_t[:, 1, cols], ecol[:, :] if w is None else base_w[:, j - 1, :], onehot[:, j, :],
                                        start=(j == js[0]), stop=(j == js[-1]))
                ins.then_inc(tab_done, 1)
                pe.wait_ge(h_lo_made, 4)
                pe.wait_ge(w_lo_made, 4)
                for s in range(NT):
                    if s >= 2:
                        pe.wait_ge(acc_ready, s - 1)
                    for half in range(2):
                        for c in range(2):
                            ins = mm3(pe, ps_s[:, 2 * (s % 2) + half, :], h_hi[:, c, s:L:NT], h_lo[:, c, s:L:NT],
                                      d_hi[:, c, 512 * half:512 * half + 512], d_lo[:, c, 512 * half:512 * half + 512], c == 0, c == 1)
                    ins.then_inc(dn_done, 1)

            @block.scalar
            def _(act):
                act.wait_ge(ld_r, 16)
                act.activation(r_hi[:, :, :], r_raw[:, :, :], ACT.Copy).then_inc(w_hi_made, 1)
                for n in range(2 * NT):
                    act.wait_ge(turned, n + 1)
                    s, half = n // 2, n % 2
                    act.activation(xT_hi[:, 4 * half:4 * half + 4, s:L:NT], ps_t[:, n % 2, :].rearrange("p (k t) -> p k t", k=4),
                                   ACT.Copy).then_inc(x_hi_made, 1)
                act.wait_ge(ld_w, 32)
                for w in range(2):
                    act.activation(hi[w][:, :, :], raw[w][:, :, :], ACT.Copy).then_inc(w_hi_made, 1)
                act.wait_ge(r_done, 1)
                act.activation(score[:, :, :], ps_r[:, :, :], ACT.Sigmoid).then_inc(score_ready, 1)
                for n in range(4):
                    act.wait_ge(gu_done, n + 1)
                    if n:
                        act.wait_ge(h_made, n)
                    act.activation(silu[:, :], ps_s[:, 2 * (n % 2), :], ACT.Silu).then_inc(silu_made, 1)
                    act.wait_ge(h_made, n + 1)
                    act.activation(h_hi[:, n // 2, 512 * (n % 2):512 * (n % 2) + 512], h[:, :], ACT.Copy).then_inc(h_hi_made, 1)
                act.wait_ge(ld_dn, 16)
                act.activation(d_hi[:, :, :], d_raw, ACT.Copy).then_inc(w_hi_made, 1)

            @block.vector
            def _(dve):
                ch = Chain(dve, dve_sem)
                tt, ts = dve.tensor_tensor, dve.tensor_scalar

                def split_lo(o, r, hh, n):
                    dve.wait_ge(w_hi_made, n)
                    tt(o[:, :, :], r, hh[:, :, :].bitcast(F32), ALU.subtract).then_inc(w_lo_made, 1)

                split_lo(r_lo, r_raw[:, :, :], r_hi, 1)
                for n in range(2 * NT):
                    dve.wait_ge(x_hi_made, n + 1)
                    s, half = n // 2, n % 2
                    tt(xT_lo[:, 4 * half:4 * half + 4, s:L:NT], ps_t[:, n % 2, :].rearrange("p (k t) -> p k t", k=4),
                       xT_hi[:, 4 * half:4 * half + 4, s:L:NT].bitcast(F32), ALU.subtract).then_inc(x_lo_made, 1)
                for w in range(2):
                    split_lo(lo[w], raw[w][:, :, :], hi[w], w + 2)

                def share(n):
                    dve.wait_ge(silu_made, n + 1)
                    if n:
                        dve.wait_ge(h_hi_made, n)
                        dve.wait_ge(h_lo_made, n)
                    tt(h[:, :], silu[:, :], ps_s[:, 2 * (n % 2) + 1, :], ALU.mult).then_inc(h_made, 1)
                    dve.wait_ge(h_hi_made, n + 1)
                    cols = slice(512 * (n % 2), 512 * (n % 2) + 512)
                    tt(h_lo[:, n // 2, cols], h[:, :], h_hi[:, n // 2, cols].bitcast(F32), ALU.subtract).then_inc(h_lo_made, 1)

                dve.wait_ge(score_ready, 1)
                dve.wait_ge(ld_b, 16)
                dve.wait_ge(pat_ready, 1)
                ch.do(tt(sel[:, :, :], score[:, :, :], bias[:, :].unsqueeze(1).broadcast_to(W), ALU.add))
                for s in range(NT):
                    for g in range(8):
                        ch(dve.max(top2[:, s, g, :], sel[:, s, 8 * g:8 * g + 8]))
                ch.sync()
                gs, rank, gm, neg = (grp[:, j, :, :] for j in range(4))
                ch.do(tt(gs, top2[:, :, :, 0], top2[:, :, :, 1], ALU.add))
                G = (P, NT, 8, 8)
                mine, other = gs.unsqueeze(3).broadcast_to(G), gs.unsqueeze(2).broadcast_to(G)
                gt, eq = (t64[:, j, :, :].rearrange("p s (g h) -> p s g h", g=8) for j in range(2))
                ch(tt(gt, other, mine, ALU.is_gt))
                ch.do(tt(eq, other, mine, ALU.is_equal))
                ch.do(tt(eq, eq, low8[:, :, :].unsqueeze(1).broadcast_to(G), ALU.mult))
                ch.do(tt(gt, gt, eq, ALU.add))
                ch.do(dve.tensor_reduce(rank, gt, AX.X, ALU.add))
                ch.do(ts(gm, rank, 3.5, 0.0, ALU.is_lt, ALU.add))
                ch.do(ts(neg, gm, -1.0, -NEG, ALU.add, ALU.mult))
                view = lambda t: t[:, :, :].rearrange("p s (g e) -> p s g e", g=8)
                ch.do(tt(view(key), view(sel), gm.unsqueeze(3).broadcast_to(G), ALU.mult))
                ch.do(tt(view(key), view(key), neg.unsqueeze(3).broadcast_to(G), ALU.add))
                for s in range(NT):
                    ch(dve.max(top8[:, s, :], key[:, s, :]))
                ch.sync()
                for s in range(NT):
                    ch(dve.match_replace(sel[:, s, :], top8[:, s, :], key[:, s, :], 2 * NEG))
                ch.sync()
                chosen = t64[:, 0, :, :]
                ch.do(ts(chosen, sel[:, :, :], 1.5 * NEG, 0.0, ALU.is_lt, ALU.add))
                dve.tensor_copy(mask[:, :, :], chosen).then_inc(mask_ready, 1)
                ch.do(tt(gates[:, :, :], score[:, :, :], chosen, ALU.mult))
                ch.do(dve.tensor_reduce(tot[:, 0, :], gates[:, :, :], AX.X, ALU.add))
                ch.do(dve.reciprocal(tot[:, 1, :], tot[:, 0, :]))
                ch.do(ts(tot[:, 1, :], tot[:, 1, :], 2.5, 0.0, ALU.mult, ALU.add))
                tt(gates[:, :, :], gates[:, :, :], tot[:, 1, :].unsqueeze(2).broadcast_to(W), ALU.mult).then_inc(gates_ready, 1)
                for n in range(4):
                    share(n)
                split_lo(d_lo, d_raw, d_hi, 4)
                dve.wait_ge(pos_done, 1)
                ch.do(ts(t64[:, 1, :, :], ps_pos[:, :].rearrange("p (s e) -> p s e", s=NT), 1.0, 0.0, ALU.add, ALU.add))
                ch.do(tt(t64[:, 1, :, :], t64[:, 1, :, :], chosen, ALU.mult))
                ch.do(ts(tab["pos_m"][:, :, :], t64[:, 1, :, :], -1.0, 0.0, ALU.add, ALU.add))
                dve.wait_ge(cnt_done, 1)
                ch.do(dve.tensor_copy(cnt[:, 0:1], ps_t[0:NE, 0, 0:1]))
                for j in range(NX):
                    ch(ts(over[:, j:j + 1], cnt[:, 0:1], CAP * (j + 1) + 0.5, 0.0, ALU.is_gt, ALU.add))
                ch.sync()
                dve.tensor_reduce(cnt[:, 1:2], over[:, :], AX.X, ALU.add).then_inc(over_ready, 1)
                dve.wait_ge(place_done, 1)
                for j in range(NX):
                    ch(ts(place[:, j:j + 1], ps_t[0:NE, 0, 4:5], float(NE + j), 0.0, ALU.add, ALU.add))
                ch(ts(small[:, 0:1], ps_t[:, 0, 8:9], 0.5, 0.25, ALU.mult, ALU.add))
                ch(ts(small[:, 2:3], ps_t[:, 0, 8:9], float(NE), 0.0, ALU.add, ALU.add))
                ch.sync()
                ch.do(ts(small[:, 1:2], small[:, 0:1], ROUND, -ROUND, ALU.add, ALU.add))
                ch.do(ts(tab["loops"][0:1, :], small[0:1, 1:2], NE / 2 - 1, 0.0, ALU.add, ALU.add))
                ch(ts(onehot[:, 0, :], slot_n[0:NE, :], ecol[:, 0:1], None, ALU.is_equal))
                for j in range(NX):
                    ch(ts(onehot[:, j + 1, :], slot_n[0:NE, :], place[:, j:j + 1], over[:, j:j + 1], ALU.is_equal, ALU.mult))
                ch.sync()
                dve.sem_inc(place_w, 1)
                dve.wait_ge(tab_done, 1)
                ch(dve.tensor_copy(tab["item_e"][:, :], ps_t[0:1, 1, 0:P]))
                ch.do(ts(tab["item_base"][:, :], slot_n[:, :], small[:, 2:3], 2048.0, ALU.is_ge, ALU.mult))
                ch.do(tt(tab["item_base"][:, :], tab["item_base"][:, :], ps_t[:, 1, P:2 * P], ALU.add))
                for s in range(NT):
                    dve.wait_ge(dn_done, s + 1)
                    dve.wait_ge(ld_x[s % 2], 16 * (NT // 2 + s // 2 + 1))
                    if s:
                        dve.wait_ge(acc_out, 16 * s)
                    dve.scalar_tensor_tensor(out=acc[:, :], in0=x_in[:, s % 2, :], scalar=ALPHA,
                                             in1=ps_s[:, 2 * (s % 2):2 * (s % 2) + 2, :].rearrange("p h n -> p (h n)"),
                                             op0=ALU.mult, op1=ALU.add).then_inc(acc_ready, 1)


def experts(nc, m, cst, io, scr, tab):
    with ExitStack() as stack:
        a = Memory(nc, stack)
        XW = D + NE
        GATE, UP, DOWN = range(3)
        raw = [[a.sb(f"w_raw_{j}{w}", [P, 2048]) for w in range(3)] for j in range(2)]
        hi = [[a.sb(f"w_hi_{j}{w}", [P, 2048], F32R) for w in range(3)] for j in range(2)]
        lo = [[a.sb(f"w_lo_{j}{w}", [P, 2048], F32R) for w in range(3)] for j in range(2)]
        x_main = [a.sb(f"x_main_{j}", [P, XW]) for j in range(2)]
        x_rest = [a.sb(f"x_rest_{j}", [REST, XW]) for j in range(2)]
        xT = a.sb("xe", [P, KD, 2, CAP], F32R)
        cross = a.sb("e_cross", [P, 2, CAP])
        pre = a.sb("e_pre", [P, 2, CAP])
        silu, h = a.sb("e_silu", [P, 2, CAP]), a.sb("e_h", [P, 2, CAP])
        h_hi, h_lo = a.sb("e_h_hi", [P, 2, CAP], F32R), a.sb("e_h_lo", [P, 2, CAP], F32R)
        y_main = [a.sb(f"y_main_{j}", [P, D]) for j in range(2)]
        y_rest = [a.sb(f"y_rest_{j}", [REST, D]) for j in range(2)]
        g_main = [a.sb(f"g_main_{j}", [P, 1]) for j in range(2)]
        g_rest = [a.sb(f"g_rest_{j}", [REST, 1]) for j in range(2)]
        slots, here = a.sb("e_slots", [P, CAP]), a.sb("e_here", [P, CAP])
        sel = a.sb("e_sel", [P, NT, CAP], FP16)
        info = a.sb("e_info", [P, NT, 2], FP16)
        dummy = a.sb("e_dummy", [P, 2])
        neg_slot = a.sb("e_neg_slot", [P, 2])
        idx_f = a.sb("e_idx_f", [P, 2])
        idx_main = [a.sb(f"idx_main_{j}", [P, 1], I32) for j in range(2)]
        idx_rest = [a.sb(f"idx_rest_{j}", [REST, 1], I32) for j in range(2)]
        out_main = [a.sb(f"out_main_{j}", [P, 1], I32) for j in range(2)]
        out_rest = [a.sb(f"out_rest_{j}", [REST, 1], I32) for j in range(2)]
        ps_gu = a.ps("ps_gu", [P, 2, 512])
        ps_t = a.ps("ps_xt", [P, 3, 512])
        ps_y = a.ps("ps_ye", [P, 3, 512])
        IDX = 8 * REST
        ld = [[a.sem(f"ld_e{j}{w}") for w in range(3)] for j in range(2)]
        (hi_made, lo_made, gu_done, cross_made, summed, silu_made, h_made, turned, xhi_made, xlo_made, y_done, y_evac, patterns,
         sel_ready, sums_done, idx_made, idx_kept, gate_kept, pool_sem, pool_held, dve_sem, dve_idx_sem) = (
            a.sem("ex_" + n) for n in
            ("hi", "lo", "gu", "cross", "summed", "silu", "h", "turned", "xhi", "xlo", "y_done", "y_evac", "patterns",
             "sel", "sums", "idx", "idx_kept", "gate_kept", "pool_ch", "pool_held", "dve_ch", "dve_idx"))
        gathered = [a.sem("gathered_0"), a.sem("gathered_1")]
        scattered = [a.sem("scattered_0"), a.sem("scattered_1")]
        ident = cst["ident"]
        src = [io["exp_w_gate"][0].rearrange("e (q k) n -> q e (k n)", k=KD),
               io["exp_w_up"][0].rearrange("e (q k) n -> q e (k n)", k=KD),
               io["exp_w_down"][0].rearrange("e (c p) n -> p e c n", p=P)]
        flat = lambda t: t[:, :]
        w3 = lambda t: t[:, :].rearrange("p (k n) -> p k n", k=KD)
        d3 = lambda t: t[:, :].rearrange("p (c n) -> p c n", c=2)

        with nc.Block() as block:
            @block.sync
            def _(sp):
                def load(n, j, wait=True):
                    e = sp.value_load(tab["item_e"][0:1, bass.ds(n, 1)], min_val=0, max_val=NE - 1)
                    for w in range(3):
                        if wait:
                            sp.wait_ge(lo_made, 6 * (n - 2) + 2 * w + 2)
                        if w == DOWN:
                            sp.dma_start(d3(raw[j][w]).unsqueeze(1), src[w][:, bass.ds(e, 1), :, :]).then_inc(ld[j][w], 16)
                        else:
                            sp.dma_start(flat(raw[j][w]).unsqueeze(1), src[w][:, bass.ds(e, 1), :]).then_inc(ld[j][w], 16)

                load(0, 0, wait=False)
                load(1, 1, wait=False)
                loops = sp.value_load(tab["loops"][0:1, 0:1], min_val=NE // 2 - 1, max_val=57)
                with sp.Fori(1, loops + 1) as i:
                    for j in range(2):
                        load(2 * i + j, j)

            @block.gpsimd
            def _(pool):
                ch = Chain(pool, pool_sem)
                ch(pool.iota(slots[:, :], pattern=[[1, CAP]], base=0, channel_multiplier=0, allow_small_or_imprecise_dtypes=True))
                ch(pool.iota(info[:, :, 0], pattern=[[1, NT]], base=-L, channel_multiplier=NT, allow_small_or_imprecise_dtypes=True))
                ch(pool.iota(dummy[:, :], pattern=[[P, 2]], base=L, channel_multiplier=1, allow_small_or_imprecise_dtypes=True))
                ch(pool.iota(neg_slot[:, :], pattern=[[-P, 2]], base=0, channel_multiplier=-1, allow_small_or_imprecise_dtypes=True))
                ch.do(pool.memset(info[:, :, 1], 1.0))
                pool.sem_inc(patterns, 1)

                def hold(sem, value):
                    pool.wait_ge(sem, value)
                    pool.sem_inc(pool_held, 1)

                def gather(n, j, first=False):
                    hold(idx_made, n + 1)
                    if not first:
                        hold(turned, 3 * (n - 1))
                    for x, ix in ((x_main[j], idx_main[j]), (x_rest[j], idx_rest[j])):
                        pool.indirect_dma_start(out=x[:, :], out_offset=None, in_=scr["x1"][:, :],
                                                in_offset=bass.IndirectOffsetOnAxis(ap=ix[:, 0:1], axis=0)).then_inc(gathered[j], 16)

                def keep_gate(n, j, uses):
                    e = pool.value_load(tab["item_e"][0:1, bass.ds(n, 1)], min_val=0, max_val=NE - 1)
                    hold(gathered[j], 32 * uses)
                    pool.tensor_copy(g_main[j][:, :], x_main[j][:, bass.ds(e + D, 1)]).then_inc(gate_kept, 1)
                    pool.tensor_copy(g_rest[j][:, :], x_rest[j][:, bass.ds(e + D, 1)]).then_inc(gate_kept, 1)

                def keep_indices(j):
                    pool.tensor_copy(out_main[j][:, :], idx_main[j][:, :]).then_inc(idx_kept, 1)
                    pool.tensor_copy(out_rest[j][:, :], idx_rest[j][:, :]).then_inc(idx_kept, 1)

                def turn(n, j, ahead1, ahead2, pair):
                    keep_indices(j)
                    if ahead1:
                        keep_gate(n + 1, 1 - j, pair + 1 + (1 if j else 0))
                    if ahead2:
                        gather(n + 2, j)
                    hold(y_evac, 4 * n + 4)
                    hold(idx_kept, 2 * n + 2)
                    hold(scattered[1 - j], 32 * (pair + j))
                    for y, ix in ((y_main[j], out_main[j]), (y_rest[j], out_rest[j])):
                        pool.indirect_dma_start(out=scr["acc"][:, :], out_offset=bass.IndirectOffsetOnAxis(ap=ix[:, 0:1], axis=0),
                                                in_=y[:, :], in_offset=None, compute_op=ALU.add).then_inc(scattered[j], 16)

                for n in range(2):
                    gather(n, n, first=True)
                keep_gate(0, 0, 1)
                loops = pool.value_load(tab["loops"][0:1, 0:1], min_val=NE // 2 - 1, max_val=57)
                with pool.Fori(0, loops) as i:
                    for j in range(2):
                        turn(2 * i + j, j, True, True, i)
                turn(2 * loops, 0, True, False, loops)
                turn(2 * loops + 1, 1, False, False, loops)
                for j in range(2):
                    pool.wait_ge(scattered[j], 32 * (loops + 1))

            @block.tensor
            def _(pe):
                pe.wait_ge(patterns, 1)

                def sums(n):
                    pe.wait_ge(sel_ready, n + 1)
                    pe.wait_ge(idx_made, n)
                    for s in range(NT):
                        pe.matmul(ps_t[:, 2, IDX:IDX + 2], sel[:, s, 0:P], info[:, s, :], start=(s == 0), stop=(s == NT - 1))
                    for s in range(NT):
                        ins = pe.matmul(ps_t[0:REST, 2, IDX + 4:IDX + 6], sel[:, s, P:CAP], info[:, s, :], start=(s == 0), stop=(s == NT - 1))
                    ins.then_inc(sums_done, 1)

                def turn_rows(j, uses, sums_before):
                    pe.wait_ge(idx_made, sums_before)
                    pe.wait_ge(gathered[j], 32 * uses)
                    for b in range(2):
                        for k in range(4):
                            ins = pe.transpose(ps_t[:, b, P * k:P * k + P], x_main[j][:, 4 * b + k:D:KD], ident[:, :])
                        ins.then_inc(turned, 1)
                    for k in range(KD):
                        ins = pe.transpose(ps_t[:, 2, REST * k:REST * k + REST], x_rest[j][:, k:D:KD], ident[0:REST, 0:REST])
                    ins.then_inc(turned, 1)

                def turn(n, j, ahead1, ahead2, pair):
                    pe.wait_ge(xlo_made, 3 * n + 3)
                    pe.wait_ge(lo_made, 6 * n + 4)
                    for c in range(2):
                        for w in (GATE, UP):
                            if c:
                                pe.wait_ge(summed, 4 * n + w + 1)
                            for k in range(KD):
                                cols = slice(P * c, P * c + P)
                                pe.matmul(ps_gu[:, w, 0:2 * CAP], w3(hi[j][w])[:, k, cols], xT[:, k, :, :],
                                          start=(k == 0), stop=False, skip_group_check=True)
                                ins = pe.matmul(ps_gu[:, w, 0:CAP], w3(lo[j][w])[:, k, cols], xT[:, k, 0, :],
                                                start=False, stop=(k == KD - 1), skip_group_check=True)
                            ins.then_inc(gu_done, 1)
                        if c == 0 and ahead2:
                            sums(n + 2)
                    if ahead1:
                        turn_rows(1 - j, pair + 1 + j, n + 3 if ahead2 else n + 2)
                    pe.wait_ge(h_made, 2 * n + 2)
                    pe.wait_ge(lo_made, 6 * n + 6)
                    pe.wait_ge(y_evac, 4 * n)
                    for seg in range(4):
                        tok, rows = (slice(0, P), P) if seg < 2 else (slice(P, CAP), REST)
                        cols = slice(512 * (seg % 2), 512 * (seg % 2) + 512)
                        if seg == 3:
                            pe.wait_ge(y_evac, 4 * n + 1)
                        for c in range(2):
                            ins = mm3(pe, ps_y[0:rows, seg % 3, :], h_hi[:, c, tok], h_lo[:, c, tok],
                                      d3(hi[j][DOWN])[:, c, cols], d3(lo[j][DOWN])[:, c, cols], c == 0, c == 1)
                        ins.then_inc(y_done, 1)

                sums(0)
                sums(1)
                turn_rows(0, 1, 2)
                loops = pe.value_load(tab["loops"][0:1, 0:1], min_val=NE // 2 - 1, max_val=57)
                with pe.Fori(0, loops) as i:
                    for j in range(2):
                        turn(2 * i + j, j, True, True, i)
                turn(2 * loops, 0, True, False, loops)
                turn(2 * loops + 1, 1, False, False, loops)

            @block.scalar
            def _(act):
                def split_hi(w, j, uses, piece):
                    if piece == 0:
                        act.wait_ge(ld[j][w], 16 * uses)
                    cols = slice(1024 * piece, 1024 * piece + 1024)
                    act.activation(hi[j][w][:, cols], raw[j][w][:, cols], ACT.Copy).then_inc(hi_made, 1)

                def rows_hi(n):
                    for b in range(3):
                        act.wait_ge(turned, 3 * n + b + 1)
                        if b < 2:
                            out, in_ = xT[:, 4 * b:4 * b + 4, 0, 0:P], ps_t[:, b, :].rearrange("p (k t) -> p k t", k=4)
                        else:
                            out, in_ = xT[:, :, 0, P:CAP], ps_t[:, 2, 0:KD * REST].rearrange("p (k t) -> p k t", k=KD)
                        act.activation(out, in_, ACT.Copy).then_inc(xhi_made, 1)

                def turn(n, j, ahead1, ahead2, pair):
                    uses = pair + 1 + j
                    def low_products(g):
                        act.wait_ge(gu_done, 4 * n + g + 1)
                        act.activation(cross[:, g % 2, :], ps_gu[:, g % 2, CAP:2 * CAP], ACT.Copy).then_inc(cross_made, 1)

                    def gated(c):
                        act.wait_ge(summed, 4 * n + 2 * c + 1)
                        act.activation(silu[:, c, :], pre[:, GATE, :], ACT.Silu).then_inc(silu_made, 1)

                    if ahead1:
                        split_hi(GATE, 1 - j, uses, 0)
                        split_hi(GATE, 1 - j, uses, 1)
                    low_products(0)
                    if ahead1:
                        split_hi(UP, 1 - j, uses, 0)
                    gated(0)
                    low_products(1)
                    if ahead1:
                        split_hi(UP, 1 - j, uses, 1)
                    low_products(2)
                    gated(1)
                    low_products(3)
                    if ahead1:
                        rows_hi(n + 1)
                    act.wait_ge(gate_kept, 2 * n + 2)
                    act.wait_ge(scattered[j], 32 * pair)
                    for seg in range(4):
                        if ahead1 and seg < 2:
                            split_hi(DOWN, 1 - j, uses, seg)
                        act.wait_ge(y_done, 4 * n + seg + 1)
                        cols = slice(512 * (seg % 2), 512 * (seg % 2) + 512)
                        y, g, rows = (y_main, g_main, P) if seg < 2 else (y_rest, g_rest, REST)
                        act.activation(y[j][:, cols], ps_y[0:rows, seg % 3, :], ACT.Copy, scale=g[j][:, 0:1]).then_inc(y_evac, 1)

                for w in range(3):
                    for piece in range(2):
                        split_hi(w, 0, 1, piece)
                rows_hi(0)
                loops = act.value_load(tab["loops"][0:1, 0:1], min_val=NE // 2 - 1, max_val=57)
                with act.Fori(0, loops) as i:
                    for j in range(2):
                        turn(2 * i + j, j, True, True, i)
                turn(2 * loops, 0, True, False, loops)
                turn(2 * loops + 1, 1, False, False, loops)

            @block.vector
            def _(dve):
                tt = dve.tensor_tensor
                ch, chi = Chain(dve, dve_sem), Chain(dve, dve_idx_sem)
                dve.wait_ge(patterns, 1)

                def split_lo(n, w, j, piece):
                    dve.wait_ge(hi_made, 6 * n + 2 * w + piece + 1)
                    cols = slice(1024 * piece, 1024 * piece + 1024)
                    tt(lo[j][w][:, cols], raw[j][w][:, cols], hi[j][w][:, cols].bitcast(F32), ALU.subtract).then_inc(lo_made, 1)

                def rows_lo(n):
                    for b in range(3):
                        dve.wait_ge(xhi_made, 3 * n + b + 1)
                        if b < 2:
                            view, in_ = (lambda part: xT[:, 4 * b:4 * b + 4, part, 0:P]), ps_t[:, b, :].rearrange("p (k t) -> p k t", k=4)
                        else:
                            view, in_ = (lambda part: xT[:, :, part, P:CAP]), ps_t[:, 2, 0:KD * REST].rearrange("p (k t) -> p k t", k=KD)
                        tt(view(1), in_, view(0).bitcast(F32), ALU.subtract).then_inc(xlo_made, 1)

                def select(n):
                    e = dve.value_load(tab["item_e"][0:1, bass.ds(n, 1)], min_val=0, max_val=NE - 1)
                    chi.do(tt(here[:, :], slots[:, :], tab["item_base"][:, bass.ds(n, 1)].broadcast_to((P, CAP)), ALU.add))
                    tt(sel[:, :, :], tab["pos_m"][:, :, bass.ds(e, 1)].broadcast_to((P, NT, CAP)),
                       here[:, :].unsqueeze(1).broadcast_to((P, NT, CAP)), ALU.is_equal).then_inc(sel_ready, 1)

                def indices(n, j):
                    dve.wait_ge(sums_done, n + 1)
                    for c, (rows, out) in enumerate(((P, idx_main[j]), (REST, idx_rest[j]))):
                        number, taken = (ps_t[0:rows, 2, IDX + 4 * c + i:IDX + 4 * c + i + 1] for i in range(2))
                        chi.do(dve.tensor_scalar(idx_f[0:rows, c:c + 1], taken, neg_slot[0:rows, c:c + 1], dummy[0:rows, c:c + 1],
                                                 ALU.mult, ALU.add))
                        ins = tt(out[:, :], idx_f[0:rows, c:c + 1], number, ALU.add)
                        if c == 0:
                            chi(ins)
                        else:
                            chi.sync()
                            ins.then_inc(idx_made, 1)

                def add_cross(n, g):
                    dve.wait_ge(cross_made, 4 * n + g + 1)
                    tt(pre[:, g % 2, :], ps_gu[:, g % 2, 0:CAP], cross[:, g % 2, :], ALU.add).then_inc(summed, 1)

                def hidden(n, c):
                    dve.wait_ge(summed, 4 * n + 2 * c + 2)
                    dve.wait_ge(silu_made, 2 * n + c + 1)
                    ch.do(tt(h[:, c, :], silu[:, c, :], pre[:, UP, :], ALU.mult))
                    ch.do(dve.tensor_copy(h_hi[:, c, :], h[:, c, :]))
                    tt(h_lo[:, c, :], h[:, c, :], h_hi[:, c, :].bitcast(F32), ALU.subtract).then_inc(h_made, 1)

                def turn(n, j, ahead1, ahead2):
                    if ahead2:
                        select(n + 2)
                    for g in range(4):
                        if ahead1 and g < 3:
                            split_lo(n + 1, g // 2, 1 - j, g % 2)
                        add_cross(n, g)
                        if g % 2:
                            hidden(n, g // 2)
                        if g == 1 and ahead2:
                            dve.wait_ge(idx_kept, 2 * n + 2)
                            indices(n + 2, j)
                    if ahead1:
                        rows_lo(n + 1)
                        split_lo(n + 1, UP, 1 - j, 1)
                        for piece in range(2):
                            split_lo(n + 1, DOWN, 1 - j, piece)

                for n in range(2):
                    select(n)
                    indices(n, n)
                for w in range(3):
                    for piece in range(2):
                        split_lo(0, w, 0, piece)
                rows_lo(0)
                loops = dve.value_load(tab["loops"][0:1, 0:1], min_val=NE // 2 - 1, max_val=57)
                with dve.Fori(0, loops) as i:
                    ch.loop(i, 8)
                    chi.loop(i, 8)
                    for j in range(2):
                        turn(2 * i + j, j, True, True)
                ch.end_loop(loops)
                chi.end_loop(loops)
                turn(2 * loops, 0, True, False)
                turn(2 * loops + 1, 1, False, False)


def output_norm(nc, m, io, scr, out):
    with ExitStack() as stack:
        a = Memory(nc, stack)
        NB = 4
        rows = a.sb("ln2_rows", [P, NB, D])
        gain, shift = a.sb("ln2_gain", [P, D]), a.sb("ln2_shift", [P, D])
        buf = {"stats": a.sb("ln2_stats", [P, 2, 6]), "agg": a.sb("ln2_agg", [P, 8])}
        ld = [a.sem(f"ld_acc{j}") for j in range(NB)]
        stored = [a.sem(f"ln2_stored{j}") for j in range(NB)]
        ld_g, var, root, ready, dve_sem = (a.sem("ln2_" + n) for n in ("ld", "var", "root", "ready", "dve_ch"))
        acc_d = scr["acc"][0:L, :].rearrange("(p s) d -> p s d", s=NT)
        out_d = out[0].rearrange("(p s) d -> p s d", s=NT)
        with nc.Block() as block:
            @block.sync
            def _(sp):
                for s in range(NT):
                    if s >= NB:
                        sp.wait_ge(stored[s % NB], 16 * (s // NB))
                    sp.dma_start(rows[:, s % NB, :], acc_d[:, s, :]).then_inc(ld[s % NB], 16)
                    if s == 0:
                        for n, t in (("ln2_g", gain), ("ln2_b", shift)):
                            sp.dma_start(t[:, :], io[n].broadcast_to((P, D))).then_inc(ld_g, 16)

            @block.scalar
            def _(act):
                for s in range(NT):
                    act.wait_ge(var, s + 1)
                    act.activation(buf["agg"][:, 3:4], buf["agg"][:, 2:3], ACT.Sqrt).then_inc(root, 1)
                    act.wait_ge(ready, s + 1)
                    act.dma_start(out_d[:, s, :], rows[:, s % NB, :]).then_inc(stored[s % NB], 16)
                for j in range(NB):
                    act.wait_ge(stored[j], 16 * (NT // NB))

            @block.vector
            def _(dve):
                ch = Chain(dve, dve_sem)
                dve.wait_ge(ld_g, 32)
                for s in range(NT):
                    dve.wait_ge(ld[s % NB], 16 * (s // NB + 1))
                    row = rows[:, s % NB, :]
                    layer_norm(dve, ch, {"var": (var, 1), "wait": lambda: dve.wait_ge(root, s + 1)}, row, buf,
                               gain[:, :], shift[:, :], row).then_inc(ready, 1)


def hybrid_layer(nc, io, scr, out):
    with ExitStack() as stack:
        m = Memory(nc, stack)
        cst, cst["write"] = constants(nc, m)
        with ExitStack() as mixer:
            a = Memory(nc, mixer)
            merged = a.sb("merged", [P, KD, L])
            keep = {"bias_T": a.sb("bias_T", [P, NB_COL]), "ut_all": merged[:, 0:4, :].rearrange("p a b -> p (a b)")}
            y_T = merged[:, 0:4, :]
            y_tok = merged[:, 4:8, :].rearrange("p a (b c) -> p (a b) c", b=2)
            keep["u_tok"] = y_tok
            with ExitStack() as branches:
                b = Memory(nc, branches)
                xT_hi, xT_lo = b.sb("xT_hi", [P, KD, L], F32R), b.sb("xT_lo", [P, KD, L], F32R)
                keep["states"] = b.sb("states", [P, 2, PAIRS, NCH + 1])
                keep["scan_fac"] = b.sb("scan_fac", [P, 2, 2 * PAIRS])
                mixer_input(nc, b, cst, io, xT_hi, xT_lo, keep, scr)
                attention(nc, b, cst, io, xT_hi, xT_lo, keep, scr)
                ya = [b.sb("ya_" + n, [P, 4, L], F32R) for n in ("hi", "lo")]
                branch_outputs(nc, b, cst, io, keep, scr, ya[0], ya[1], y_tok)
                y2 = [b.sb("y2_" + n, [P, 4, L], F32R) for n in ("hi", "lo")]
                gated_ssm(nc, b, cst, io, y_tok, y_T, y2[0], y2[1])
                merge(nc, b, cst, io, xT_hi, xT_lo, y2, ya, keep, merged)
            output_projection(nc, a, cst, io, merged, scr)
        tab = {"pos_m": m.sb("pos_m", [P, NT, NE]), "item_e": m.sb("item_e", [1, P], I32),
               "item_base": m.sb("item_base", [P, P]), "loops": m.sb("loops", [1, 1], I32)}
        route_and_share(nc, m, cst, io, scr, tab)
        experts(nc, m, cst, io, scr, tab)
        output_norm(nc, m, io, scr, out)


def kernel(**inputs):
    import concourse.bacc as _bacc
    from concourse.bass_utils import run_bass_kernel_spmd as _run

    nc = _bacc.Bacc("TRN2", target_bir_lowering=False, num_devices=1)
    arrays, io = {}, {}
    for name, value in inputs.items():
        arr = np.ascontiguousarray(value)
        arrays["in_" + name] = arr
        io[name] = nc.dram_tensor("in_" + name, arr.shape, mybir.dt.from_np(arr.dtype), kind="ExternalInput").ap()
    out = nc.dram_tensor("out_0", (1, L, D), F32, kind="ExternalOutput").ap()
    scr = {"c_pow": nc.dram_tensor("scr_c_pow", (P, 2 * PAIRS * (T + 1) * SSM_C), F32).ap(),
           "k_pad": nc.dram_tensor("scr_k_pad", (SSM_C, SSM_G, KP0 + P), F32).ap(),
           "att": nc.dram_tensor("scr_att", (NG, L, NH * ROW), F32).ap(),
           "x1": nc.dram_tensor("scr_x1", (L + CAP, D + NE), F32).ap(),
           "acc": nc.dram_tensor("scr_acc", (L + CAP, D), F32).ap()}
    hybrid_layer(nc, io, scr, out)
    r = _run(nc, [arrays], core_ids=[0])
    return r.results[0]["out_0"]
```

```python
from contextlib import ExitStack

import numpy as np
import concourse.bass as bass
from concourse import mybir

F32 = mybir.dt.float32
F32R = mybir.dt.float32r
BF16 = mybir.dt.bfloat16
FP16 = mybir.dt.float16
I32 = mybir.dt.int32
ALU = mybir.AluOpType
ACT = mybir.ActivationFunctionType
AX = mybir.AxisListType

P = 128
D = 1024
L = 1024
KD = D // P
NT = L // P
SSM_W, SSM_C, SSM_G, SSM_N = 512, 16, 32, 64
PAIRS = SSM_G // 2
T = 8
NCH = L // T
KP0 = (T - 1) * SSM_C
NG, NH, DH = 3, 8, 64
HP = NH // 2
QKV = NG * NH * DH
IN_W = SSM_W + 3 * QKV + 2 * D
C_Q, C_K, C_V, C_GS, C_GA = SSM_W, SSM_W + QKV, SSM_W + 2 * QKV, SSM_W + 3 * QKV, SSM_W + 3 * QKV + D
NB_COL = IN_W // P
ROW = DH + 2
NE, EH = 64, 256
ROUTED_SCALE = 2.5
CAP = 160
REST = CAP - P
NEG = -1.0e30
ROUND = 1.5 * 2.0 ** 23
ALPHA = 2.0 ** 0.25
LN_EPS = 1e-5


class Chain:

    def __init__(self, eng, sem):
        self.eng, self.sem, self.base, self.n = eng, sem, 0, 0

    def __call__(self, ins):
        ins.then_inc(self.sem, 1)
        self.n += 1

    def sync(self):
        self.eng.wait_ge(self.sem, self.base + self.n)

    def do(self, ins):
        self(ins)
        self.sync()

    def loop(self, i, per_turn):
        self.before, self.n, self.per_turn = self.base + self.n, 0, per_turn
        self.base = self.before + i * per_turn

    def end_loop(self, turns):
        assert self.n == self.per_turn, (self.n, self.per_turn)
        self.base, self.n = self.before + turns * self.per_turn, 0


def mm3(eng, out, lh, ll, rh, rl, first, last):
    eng.matmul(out, lh, rh, start=first, stop=False, skip_group_check=True)
    eng.matmul(out, lh, rl, start=False, stop=False, skip_group_check=True)
    return eng.matmul(out, ll, rh, start=False, stop=last, skip_group_check=True)


class Memory:

    def __init__(self, nc, stack):
        self.nc, self.stack, self.sems = nc, stack, []
        stack.callback(self.clear)

    def clear(self):
        if self.sems:
            self.nc.clear_and_free_semaphores(self.sems)
            self.nc.all_engine_barrier()

    def sb(self, name, shape, dt=F32):
        return self.stack.enter_context(self.nc.sbuf_tensor(name, shape, dt))

    def ps(self, name, shape, dt=F32):
        return self.stack.enter_context(self.nc.psum_tensor(name, shape, dt))

    def sem(self, name):
        self.sems.append(self.nc.alloc_semaphore(name))
        return self.sems[-1]


def constants(nc, m):
    c = {}
    c["ident"] = m.sb("ident", [P, P])
    c["identb"] = m.sb("identb", [P, P], BF16)
    c["mask_band"] = m.sb("mask_band", [P, 2 * P], BF16)
    c["mask_pair"] = m.sb("mask_pair", [P, P], BF16)
    parity = m.sb("parity", [P, 2, P])
    c["ready"] = m.sem("const_ready")
    chain_sem = m.sem("const_chain")

    def write(pool):
        ch = Chain(pool, chain_sem)
        ident, identb, band, pair = (c[n][:, :] for n in ("ident", "identb", "mask_band", "mask_pair"))
        for t in (ident, identb):
            ch(pool.memset(t, 0.0))
        ch(pool.memset(band, 0.0))
        odd, near = parity[:, 0, :], parity[:, 1, :]
        ch(pool.iota(odd, pattern=[[-1, P]], base=0, channel_multiplier=1, allow_small_or_imprecise_dtypes=True))
        ch.sync()
        ch.do(pool.tensor_scalar(odd, odd, 0.5, 0.0, ALU.mult, ALU.add))
        ch.do(pool.tensor_scalar(near, odd, ROUND, -ROUND, ALU.add, ALU.add))
        ch.do(pool.tensor_tensor(odd, odd, near, ALU.subtract))
        ch.do(pool.tensor_tensor(odd, odd, odd, ALU.mult))
        ch.do(pool.tensor_scalar(pair, odd, 4.0 * NEG, 0.0, ALU.mult, ALU.add))
        for t in (ident, identb):
            ch(pool.affine_select(out=t, in_=t, compare_op=ALU.not_equal, fill=1.0, base=0,
                                  pattern=[[-1, P]], channel_multiplier=1))
        ch(pool.affine_select(out=band, in_=band, compare_op=ALU.is_ge, fill=NEG, base=0,
                              pattern=[[1, 2 * P]], channel_multiplier=-1))
        ch(pool.affine_select(out=pair, in_=pair, compare_op=ALU.is_ge, fill=NEG, base=0,
                              pattern=[[-1, P]], channel_multiplier=1))
        ch.sync()
        ch(pool.affine_select(out=band, in_=band, compare_op=ALU.is_ge, fill=NEG, base=P,
                              pattern=[[-1, 2 * P]], channel_multiplier=1))
        ch.sync()
        pool.sem_inc(c["ready"], 1)

    return c, write


def s5_parameters(pool, sem, t, out):
    ch = Chain(pool, sem)
    free = iter(range(24))
    new = lambda: t["scratch"][:, next(free), :]
    dt, er, ph, a, b, c2, n = (new() for _ in range(7))
    bits = t["bits"][:, :]

    def ts(o, i, s1, s2, op0, op1):
        ch.do(pool.tensor_scalar(o, i, s1, s2, op0, op1))

    def tt(o, i, j, op):
        ch.do(pool.tensor_tensor(o, i, j, op))

    def poly(o, x, coefs):
        ts(o, x, coefs[0], coefs[1], ALU.mult, ALU.add)
        for c in coefs[2:]:
            tt(o, o, x, ALU.mult)
            ts(o, o, c, 0.0, ALU.add, ALU.add)

    def exp(o, x):
        ts(a, x, -87.0, 88.0, ALU.max, ALU.min)
        ts(b, a, 1.0 / float(np.log(2.0)), 0.0, ALU.mult, ALU.add)
        ts(n, b, ROUND, -ROUND, ALU.add, ALU.add)
        ts(b, n, -0.693359375, 0.0, ALU.mult, ALU.add)
        tt(a, a, b, ALU.add)
        ts(b, n, 2.12194440e-4, 0.0, ALU.mult, ALU.add)
        tt(a, a, b, ALU.add)
        poly(b, a, [1 / 5040, 1 / 720, 1 / 120, 1 / 24, 1 / 6, 0.5, 1.0, 1.0])
        ts(c2, n, 127.0, 8388608.0, ALU.add, ALU.mult)
        ch.do(pool.tensor_copy(bits, c2))
        tt(o, b, bits.bitcast(F32), ALU.mult)

    lre, lim, ldt = (t["raw"][:, j, :] for j in range(3))
    exp(dt, ldt)
    tt(er, lre, dt, ALU.mult)
    exp(er, er)
    tt(ph, lim, dt, ALU.mult)
    ts(n, ph, 1.0 / (2 * float(np.pi)), 0.0, ALU.mult, ALU.add)
    ts(n, n, ROUND, -ROUND, ALU.add, ALU.add)
    for part in (6.28125, 1.9350051879882812e-3, 3.0199159819e-7):
        ts(b, n, -part, 0.0, ALU.mult, ALU.add)
        tt(ph, ph, b, ALU.add)
    ts(ph, ph, 0.5, 0.0, ALU.mult, ALU.add)
    tt(a, ph, ph, ALU.mult)
    f = float
    from_fact = lambda k: f(1.0 / np.prod(np.arange(1.0, k + 1)))
    poly(b, a, [from_fact(13), -from_fact(11), from_fact(9), -from_fact(7), from_fact(5), -from_fact(3), 1.0])
    tt(b, b, ph, ALU.mult)
    poly(c2, a, [from_fact(12), -from_fact(10), from_fact(8), -from_fact(6), from_fact(4), -0.5, 1.0])
    sn, cs, lbr, lbi, den, m1 = (new() for _ in range(6))
    tt(sn, b, c2, ALU.mult)
    ts(sn, sn, 2.0, 0.0, ALU.mult, ALU.add)
    tt(cs, b, b, ALU.mult)
    ts(cs, cs, -2.0, 1.0, ALU.mult, ALU.add)
    tt(lbr, er, cs, ALU.mult)
    tt(lbi, er, sn, ALU.mult)
    ts(m1, lbr, -1.0, 0.0, ALU.add, ALU.add)
    tt(a, lre, lre, ALU.mult)
    tt(b, lim, lim, ALU.mult)
    tt(den, a, b, ALU.add)
    pool.sem_inc(t["den_ready"], 1)
    pool.wait_ge(t["rden_ready"], 1)
    rden = t["rden"][:, :]
    for o, x, y, op in ((out["fac_re"], m1, lbi, ALU.add), (out["fac_im"], lbi, m1, ALU.subtract)):
        tt(a, x, lre, ALU.mult)
        tt(b, y, lim, ALU.mult)
        tt(a, a, b, op)
        tt(o[:, :], a, rden, ALU.mult)
    pr, pi = out["pow_re"], out["pow_im"]
    ch(pool.memset(pr[:, :, 0], 1.0))
    ch(pool.memset(pi[:, :, 0], 0.0))
    ch(pool.tensor_copy(pr[:, :, 1], lbr))
    ch.do(pool.tensor_copy(pi[:, :, 1], lbi))
    for j in range(2, T + 1):
        tt(a, pr[:, :, j - 1], lbr, ALU.mult)
        tt(b, pi[:, :, j - 1], lbi, ALU.mult)
        tt(pr[:, :, j], a, b, ALU.subtract)
        tt(a, pr[:, :, j - 1], lbi, ALU.mult)
        tt(b, pi[:, :, j - 1], lbr, ALU.mult)
        tt(pi[:, :, j], a, b, ALU.add)
    for j in range(T):
        ch(pool.tensor_copy(out["rpow_re"][:, :, j], pr[:, :, T - 1 - j]))
        ch(pool.tensor_copy(out["rpow_im"][:, :, j], pi[:, :, T - 1 - j]))
    for j, (src, sign) in enumerate(((pr, 1.0), (pr, 1.0), (pi, 1.0), (pi, -1.0))):
        ch(pool.tensor_scalar(out["scan_fac"][:, j // 2, (j % 2) * PAIRS:(j % 2 + 1) * PAIRS],
                              src[:, :, T], sign, 0.0, ALU.mult, ALU.add))
    ch.sync()


def mixer_input(nc, m, cst, io, xT_hi, xT_lo, keep, scr):
    with ExitStack() as stack:
        a = Memory(nc, stack)
        XR = 2
        x_tok = a.sb("x_tok", [P, XR, D])
        w_raw = a.sb("u_w_raw", [P, KD, 256])
        WR = 4
        w_hi = a.sb("u_w_hi", [P, WR, 256], F32R)
        w_lo = a.sb("u_w_lo", [P, WR, 256], F32R)
        bias_u = a.sb("bias_u", [P, SSM_W])
        bias_rows = a.sb("bias_rows", [NB_COL, P])
        u_tok = keep["u_tok"]
        lam_rows = a.sb("lam_rows", [PAIRS, 3, P])
        dt_rows = a.sb("dt_rows", [PAIRS, 2])
        lam_raw = a.sb("lam_raw", [P, 3, PAIRS])
        b_raw = a.sb("b_raw", [P, 2, PAIRS, SSM_C])
        b_bar = a.sb("b_bar", [P, 2, PAIRS, SSM_C])
        c_rows = a.sb("c_rows", [P, 2, 2, P])
        c_col = a.sb("c_col", [P, 2, PAIRS, SSM_C])
        c_pow = a.sb("c_pow", [P, 2, PAIRS, T + 1, SSM_C])
        prod = [keep["ut_all"][:, :], keep["states"][:, :, :, :].rearrange("p r a k -> p (r a k)")]
        scratch = a.sb("lam_scratch", [P, 24, PAIRS])
        bits = a.sb("lam_bits", [P, PAIRS], I32)
        rden = a.sb("rden", [P, PAIRS])
        par = {n: a.sb("s5_" + n, [P, PAIRS, w]) for n, w in
               (("pow_re", T + 1), ("pow_im", T + 1), ("rpow_re", T), ("rpow_im", T))}
        par |= {n: a.sb("s5_" + n, [P, PAIRS]) for n in ("fac_re", "fac_im")}
        par["scan_fac"] = keep["scan_fac"]
        u_stage = a.sb("u_stage", [P, 4, P])
        w_stage = a.sb("w_stage", [P, 2, 2, P])
        w_prod = a.sb("w_prod", [P, 4, 2, P])
        b_pad = a.sb("b_pad", [P, 4, 2, SSM_C])
        ut_stage = a.sb("ut_stage", [P, 4, P])
        wt_stage = a.sb("wt_stage", [P, 2, 2, P])
        k_resp = a.sb("k_resp", [SSM_C, SSM_G, P])
        zeros = a.sb("k_zeros", [SSM_C, (T - 1) * SSM_C])
        d_row = a.sb("d_row", [SSM_C, SSM_G, SSM_C])

        ps_x = a.ps("ps_x", [P, 4, 512])
        ps_u = a.ps("ps_u", [P, NT // 2, 2, 256])
        ld_x = [a.sem(f"ld_x{j}") for j in range(XR)]
        ld_dt, dt_ready, ld_lam, lam_copied = (a.sem(n) for n in ("ld_dt", "dt_ready", "ld_lam", "lam_copied"))
        ld_w, ld_par, ld_bias = a.sem("ld_uw"), a.sem("ld_par"), a.sem("ld_bias")
        x_turned, x_hi_made, x_lo_made = a.sem("x_turned"), a.sem("x_hi_made"), a.sem("x_lo_made")
        p_turned, p_copied = a.sem("p_turned"), a.sem("p_copied")
        w_hi_made, w_lo_made, w_used = a.sem("uw_hi_made"), a.sem("uw_lo_made"), a.sem("uw_used")
        u_evac = a.sem("u_evac")
        den_ready, rden_ready, par_ready = a.sem("den_ready"), a.sem("rden_ready"), a.sem("par_ready")
        pool_ch, dve_ch = a.sem("mi_pool_ch"), a.sem("mi_dve_ch")
        cpow_ready, zero_ready = a.sem("cpow_ready"), a.sem("zero_ready")
        staged, turned, copied_u, copied_w = a.sem("s5_staged"), a.sem("s5_turned"), a.sem("s5_ut"), a.sem("s5_wt")
        k_done, k_copied, v_done, v_copied = a.sem("s5_k"), a.sem("s5_kc"), a.sem("s5_v"), a.sem("s5_vc")
        ut_kept, stored, kd_ready = a.sem("s5_ut_kept"), a.sem("mi_stored"), a.sem("kd_ready")
        ident = cst["ident"]
        x_d = io["x"][0].rearrange("(p s) d -> p s d", s=NT)
        w_d = io["w_in"][0].rearrange("(q k) n -> q k n", k=KD)
        b_row = io["b_in"]
        TURNS = SSM_G // 4
        ps_ut = ps_u[:, 0].rearrange("p a (b c) -> p (a b) c", b=2)
        ps_wt = ps_u[:, 1].rearrange("p a (b c) -> p a b c", b=2)
        ps_k = ps_u[:, 2].rearrange("p a (b c) -> p (a b) c", b=2)
        ps_v = ps_u[:, 3].rearrange("p a (b c) -> p a b c", b=2)
        N_PAR = 4

        def split_hi(act, n):
            act.wait_ge(ld_w, 16 * (n // KD + 1))
            if n >= WR:
                act.wait_ge(w_used, n - WR + 1)
            act.activation(w_hi[:, n % WR, :], w_raw[:, n % KD, :], ACT.Copy).then_inc(w_hi_made, 1)

        def s5_inputs(dve, ch):
            dve.wait_ge(par_ready, 1)
            dve.wait_ge(ld_par, 16 * (2 + 8 + 1))
            fr, fi = (par[n][:, :].unsqueeze(2).broadcast_to((P, PAIRS, SSM_C)) for n in ("fac_re", "fac_im"))
            pb = [prod[j][:, 0:PAIRS * SSM_C].rearrange("p (a c) -> p a c", c=SSM_C) for j in range(2)]
            for part, op in enumerate((ALU.subtract, ALU.add)):
                ch(dve.tensor_tensor(pb[0], b_raw[:, part, :, :], fr, ALU.mult))
                ch.do(dve.tensor_tensor(pb[1], b_raw[:, 1 - part, :, :], fi, ALU.mult))
                ch.do(dve.tensor_tensor(b_bar[:, part, :, :], pb[0], pb[1], op))

        def s5_outputs(dve, ch, step):
            W4 = (P, PAIRS, T + 1, SSM_C)
            pp = [prod[j][:, 0:PAIRS * (T + 1) * SSM_C].rearrange("p (a t c) -> p a t c", t=T + 1, c=SSM_C) for j in range(2)]
            cc = [c_col[:, j, :, :].unsqueeze(2).broadcast_to(W4) for j in range(2)]
            power = [par[n][:, :, :].unsqueeze(3).broadcast_to(W4) for n in ("pow_re", "pow_im")]
            part, step = divmod(step, 3)
            if step < 2:
                if (part, step) == (0, 0):
                    dve.wait_ge(p_copied, N_PAR)
                ch.do(dve.tensor_tensor(pp[step], cc[step], power[(step + part) % 2], ALU.mult))
            elif part == 0:
                ch.do(dve.tensor_tensor(c_pow[:, 0], pp[0], pp[1], ALU.subtract))
            else:
                ch.do(dve.scalar_tensor_tensor(out=c_pow[:, 1], in0=pp[0], scalar=-1.0, in1=pp[1],
                                               op0=ALU.mult, op1=ALU.subtract))
                dve.sem_inc(cpow_ready, 1)

        with nc.Block() as block:
            @block.sync
            def _(sp):
                for s in range(NT):
                    if s >= XR:
                        sp.wait_ge(x_turned, 2 * (s - XR + 1))
                    sp.dma_start(x_tok[:, s % XR, :], x_d[:, s, :]).then_inc(ld_x[s % XR], 16)
                    if s == 0:
                        sp.dma_start(w_raw[:, :, :], w_d[:, :, 0:256]).then_inc(ld_w, 16)
                sp.wait_ge(w_hi_made, KD)
                sp.wait_ge(w_lo_made, KD)
                sp.dma_start(w_raw[:, :, :], w_d[:, :, 256:512]).then_inc(ld_w, 16)

                sp.wait_ge(cpow_ready, 1)
                sp.dma_start(scr["c_pow"], c_pow[:, :, :, :, :].rearrange("p a b c d -> p (a b c d)")).then_inc(stored, 16)
                sp.wait_ge(zero_ready, 1)
                sp.dma_start(scr["k_pad"][:, :, 0:KP0], zeros[:, :].unsqueeze(1).broadcast_to((SSM_C, SSM_G, KP0))).then_inc(stored, 16)
                sp.wait_ge(kd_ready, 1)
                sp.dma_start(scr["k_pad"][:, :, KP0:KP0 + P], k_resp[:, :, :]).then_inc(stored, 16)
                sp.wait_ge(stored, 48)

            @block.gpsimd
            def _(pool):
                cst["write"](pool)
                pool.memset(zeros[:, :], 0.0).then_inc(zero_ready, 1)
                pool.memset(b_pad[:, :, :, :], 0.0).then_inc(zero_ready, 1)
                pool.wait_ge(lam_copied, 4)
                t = {"raw": lam_raw, "scratch": scratch, "bits": bits, "rden": rden,
                     "den": None, "den_ready": den_ready, "rden_ready": rden_ready}
                s5_parameters(pool, pool_ch, t, par)
                pool.sem_inc(par_ready, 1)
                with pool.Fori(0, TURNS) as it:
                    pool.wait_ge(copied_u, it + 1)
                    pool.tensor_copy(keep["ut_all"][:, bass.ds(it * 512, 512)],
                                     ut_stage[:, :, :].rearrange("p a b -> p (a b)")).then_inc(ut_kept, 1)

            @block.tensor
            def _(pe):
                pe.wait_ge(cst["ready"], 1)
                pe.wait_ge(ld_lam, 16 * 3)
                pe.wait_ge(dt_ready, 1)
                pe.transpose(ps_x[:, 2, 0:NB_COL], bias_rows[:, :], ident[0:NB_COL, 0:NB_COL])
                for j in range(3):
                    ins = pe.transpose(ps_x[:, 3, 32 * j:32 * j + PAIRS], lam_rows[:, j, :], ident[0:PAIRS, 0:PAIRS])
                ins.then_inc(p_turned, 1)
                for s in range(NT):
                    pe.wait_ge(ld_x[s % XR], 16 * (s // XR + 1))
                    if s == 1:
                        pe.wait_ge(lam_copied, 4)
                    for h in range(2):
                        n = 2 * s + h
                        if n >= 4:
                            pe.wait_ge(x_hi_made, n - 3)
                            pe.wait_ge(x_lo_made, n - 3)
                        for j in range(4):
                            ins = pe.transpose(ps_x[:, n % 4, P * j:P * j + P],
                                               x_tok[:, s % XR, 4 * h + j:D:KD], ident[:, :])
                        ins.then_inc(x_turned, 1)
                pe.wait_ge(x_hi_made, 2 * NT)
                pe.wait_ge(x_lo_made, 2 * NT)
                pe.wait_ge(ld_par, 16 * (2 + 8 + 1))
                for j in range(4):
                    ins = pe.transpose(ps_x[:, 2, P * j:P * j + P], c_rows[:, j // 2, j % 2, :], ident[:, :])
                ins.then_inc(p_turned, 1)
                for half in range(2):
                    if half:
                        pe.wait_ge(u_evac, NT)
                    for k in range(KD):
                        n = half * KD + k
                        pe.wait_ge(w_hi_made, n + 1)
                        pe.wait_ge(w_lo_made, n + 1)
                        for s in range(NT):
                            ins = mm3(pe, ps_u[:, s // 2, s % 2, :], xT_hi[:, k, s:L:NT], xT_lo[:, k, s:L:NT],
                                      w_hi[:, n % WR, :], w_lo[:, n % WR, :], k == 0 and s % 2 == 0, k == KD - 1)
                        ins.then_inc(w_used, 1)
                pe.wait_ge(u_evac, 2 * NT)
                pe.wait_ge(cpow_ready, 1)
                with pe.Fori(0, TURNS) as it:
                    pe.wait_ge(staged, it + 1)
                    for g in range(4):
                        pe.transpose(ps_ut[:, g, :], u_stage[:, g, :], ident[:, :])
                    for j in range(4):
                        ins = pe.transpose(ps_wt[:, j // 2, j % 2, :], w_stage[:, j // 2, j % 2, :], ident[:, :])
                    ins.then_inc(turned, 1)
                    pe.wait_ge(k_copied, it)
                    for g in range(4):
                        for part in range(2):
                            rhs = c_pow[:, part, bass.ds(2 * it + g // 2, 1), 0:T, :]
                            ins = pe.matmul(ps_k[0:SSM_C, g, :], b_pad[:, g, part, :],
                                            rhs.rearrange("p o t c -> p (o t c)"),
                                            start=(part == 0), stop=(part == 1))
                    ins.then_inc(k_done, 1)
                    pe.wait_ge(copied_u, it + 1)
                    pe.wait_ge(copied_w, it + 1)
                    pe.wait_ge(v_copied, it)
                    for j in range(2):
                        for part in range(2):
                            for g2 in range(2):
                                ins = pe.matmul(ps_v[64 * g2:64 * g2 + 64, j, part, :],
                                                wt_stage[:, j, part, 64 * g2:64 * g2 + 64],
                                                ut_stage[:, 2 * j + g2, :],
                                                start=True, stop=True)
                    ins.then_inc(v_done, 1)

            @block.scalar
            def _(act):
                act.dma_start(dt_rows[:, :], io["ssm_log_dt"][0].rearrange("(a g) -> a g", g=2)).then_inc(ld_dt, 16)
                act.dma_start(bias_rows[:, :], b_row[0].rearrange("(c p) -> c p", p=P)).then_inc(ld_lam, 16)
                act.dma_start(lam_rows[:, 0, :], io["ssm_lam_re"][0].rearrange("(a g) n -> a (g n)", g=2)).then_inc(ld_lam, 16)
                act.dma_start(lam_rows[:, 1, :], io["ssm_lam_im"][0].rearrange("(a g) n -> a (g n)", g=2)).then_inc(ld_lam, 16)
                for j, n in enumerate(("ssm_b_re", "ssm_b_im")):
                    act.dma_start(b_raw[:, j, :, :], io[n][0].rearrange("(a g) n c -> (g n) a c", g=2)).then_inc(ld_par, 16)
                for j, n in enumerate(("ssm_c_re", "ssm_c_im")):
                    for half in range(2):
                        for g in range(2):
                            act.dma_start(c_rows[:, j, half, SSM_N * g:SSM_N * g + SSM_N],
                                          io[n][0, 16 * half + g:16 * half + 16:2]).then_inc(ld_par, 16)
                act.dma_start(d_row[:, :, :], io["ssm_d"].rearrange("o g c -> o (g c)").broadcast_to((SSM_C, SSM_G * SSM_C))
                              .rearrange("p (g c) -> p g c", c=SSM_C)).then_inc(ld_par, 16)
                act.dma_start(bias_u[:, :], b_row[:, 0:SSM_W].broadcast_to((P, SSM_W))).then_inc(ld_bias, 16)
                act.wait_ge(ld_dt, 16)
                act.activation(lam_rows[:, 2, :].rearrange("a (g n) -> a g n", g=2),
                               dt_rows[:, :].unsqueeze(2).broadcast_to((PAIRS, 2, SSM_N)), ACT.Copy).then_inc(dt_ready, 1)
                act.wait_ge(p_turned, 1)
                act.activation(keep["bias_T"][:, :], ps_x[:, 2, 0:NB_COL], ACT.Copy).then_inc(lam_copied, 1)
                for j in range(3):
                    act.activation(lam_raw[:, j, :], ps_x[:, 3, 32 * j:32 * j + PAIRS], ACT.Copy).then_inc(lam_copied, 1)
                for n in range(2 * NT):
                    act.wait_ge(x_turned, n + 1)
                    s, h = n // 2, n % 2
                    act.activation(xT_hi[:, 4 * h:4 * h + 4, s:L:NT],
                                   ps_x[:, n % 4, :].rearrange("p (k t) -> p k t", k=4), ACT.Copy).then_inc(x_hi_made, 1)
                    if n == 1:
                        for k in range(WR):
                            split_hi(act, k)
                act.wait_ge(p_turned, 2)
                for j in range(4):
                    act.activation(c_col[:, j // 2, 8 * (j % 2):8 * (j % 2) + 8, :],
                                   ps_x[:, 2, P * j:P * j + P].rearrange("p (a c) -> p a c", c=SSM_C), ACT.Copy).then_inc(p_copied, 1)
                for n in range(WR, 2 * KD):
                    split_hi(act, n)
                with act.Fori(0, TURNS) as it:
                    act.wait_ge(turned, it + 1)
                    act.wait_ge(ut_kept, it)
                    act.wait_ge(v_done, it)
                    act.activation(ut_stage[:, :, :], ps_ut, ACT.Copy).then_inc(copied_u, 1)
                    act.activation(wt_stage[:, :, :, :], ps_wt, ACT.Copy).then_inc(copied_w, 1)
                    act.wait_ge(k_done, it + 1)
                    act.activation(k_resp[:, bass.ds(4 * it, 4), :], ps_k[0:SSM_C, :, :], ACT.Copy).then_inc(k_copied, 1)

            @block.vector
            def _(dve):
                ch = Chain(dve, dve_ch)

                def split_lo(n):
                    dve.wait_ge(w_hi_made, n + 1)
                    dve.tensor_tensor(w_lo[:, n % WR, :], w_raw[:, n % KD, :], w_hi[:, n % WR, :].bitcast(F32),
                                      ALU.subtract).then_inc(w_lo_made, 1)

                for n in range(2 * NT):
                    dve.wait_ge(x_hi_made, n + 1)
                    s, h = n // 2, n % 2
                    dve.tensor_tensor(xT_lo[:, 4 * h:4 * h + 4, s:L:NT], ps_x[:, n % 4, :].rearrange("p (k t) -> p k t", k=4),
                                      xT_hi[:, 4 * h:4 * h + 4, s:L:NT].bitcast(F32), ALU.subtract).then_inc(x_lo_made, 1)
                    if n == 4:
                        for k in range(WR):
                            split_lo(k)
                for n in range(WR, KD):
                    split_lo(n)
                    if n == WR:
                        dve.wait_ge(den_ready, 1)
                        dve.reciprocal(rden[:, :], scratch[:, 11, :]).then_inc(rden_ready, 1)
                dve.wait_ge(ld_bias, 16)
                for half in range(2):
                    dve.wait_ge(w_used, KD * (half + 1))
                    for s in range(NT):
                        dve.tensor_tensor(u_tok[:, s, 256 * half:256 * half + 256], ps_u[:, s // 2, s % 2, :],
                                          bias_u[:, 256 * half:256 * half + 256], ALU.add).then_inc(u_evac, 1)
                    if half == 0:
                        for n in range(KD, 2 * KD):
                            split_lo(n)
                            if n == KD + 3:
                                s5_inputs(dve, ch)
                            if n > KD + 3:
                                s5_outputs(dve, ch, n - KD - 4)
                        for step in (4, 5):
                            s5_outputs(dve, ch, step)
                dve.wait_ge(u_evac, 2 * NT)
                dve.wait_ge(zero_ready, 2)

                def stage(it, first=False):
                    if not first:
                        dve.wait_ge(turned, it)
                    for j in range(2):
                        for n, (w, part) in enumerate((("re", 0), ("im", 1), ("re", 1), ("im", 0))):
                            power = par["rpow_" + w][:, bass.ds(2 * it + j, 1), :].rearrange("p o s -> p (o s)")
                            ins = dve.tensor_tensor(w_prod[:, n, j, :].rearrange("p (s c) -> p s c", s=T),
                                                    power.unsqueeze(2).broadcast_to((P, T, SSM_C)),
                                                    b_bar[:, part, bass.ds(2 * it + j, 1), :].broadcast_to((P, T, SSM_C)), ALU.mult)
                    ch(ins)
                    for g in range(4):
                        ch(dve.tensor_copy(u_stage[:, g, :].rearrange("p (s c) -> p s c", s=T),
                                           u_tok[:, :, bass.ds(64 * it + 16 * g, 16)]))
                    if not first:
                        dve.wait_ge(k_done, it)
                    for g in range(4):
                        for part in range(2):
                            rows = slice(64 * (g % 2), 64 * (g % 2) + 64)
                            ins = dve.tensor_scalar(b_pad[rows, g, part, :],
                                                    b_bar[rows, part, bass.ds(2 * it + g // 2, 1), :].rearrange("p o c -> p (o c)"),
                                                    1.0, None, ALU.mult)
                    ch(ins)
                    ch.sync()
                    dve.tensor_tensor(w_stage[:, :, 0, :], w_prod[:, 0, :, :], w_prod[:, 1, :, :], ALU.subtract)
                    dve.tensor_tensor(w_stage[:, :, 1, :], w_prod[:, 2, :, :], w_prod[:, 3, :, :], ALU.add).then_inc(staged, 1)

                def keep_states(it):
                    dve.wait_ge(v_done, it + 1)
                    dve.tensor_copy(keep["states"][:, :, bass.ds(2 * it, 2), 1:NCH + 1],
                                    ps_v.rearrange("p a r k -> p r a k")).then_inc(v_copied, 1)

                stage(0, first=True)
                with dve.Fori(0, TURNS - 1) as it:
                    ch.loop(it, 6)
                    stage(it + 1)
                    keep_states(it)
                ch.end_loop(TURNS - 1)
                keep_states(TURNS - 1)
                dve.wait_ge(k_copied, TURNS)
                eye = ident[0:SSM_C, 0:SSM_C].unsqueeze(1).broadcast_to((SSM_C, SSM_G, SSM_C))
                ch.do(dve.tensor_tensor(d_row[:, :, :], d_row[:, :, :], eye, ALU.mult))
                dve.tensor_tensor(k_resp[:, :, 0:SSM_C], k_resp[:, :, 0:SSM_C], d_row[:, :, :],
                                  ALU.add).then_inc(kd_ready, 1)


def attention(nc, m, cst, io, xT_hi, xT_lo, keep, scr):
    with ExitStack() as stack:
        a = Memory(nc, stack)
        WR = 4
        NBLK, NU = 8, 16
        w_raw = a.sb("v_w_raw", [P, KD, 256])
        w_hi = a.sb("v_w_hi", [P, WR, 256], F32R)
        w_lo = a.sb("v_w_lo", [P, WR, 256], F32R)
        bias_v = a.sb("bias_v", [P, 512])
        v_cur = a.sb("v_cur", [P, NBLK, 512])
        qk_raw = [a.sb(n + "_w_raw", [P, KD, P]) for n in "qk"]
        qk_hi = [a.sb(n + "_w_hi", [P, KD, P], F32R) for n in "qk"]
        qk_lo = [a.sb(n + "_w_lo", [P, KD, P], F32R) for n in "qk"]
        nxt = [a.sb(n + "_next", [P, L]) for n in "qk"]
        cur = [a.sb(n + "_cur", [P, L]) for n in "qk"]
        probs = a.sb("probs", [P, 2, 256])
        probs_T = a.sb("probs_T", [P, 2, 256])
        o_stage = a.sb("o_stage", [P, NBLK, 2 * ROW])
        scan_prod = a.sb("scan_prod", [P, 2, 2 * PAIRS])
        ps_st = a.ps("ps_st", [P, 4, 512])
        ps_o = a.ps("ps_o", [P, 2, 512])
        ps_p = a.ps("ps_p", [P, 2, 512])
        ld_vw, ld_bv = a.sem("ld_vw"), a.sem("ld_bv")
        ld_qk = [a.sem("ld_qw"), a.sem("ld_kw")]
        vw_hi_made, vw_lo_made, vw_used, v_evac = a.sem("vw_hi_made"), a.sem("vw_lo_made"), a.sem("vw_used"), a.sem("v_evac")
        qk_hi_made = [a.sem("qw_hi_made"), a.sem("kw_hi_made")]
        qk_lo_made = [a.sem("qw_lo_made"), a.sem("kw_lo_made")]
        proj_done, proj_q_evac, proj_k_evac = a.sem("proj_done"), a.sem("proj_q_evac"), a.sem("proj_k_evac")
        cur_ready = a.sem("cur_ready")
        s_ready, m_ready, p_ready = a.sem("scores_ready"), a.sem("max_ready"), a.sem("probs_ready")
        t_ready = a.sem("turned_ready")
        tc_even, tc_odd = a.sem("probs_T_even"), a.sem("probs_T_odd")
        o_ready, o_evac = a.sem("o_ready"), a.sem("o_evac")
        stored = [a.sem("o_stored_0"), a.sem("o_stored_1")]
        scan_sem = a.sem("scan_chain")
        identb, ident = cst["identb"], cst["ident"]
        w_d = io["w_in"][0].rearrange("(q k) n -> q k n", k=KD)
        b_d = io["b_in"]

        def has_before(g, blk):
            return (blk > 0, blk >= 4, False)[g]

        def block_before(g, blk):
            return (blk - 1, blk - 4, None)[g]

        def tokens(rows, g, blk, before=False):
            n = 2 * P if before else P
            if g == 0:
                at = P * blk - (P if before else 0)
                return rows[:, at:at + n]
            if g == 1:
                nb, r = divmod(blk, 4)
                at = 512 * nb + r - (512 if before else 0)
                return rows[:, at:at + 4 * (n - 1) + 1:4]
            return rows[:, blk:L:8]


        def unit(u):
            return u // 2, u % 2

        def sp_load_v(sp, g, half):
            sp.dma_start(w_raw[:, :, :], w_d[:, :, C_V + 512 * g + 256 * half:C_V + 512 * g + 256 * half + 256]).then_inc(ld_vw, 16)

        def sp_load_qk(sp, which, h):
            sp.dma_start(qk_raw[which][:, :, :], w_d[:, :, bass.ds((C_Q, C_K)[which] + P * h, P)]).then_inc(ld_qk[which], 16)

        def sp_store(sp, g, hp, half):
            cols = bass.ds(2 * ROW * hp, 2 * ROW)
            rows = scr["att"][g]
            src = o_stage[:, 4 * half:4 * half + 4, :]
            if g == 0:
                dst = rows.rearrange("(b p) c -> p b c", p=P)[:, 4 * half:4 * half + 4, cols]
            elif g == 1:
                dst = rows.rearrange("(b p r) c -> b p r c", b=2, r=4)[half, :, :, cols]
            else:
                dst = rows.rearrange("(p b) c -> p b c", b=8)[:, 4 * half:4 * half + 4, cols]
            sp.dma_start(dst, src).then_inc(stored[half], 16)

        def sp_turn(sp, g, hp, h, ahead):
            for half in range(2):
                if ahead:
                    which = 1 - half
                    sp.wait_ge(qk_lo_made[which], h + 2 + half)
                    sp_load_qk(sp, which, h + 2 + half)
                sp.wait_ge(o_evac, NU * h + 8 * (half + 1))
                sp.wait_ge(p_ready, NU * h + 8 * (half + 1))
                sp_store(sp, g, hp, half)

        def act_split(act, which, n, first=False):
            act.wait_ge(ld_qk[which], 16 * n)
            if not first:
                act.wait_ge(proj_done, 4 * (n - 1) - (0 if which else 2))
            act.activation(qk_hi[which][:, :, :], qk_raw[which][:, :, :], ACT.Copy).then_inc(qk_hi_made[which], 1)

        def dve_split(dve, which, n):
            dve.wait_ge(qk_hi_made[which], n)
            dve.tensor_tensor(qk_lo[which][:, :, :], qk_raw[which][:, :, :], qk_hi[which][:, :, :].bitcast(F32),
                              ALU.subtract).then_inc(qk_lo_made[which], 1)

        def pe_project(pe, step, h):
            quarter, part = divmod(step, 4)
            which, half = divmod(quarter, 2)
            if part == 0:
                if half == 0:
                    pe.wait_ge(qk_lo_made[which], h + 1)
                if which == 0:
                    pe.wait_ge(proj_k_evac, 2 * h)
                else:
                    pe.wait_ge(proj_q_evac, 2 * h + half + 1)
            for k in (2 * part, 2 * part + 1):
                ins = mm3(pe, ps_p[:, quarter % 2, :], qk_hi[which][:, k, :], qk_lo[which][:, k, :],
                          xT_hi[:, k, 512 * half:512 * half + 512], xT_lo[:, k, 512 * half:512 * half + 512],
                          k == 0, k == KD - 1)
            if part == 3:
                ins.then_inc(proj_done, 1)

        def dve_q_evac(dve, half, h):
            dve.wait_ge(proj_done, 4 * h + half + 1)
            dve.tensor_scalar(nxt[0][:, 512 * half:512 * half + 512], ps_p[:, half, :],
                              keep["bias_T"][:, bass.ds(C_Q // P + h, 1)], DH ** -0.5, ALU.add, ALU.mult).then_inc(proj_q_evac, 1)

        def dve_k_evac(dve, half, h):
            dve.wait_ge(proj_done, 4 * h + half + 3)
            dve.tensor_scalar(nxt[1][:, 512 * half:512 * half + 512], ps_p[:, half, :],
                              keep["bias_T"][:, bass.ds(C_K // P + h, 1)], 0.0, ALU.add, ALU.add).then_inc(proj_k_evac, 1)

        def pe_turn(pe, g, hp, h, ahead):
            pe.wait_ge(cur_ready, 2 * h + 2)
            for u in range(NU + 2):
                if u < NU:
                    blk, h2 = unit(u)
                    rows = slice(64 * h2, 64 * h2 + 64)
                    before = has_before(g, blk)
                    out = ps_st[:, u % 2, 0:256 if before else P]
                    if u >= 2:
                        pe.wait_ge(p_ready, NU * h + u - 1)
                    mask = cst["mask_pair"][:, :] if g == 2 else cst["mask_band"][:, 0 if before else P:2 * P]
                    pe.matmul(out, identb[:, :], mask, start=True, stop=False, skip_group_check=True)
                    pe.matmul(out, tokens(cur[0][rows, :], g, blk), tokens(cur[1][rows, :], g, blk, before),
                              start=False, stop=True, skip_group_check=True).then_inc(s_ready, 1)
                    if ahead:
                        for step in (0, 1) if u == 0 else (u + 1,) if u + 1 < 16 else ():
                            pe_project(pe, step, h + 1)
                if 1 <= u <= NU:
                    v = u - 1
                    blk, h2 = unit(v)
                    pe.wait_ge(p_ready, NU * h + v + 1)
                    if v >= 2:
                        pe.wait_ge((tc_even, tc_odd)[v % 2], 8 * h + v // 2)
                    for j in range(2 if has_before(g, blk) else 1):
                        ins = pe.transpose(ps_st[:, 2 + v % 2, P * j:P * j + P], probs[:, v % 2, P * j:P * j + P], ident[:, :])
                    ins.then_inc(t_ready, 1)
                if u >= 2:
                    v = u - 2
                    blk, h2 = unit(v)
                    pe.wait_ge((tc_even, tc_odd)[v % 2], 8 * h + v // 2 + 1)
                    pe.wait_ge(o_evac, NU * h + max(0, v - 1))
                    blocks = [block_before(g, blk), blk] if has_before(g, blk) else [blk]
                    for j, kb in enumerate(blocks):
                        ins = pe.matmul(ps_o[:, v % 2, 0:DH], probs_T[:, v % 2, P * j:P * j + P],
                                        v_cur[:, kb, bass.ds(P * hp + DH * h2, DH)],
                                        start=(j == 0), stop=(j == len(blocks) - 1))
                    ins.then_inc(o_ready, 1)

        def dve_next_q(dve, h):
            dve.wait_ge(s_ready, NU * h)
            dve.wait_ge(proj_q_evac, 2 * h + 2)
            dve.tensor_copy(cur[0][:, :], nxt[0][:, :]).then_inc(cur_ready, 1)

        def act_next_k(act, h):
            act.wait_ge(s_ready, NU * h)
            act.wait_ge(proj_k_evac, 2 * h + 2)
            act.activation(cur[1][:, :], nxt[1][:, :], ACT.Copy).then_inc(cur_ready, 1)

        def dve_turn(dve, g, hp, h, ahead):
            for u in range(NU + 2):
                if u < NU:
                    blk, h2 = unit(u)
                    n = 256 if has_before(g, blk) else P
                    if u % 8 == 0:
                        dve.wait_ge(stored[u // 8], 16 * h)
                    dve.wait_ge(s_ready, NU * h + u + 1)
                    dve.tensor_reduce(o_stage[:, blk, ROW * h2 + DH + 1:ROW * h2 + DH + 2], ps_st[:, u % 2, 0:n],
                                      AX.X, ALU.max, negate=True).then_inc(m_ready, 1)
                if 1 <= u <= NU and (u - 1) % 2:
                    v = u - 1
                    n = 256 if has_before(g, unit(v)[0]) else P
                    dve.wait_ge(t_ready, NU * h + v + 1)
                    if v >= 2:
                        dve.wait_ge(o_ready, NU * h + v - 1)
                    dve.tensor_copy(probs_T[:, 1, 0:n], ps_st[:, 3, 0:n]).then_inc(tc_odd, 1)
                if u >= 2:
                    v = u - 2
                    blk, h2 = unit(v)
                    dve.wait_ge(o_ready, NU * h + v + 1)
                    dve.tensor_copy(o_stage[:, blk, ROW * h2:ROW * h2 + DH], ps_o[:, v % 2, 0:DH]).then_inc(o_evac, 1)
                if ahead:
                    if u == 1:
                        dve_split(dve, 1, h + 2)
                    if u == 10:
                        dve_split(dve, 0, h + 3)
                    if u in (4, 8):
                        dve_q_evac(dve, u // 4 - 1, h + 1)
                    if u in (12, 15):
                        dve_k_evac(dve, 0 if u == 12 else 1, h + 1)
                    if u == 16:
                        dve_next_q(dve, h + 1)

        def act_turn(act, g, hp, h, ahead):
            for u in range(NU + 1):
                if u < NU:
                    blk, h2 = unit(u)
                    n = 256 if has_before(g, blk) else P
                    act.wait_ge(m_ready, NU * h + u + 1)
                    if u >= 2:
                        act.wait_ge(t_ready, NU * h + u - 1)
                    at = ROW * h2 + DH
                    act.activation(probs[:, u % 2, 0:n], ps_st[:, u % 2, 0:n], ACT.Exp,
                                   bias=o_stage[:, blk, at + 1:at + 2],
                                   accum_out=o_stage[:, blk, at:at + 1]).then_inc(p_ready, 1)
                if u >= 1 and (u - 1) % 2 == 0:
                    v = u - 1
                    n = 256 if has_before(g, unit(v)[0]) else P
                    act.wait_ge(t_ready, NU * h + v + 1)
                    if v >= 2:
                        act.wait_ge(o_ready, NU * h + v - 1)
                    act.activation(probs_T[:, 0, 0:n], ps_st[:, 2, 0:n], ACT.Copy).then_inc(tc_even, 1)
                if ahead:
                    if u == 0:
                        act_split(act, 1, h + 2)
                    if u == 9:
                        act_split(act, 0, h + 3)
                    if u == 16:
                        act_next_k(act, h + 1)

        def turns(eng, g, turn):
            n = HP if g < NG - 1 else HP - 1
            with eng.Fori(0, n) as hp:
                turn(eng, g, hp, HP * g + hp, True)
            if n < HP:
                turn(eng, g, n, HP * g + n, False)

        with nc.Block() as block:
            @block.sync
            def _(sp):
                sp_load_qk(sp, 0, 0)
                sp_load_qk(sp, 1, 0)
                sp_load_v(sp, 0, 0)
                for which, n in ((0, 1), (1, 1), (0, 2)):
                    sp.wait_ge(qk_lo_made[which], n)
                    sp_load_qk(sp, which, n)
                for g in range(NG):
                    sp.wait_ge(vw_lo_made, 2 * KD * g + KD)
                    sp_load_v(sp, g, 1)
                    sp.wait_ge(v_evac, 8 * g + 4)
                    if g + 1 < NG:
                        sp.wait_ge(vw_lo_made, 2 * KD * (g + 1))
                        sp_load_v(sp, g + 1, 0)
                    turns(sp, g, sp_turn)
                for half in range(2):
                    sp.wait_ge(stored[half], 16 * NG * HP)

            @block.tensor
            def _(pe):
                for step in range(16):
                    pe_project(pe, step, 0)
                for g in range(NG):
                    for half in range(2):
                        if g and not half:
                            pe.wait_ge(v_evac, 8 * g)
                        if g and not half:
                            pe.wait_ge(o_evac, NU * HP * g)
                            pe.wait_ge(tc_odd, 8 * HP * g)
                        for k in range(KD):
                            n = 2 * KD * g + KD * half + k
                            pe.wait_ge(vw_lo_made, n + 1)
                            for blk in range(NBLK):
                                if half and k == 0 and blk % 2 == 0:
                                    pe.wait_ge(v_evac, 8 * g + blk // 2 + 1)
                                lhs = [tokens(x[:, k, :], g, blk) for x in (xT_hi, xT_lo)]
                                ins = mm3(pe, ps_st[:, blk // 2, 256 * (blk % 2):256 * (blk % 2) + 256], lhs[0], lhs[1],
                                          w_hi[:, n % WR, :], w_lo[:, n % WR, :], k == 0 and blk % 2 == 0, k == KD - 1)
                            ins.then_inc(vw_used, 1)
                    pe.wait_ge(v_evac, 8 * (g + 1))
                    turns(pe, g, pe_turn)

            @block.scalar
            def _(act):
                act_split(act, 0, 1, first=True)
                act_split(act, 1, 1, first=True)
                act_split(act, 0, 2)
                act_next_k(act, 0)
                for g in range(NG):
                    if g:
                        act.wait_ge(v_evac, 8 * g)
                    act.dma_start(bias_v[:, :], b_d[:, C_V + 512 * g:C_V + 512 * g + 512].broadcast_to((P, 512))).then_inc(ld_bv, 16)
                    for n in range(2 * KD * g, 2 * KD * (g + 1)):
                        act.wait_ge(ld_vw, 16 * (n // KD + 1))
                        if n >= WR:
                            act.wait_ge(vw_used, n - WR + 1)
                        act.activation(w_hi[:, n % WR, :], w_raw[:, n % KD, :], ACT.Copy).then_inc(vw_hi_made, 1)
                    turns(act, g, act_turn)

            @block.vector
            def _(dve):
                dve_split(dve, 0, 1)
                dve_split(dve, 1, 1)
                for half in range(2):
                    dve_q_evac(dve, half, 0)
                for half in range(2):
                    dve_k_evac(dve, half, 0)
                dve_split(dve, 0, 2)
                dve_next_q(dve, 0)
                for g in range(NG):
                    for half in range(2):
                        for n in range(2 * KD * g + KD * half, 2 * KD * g + KD * half + KD):
                            dve.wait_ge(vw_hi_made, n + 1)
                            dve.tensor_tensor(w_lo[:, n % WR, :], w_raw[:, n % KD, :], w_hi[:, n % WR, :].bitcast(F32),
                                              ALU.subtract).then_inc(vw_lo_made, 1)
                        dve.wait_ge(vw_used, 2 * KD * g + KD * (half + 1))
                        dve.wait_ge(ld_bv, 16 * (g + 1))
                        bias = bias_v[:, 256 * half:256 * half + 256].unsqueeze(1).broadcast_to((P, 2, 256))
                        for j in range(4):
                            dve.tensor_tensor(v_cur[:, 2 * j:2 * j + 2, 256 * half:256 * half + 256],
                                              ps_st[:, j, :].rearrange("p (b c) -> p b c", b=2), bias, ALU.add).then_inc(v_evac, 1)
                    turns(dve, g, dve_turn)

            @block.gpsimd
            def _(pool):
                ch = Chain(pool, scan_sem)
                st = keep["states"][:, :, :, :].rearrange("p r a k -> p (r a) k")
                fac = keep["scan_fac"]
                ch.do(pool.memset(st[:, :, 0:1], 0.0))
                with pool.Fori(2, NCH + 1) as k:
                    ch.loop(k - 2, 4)
                    now = lambda lo, hi: st[:, lo:hi, bass.ds(k, 1)]
                    before = st[:, :, bass.ds(k - 1, 1)].rearrange("p a o -> p (a o)").unsqueeze(1).broadcast_to((P, 2, 2 * PAIRS))
                    col = lambda j, lo, hi: scan_prod[:, j, lo:hi].unsqueeze(2)
                    ch.do(pool.tensor_tensor(scan_prod[:, :, :], fac[:, :, :], before, ALU.mult))
                    ch.do(pool.tensor_tensor(now(0, 2 * PAIRS), now(0, 2 * PAIRS), col(0, 0, 2 * PAIRS), ALU.add))
                    ch(pool.tensor_tensor(now(PAIRS, 2 * PAIRS), now(PAIRS, 2 * PAIRS), col(1, 0, PAIRS), ALU.add))
                    ch.do(pool.tensor_tensor(now(0, PAIRS), now(0, PAIRS), col(1, PAIRS, 2 * PAIRS), ALU.add))
                ch.end_loop(NCH - 1)


def branch_outputs(nc, m, cst, io, keep, scr, ya_hi, ya_lo, y_tok):
    with ExitStack() as stack:
        a = Memory(nc, stack)
        c_pow = a.sb("c_pow_in", [P, 2, PAIRS, T + 1, SSM_C])
        k_op = a.sb("k_op", [P, SSM_G, P])
        NB = 3
        att = a.sb("att_in", [P, NB, NG, NH * ROW])
        wts = a.sb("att_wts", [P, 2, 4, NG, NH])
        low = a.sb("att_low", [P, 2, NH])
        den = a.sb("att_den", [P, 2, 2, NH])
        y_att = a.sb("y_att", [P, 2, NH * DH])
        ps_y = a.ps("ps_y", [P, 2, 2, 512])
        ps_a = a.ps("ps_a", [P, 2, 512])
        ld_c, ld_k = ([a.sem(f"ld_{n}{j}") for j in range(2)] for n in ("cpow", "kop"))
        ld_att = [a.sem(f"ld_att{j}") for j in range(NB)]
        y_done, y_evac = a.sem("y_done"), a.sem("y_evac")
        shift_ready, exp_ready, wts_ready, parts_ready = a.sem("shift_ready"), a.sem("exp_ready"), a.sem("wts_ready"), a.sem("parts_ready")
        ya_ready, ya_turned, ya_hi_made, ya_lo_made = a.sem("ya_ready"), a.sem("ya_turned"), a.sem("ya_hi_made"), a.sem("ya_lo_made")
        dve_sem = a.sem("bo_dve_ch")
        ident = cst["ident"]
        att_d = scr["att"].rearrange("g (p s) c -> p s g c", s=NT)
        ut, st = keep["ut_all"], keep["states"]
        TURNS = SSM_G // 4

        with nc.Block() as block:
            @block.sync
            def _(sp):
                def operators(half):
                    pairs, groups = slice(PAIRS // 2 * half, PAIRS // 2 * (half + 1)), slice(SSM_G // 2 * half, SSM_G // 2 * (half + 1))
                    for part in range(2):
                        sp.dma_start(c_pow[:, part, pairs, :, :].rearrange("p a t c -> p (a t c)"),
                                     scr["c_pow"].rearrange("p (r a w) -> p r a w", r=2, a=PAIRS)[:, part, pairs, :]
                                     .rearrange("p a w -> p (a w)")).then_inc(ld_c[half], 16)
                    for t in range(T):
                        sp.dma_start(k_op[SSM_C * t:SSM_C * t + SSM_C, groups, :],
                                     scr["k_pad"][:, groups, KP0 - SSM_C * t:KP0 - SSM_C * t + P]).then_inc(ld_k[half], 16)

                operators(0)
                for s in range(NT):
                    if s >= NB:
                        sp.wait_ge(ya_ready, s - NB + 1)
                    sp.dma_start(att[:, s % NB, :, :], att_d[:, s, :, :]).then_inc(ld_att[s % NB], 16)
                    if s == 1:
                        operators(1)

            @block.tensor
            def _(pe):
                def merged(s):
                    pe.wait_ge(ya_ready, s + 1)
                    if s >= 2:
                        pe.wait_ge(ya_hi_made, s - 1)
                        pe.wait_ge(ya_lo_made, s - 1)
                    for c in range(4):
                        ins = pe.transpose(ps_a[:, s % 2, P * c:P * c + P], y_att[:, s % 2, P * c:P * c + P], ident[:, :])
                    ins.then_inc(ya_turned, 1)
                for it in range(TURNS):
                    if it % (TURNS // 2) == 0:
                        pe.wait_ge(ld_c[2 * it // TURNS], 16 * 2)
                        pe.wait_ge(ld_k[2 * it // TURNS], 16 * T)
                    if it >= 2:
                        pe.wait_ge(y_evac, it - 1)
                    for j in range(4):
                        g = 4 * it + j
                        pair, rows = g // 2, slice(64 * (g % 2), 64 * (g % 2) + 64)
                        out = ps_y[:, it % 2, j % 2, P * (j // 2):P * (j // 2) + P]
                        pe.matmul(out, ut[:, P * g:P * g + P], k_op[:, g, :], start=True, stop=False)
                        for part in range(2):
                            ins = pe.matmul(out, st[rows, part, pair, 0:NCH],
                                            c_pow[rows, part, pair, 1:T + 1, :].rearrange("p t c -> p (t c)"),
                                            start=False, stop=(part == 1))
                    ins.then_inc(y_done, 1)
                    if it >= 1:
                        merged(it - 1)
                merged(NT - 1)

            @block.scalar
            def _(act):
                for s in range(NT + 2):
                    if s < NT:
                        act.wait_ge(shift_ready, s + 1)
                        if s >= 2:
                            act.wait_ge(wts_ready, s - 1)
                        act.activation(wts[:, s % 2, 1, :, :], wts[:, s % 2, 0, :, :], ACT.Exp, scale=-1.0).then_inc(exp_ready, 1)
                    if 1 <= s <= TURNS:
                        n = s - 1
                        act.wait_ge(y_done, n + 1)
                        for g2 in range(2):
                            out = y_tok[:, :, 64 * n:64 * n + 64].rearrange("p t (a g c) -> p g a t c", a=2, g=2)[:, g2]
                            ins = act.activation(out, ps_y[:, n % 2, g2, 0:2 * P].rearrange("p (a t c) -> p a t c", a=2, t=T),
                                                 ACT.Gelu_apprx_tanh)
                        ins.then_inc(y_evac, 1)
                    if s >= 2:
                        n = s - 2
                        act.wait_ge(ya_turned, n + 1)
                        act.activation(ya_hi[:, :, n:L:NT], ps_a[:, n % 2, :].rearrange("p (c t) -> p c t", c=4), ACT.Copy).then_inc(ya_hi_made, 1)

            @block.vector
            def _(dve):
                ch = Chain(dve, dve_sem)

                def weigh(s):
                    b = s % 2
                    tile = att[:, s % NB, :, :].rearrange("p g (h c) -> p g h c", c=ROW)
                    dve.wait_ge(ld_att[s % NB], 16 * (s // NB + 1))
                    neg = tile[:, :, :, DH + 1]
                    ch.do(dve.tensor_tensor(low[:, b, :], neg[:, 0], neg[:, 1], ALU.min))
                    ch.do(dve.tensor_tensor(low[:, b, :], low[:, b, :], neg[:, 2], ALU.min))
                    dve.tensor_tensor(wts[:, b, 0, :, :], neg, low[:, b, :].unsqueeze(1).broadcast_to((P, NG, NH)),
                                      ALU.subtract).then_inc(shift_ready, 1)
                    dve.wait_ge(exp_ready, s + 1)
                    ch.do(dve.tensor_tensor(wts[:, b, 2, :, :], wts[:, b, 1, :, :], tile[:, :, :, DH], ALU.mult))
                    ch.do(dve.tensor_tensor(den[:, b, 0, :], wts[:, b, 2, 0, :], wts[:, b, 2, 1, :], ALU.add))
                    ch.do(dve.tensor_tensor(den[:, b, 0, :], den[:, b, 0, :], wts[:, b, 2, 2, :], ALU.add))
                    ch.do(dve.reciprocal(den[:, b, 1, :], den[:, b, 0, :]))
                    if s >= 2:
                        dve.wait_ge(parts_ready, s - 1)
                    dve.tensor_tensor(wts[:, b, 3, :, :], wts[:, b, 1, :, :],
                                      den[:, b, 1, :].unsqueeze(1).broadcast_to((P, NG, NH)), ALU.mult).then_inc(wts_ready, 1)

                def add(s):
                    b = s % 2
                    dve.wait_ge(parts_ready, s + 1)
                    v = att[:, s % NB, :, :].rearrange("p g (h c) -> p g h c", c=ROW)[:, :, :, 0:DH]
                    out = y_att[:, b, :].rearrange("p (h c) -> p h c", c=DH)
                    if s >= 2:
                        dve.wait_ge(ya_turned, s - 1)
                    ch.do(dve.tensor_tensor(out, v[:, 0], v[:, 1], ALU.add))
                    dve.tensor_tensor(out, out, v[:, 2], ALU.add).then_inc(ya_ready, 1)

                def split(s):
                    dve.wait_ge(ya_hi_made, s + 1)
                    dve.tensor_tensor(ya_lo[:, :, s:L:NT], ps_a[:, s % 2, :].rearrange("p (c t) -> p c t", c=4),
                                      ya_hi[:, :, s:L:NT].bitcast(F32), ALU.subtract).then_inc(ya_lo_made, 1)

                for s in range(NT + 2):
                    if s < NT:
                        weigh(s)
                    if 1 <= s <= NT:
                        add(s - 1)
                    if s >= 2:
                        split(s - 2)

            @block.gpsimd
            def _(pool):
                for s in range(NT):
                    b = s % 2
                    pool.wait_ge(wts_ready, s + 1)
                    tile = att[:, s % NB, :, :].rearrange("p g (h c) -> p g h c", c=ROW)
                    for g in range(NG):
                        ins = pool.tensor_tensor(tile[:, g, :, 0:DH], tile[:, g, :, 0:DH],
                                                 wts[:, b, 3, g, :].unsqueeze(2).broadcast_to((P, NH, DH)), ALU.mult)
                    ins.then_inc(parts_ready, 1)


def gated_ssm(nc, m, cst, io, y_tok, y_T, y_hi, y_lo):
    with ExitStack() as stack:
        a = Memory(nc, stack)
        sig = y_tok.rearrange("p s c -> p (s c)").rearrange("p (k t) -> p k t", k=4)
        w_raw = a.sb("glu_raw", [P, 4, SSM_W])
        w_hi, w_lo = a.sb("glu_hi", [P, 4, SSM_W], F32R), a.sb("glu_lo", [P, 4, SSM_W], F32R)
        ps = a.ps("ps_glu", [P, 4, 512])
        ps_z = a.ps("ps_z", [P, 2, 512])
        ld, w_hi_made, w_lo_made = a.sem("ld_glu"), a.sem("glu_hi_made"), a.sem("glu_lo_made")
        turned, y_hi_made, y_lo_made = a.sem("glu_turned"), a.sem("glu_y_hi"), a.sem("glu_y_lo")
        z_done, sig_made, y2_made, y2_split = a.sem("glu_z"), a.sem("glu_sig_made"), a.sem("glu_y2_made"), a.sem("glu_y2_split")
        y2_hi_made = a.sem("glu_y2_hi")
        ident = cst["ident"]
        tile = lambda t, s: t[:, :, s:L:NT]
        bank = lambda s: ps[:, s % 4, :].rearrange("p (c t) -> p c t", c=4)
        part = lambda t, n: t[:, n % 4, 512 * (n // 4):512 * (n // 4) + 512]
        with nc.Block() as block:
            @block.sync
            def _(sp):
                sp.dma_start(w_raw[:, :, :], io["w_glu"][0].rearrange("(c p) n -> p c n", p=P)).then_inc(ld, 16)

            @block.tensor
            def _(pe):
                for s in range(NT):
                    if s >= 4:
                        pe.wait_ge(y_lo_made, s - 3)
                    for c in range(4):
                        ins = pe.transpose(ps[:, s % 4, P * c:P * c + P], y_tok[:, s, P * c:P * c + P], ident[:, :])
                    ins.then_inc(turned, 1)
                pe.wait_ge(w_lo_made, 1)
                pe.wait_ge(y_lo_made, NT)
                for n in range(8):
                    if n >= 2:
                        pe.wait_ge(sig_made, n - 1)
                    c, half = n % 4, slice(512 * (n // 4), 512 * (n // 4) + 512)
                    for k in range(4):
                        ins = mm3(pe, ps_z[:, n % 2, :], w_hi[:, k, P * c:P * c + P], w_lo[:, k, P * c:P * c + P],
                                  y_hi[:, k, half], y_lo[:, k, half], k == 0, k == 3)
                    ins.then_inc(z_done, 1)

            @block.scalar
            def _(act):
                def tiles(first):
                    for s in range(first, first + 4):
                        act.wait_ge(turned, s + 1)
                        act.activation(tile(y_hi, s), bank(s), ACT.Copy).then_inc(y_hi_made, 1)

                tiles(0)
                act.wait_ge(ld, 16)
                act.activation(w_hi[:, :, :], w_raw[:, :, :], ACT.Copy).then_inc(w_hi_made, 1)
                tiles(4)
                for n in range(12):
                    if n < 8:
                        act.wait_ge(z_done, n + 1)
                        act.activation(part(sig, n), ps_z[:, n % 2, :], ACT.Sigmoid).then_inc(sig_made, 1)
                    if n >= 4:
                        if n == 8:
                            act.wait_ge(z_done, 8)
                        act.wait_ge(y2_made, n - 3)
                        act.activation(part(y_hi, n - 4), part(y_T, n - 4), ACT.Copy).then_inc(y2_hi_made, 1)

            @block.vector
            def _(dve):
                for s in range(NT):
                    dve.wait_ge(y_hi_made, s + 1)
                    dve.tensor_copy(tile(y_T, s), bank(s))
                    dve.tensor_tensor(tile(y_lo, s), bank(s), tile(y_hi, s).bitcast(F32), ALU.subtract).then_inc(y_lo_made, 1)
                    if s == 3:
                        dve.wait_ge(w_hi_made, 1)
                        dve.tensor_tensor(w_lo[:, :, :], w_raw[:, :, :], w_hi[:, :, :].bitcast(F32), ALU.subtract).then_inc(w_lo_made, 1)
                dve.wait_ge(y_lo_made, NT)
                for n in range(12):
                    if n < 8:
                        dve.wait_ge(sig_made, n + 1)
                        dve.tensor_tensor(part(y_T, n), part(y_T, n), part(sig, n), ALU.mult).then_inc(y2_made, 1)
                    if n >= 4:
                        dve.wait_ge(y2_hi_made, n - 3)
                        dve.tensor_tensor(part(y_lo, n - 4), part(y_T, n - 4), part(y_hi, n - 4).bitcast(F32), ALU.subtract).then_inc(y2_split, 1)


def merge(nc, m, cst, io, xT_hi, xT_lo, y2, ya, keep, merged):
    with ExitStack() as stack:
        a = Memory(nc, stack)
        NAMES = ("gs", "ga", "bs", "ba")
        KS = (KD, KD, 4, 4)
        free = keep["states"][:, :, :, :].rearrange("p r a k -> p (r a k)")
        sig = free[:, 0:2 * L].rearrange("p (w t) -> p w t", w=2)
        raw = [free[:, (2 + w) * L:(3 + w) * L].rearrange("p (k n) -> p k n", k=KD) for w in range(2)]
        raw += [a.sb(f"m_{n}_raw", [P, k, P]) for n, k in zip(NAMES[2:], KS[2:])]
        hi = [a.sb(f"m_{n}_hi", [P, k, P], F32R) for n, k in zip(NAMES, KS)]
        lo = [a.sb(f"m_{n}_lo", [P, k, P], F32R) for n, k in zip(NAMES, KS)]
        bias = a.sb("m_bias", [P, 2])
        added = a.sem("m_added")
        ps = a.ps("ps_merge", [P, 4, 2, 512])
        ld = [a.sem(f"ld_m_{n}") for n in NAMES]
        hi_made = [a.sem(f"m_{n}_hi_made") for n in NAMES]
        lo_made = [a.sem(f"m_{n}_lo_made") for n in NAMES]
        done = [a.sem(f"m_{n}_done") for n in NAMES]
        bias_ready, sig_made, prod_made, out_made = a.sem("m_bias_ready"), [a.sem("m_sig0"), a.sem("m_sig1")], a.sem("m_prod_made"), a.sem("m_out")
        w_in = io["w_in"][0].rearrange("(q k) n -> q k n", k=KD)
        src = (lambda j: w_in[:, :, bass.ds(C_GS + P * j, P)], lambda j: w_in[:, :, bass.ds(C_GA + P * j, P)],
               lambda j: io["w_br_ssm"][0].rearrange("(c p) n -> p c n", p=P)[:, :, bass.ds(P * j, P)],
               lambda j: io["w_br_attn"][0].rearrange("(c p) n -> p c n", p=P)[:, :, bass.ds(P * j, P)])
        rhs = ((xT_hi, xT_lo), (xT_hi, xT_lo), y2, ya)
        half = lambda h: slice(512 * h, 512 * h + 512)

        def split_hi(act, w, n):
            act.wait_ge(ld[w], 16 * n)
            act.activation(hi[w][:, :, :], raw[w][:, :, :], ACT.Copy).then_inc(hi_made[w], 1)

        def split_lo(dve, w, n):
            dve.wait_ge(hi_made[w], n)
            dve.tensor_tensor(lo[w][:, :, :], raw[w][:, :, :], hi[w][:, :, :].bitcast(F32), ALU.subtract).then_inc(lo_made[w], 1)

        def load(sp, w, j):
            sp.dma_start(raw[w][:, :, :], src[w](j)).then_inc(ld[w], 16)

        def turns(eng, turn):
            with eng.Fori(0, KD - 1) as j:
                turn(eng, j, True)
            turn(eng, KD - 1, False)

        def pe_turn(pe, j, more):
            for w in range(4):
                pe.wait_ge(lo_made[w], j + 1)
                pe.wait_ge(sig_made[w] if w < 2 else (prod_made, out_made)[w - 2], 2 * j)
                for h in range(2):
                    for k in range(KS[w]):
                        ins = mm3(pe, ps[:, w, h, :], hi[w][:, k, :], lo[w][:, k, :],
                                  rhs[w][0][:, k, half(h)], rhs[w][1][:, k, half(h)], k == 0, k == KS[w] - 1)
                    ins.then_inc(done[w], 1)

        def act_turn(act, j, more):
            act.wait_ge(bias_ready, j + 1)
            for w in range(4):
                if w < 2:
                    for h in range(2):
                        act.wait_ge(done[w], 2 * j + h + 1)
                        act.wait_ge(prod_made if w == 0 else added, 2 * j if w == 0 else j)
                        act.activation(sig[:, w, half(h)], ps[:, w, h, :], ACT.Sigmoid, bias=bias[:, w:w + 1]).then_inc(sig_made[w], 1)
                if more:
                    act.wait_ge(done[w], 2 * j + 2)
                    split_hi(act, w, j + 2)

        def dve_turn(dve, j, more):
            for w in range(2):
                if more:
                    split_lo(dve, w, j + 2)
            whole = merged[:, bass.ds(j, 1), :].rearrange("p o t -> p (o t)")
            out = lambda h: merged[:, bass.ds(j, 1), half(h)].rearrange("p o t -> p (o t)")
            for h in range(2):
                dve.wait_ge(done[2], 2 * j + h + 1)
                dve.wait_ge(sig_made[0], 2 * j + h + 1)
                dve.tensor_tensor(out(h), ps[:, 2, h, :], sig[:, 0, half(h)], ALU.mult).then_inc(prod_made, 1)
            if more:
                split_lo(dve, 2, j + 2)
            for h in range(2):
                dve.wait_ge(done[3], 2 * j + h + 1)
                dve.wait_ge(sig_made[1], 2 * j + h + 1)
                dve.tensor_tensor(sig[:, 1, half(h)], ps[:, 3, h, :], sig[:, 1, half(h)], ALU.mult).then_inc(out_made, 1)
            dve.wait_ge(out_made, 2 * j + 2)
            dve.wait_ge(prod_made, 2 * j + 2)
            dve.tensor_tensor(whole, whole, sig[:, 1, :], ALU.add).then_inc(added, 1)
            if more:
                split_lo(dve, 3, j + 2)

        with nc.Block() as block:
            @block.sync
            def _(sp):
                for w in range(4):
                    load(sp, w, 0)
                for w in range(4):
                    sp.wait_ge(lo_made[w], 1)
                    load(sp, w, 1)
                for j in range(KD - 2):
                    for w in range(4):
                        sp.wait_ge(lo_made[w], j + 2)
                        load(sp, w, j + 2)

            @block.tensor
            def _(pe):
                turns(pe, pe_turn)

            @block.scalar
            def _(act):
                for w in range(4):
                    split_hi(act, w, 1)
                turns(act, act_turn)

            @block.vector
            def _(dve):
                for w in range(4):
                    split_lo(dve, w, 1)
                turns(dve, dve_turn)

            @block.gpsimd
            def _(pool):
                with pool.Fori(0, KD) as j:
                    pool.wait_ge(sig_made[0], 2 * j)
                    pool.wait_ge(sig_made[1], 2 * j)
                    pool.tensor_copy(bias[:, 0:1], keep["bias_T"][:, bass.ds(C_GS // P + j, 1)])
                    pool.tensor_copy(bias[:, 1:2], keep["bias_T"][:, bass.ds(C_GA // P + j, 1)]).then_inc(bias_ready, 1)


class LayerNorm:

    def __init__(self, a, name, rows):
        self.rows = rows
        self.stats, self.agg = a.sb(name + "_stats", [P, NT, 2, 6]), a.sb(name + "_agg", [P, NT, 8])
        self.gain, self.shift = a.sb(name + "_gain", [P, D]), a.sb(name + "_shift", [P, D])
        self.loaded, self.var, self.root, self.scale, self.normal, self.scaled, self.ready = (
            a.sem(f"{name}_{n}") for n in ("loaded", "var", "root", "scale", "normal", "scaled", "ready"))

    def load(self, sp, gain, shift):
        for src, t in ((gain, self.gain), (shift, self.shift)):
            sp.dma_start(t[:, :], src.broadcast_to((P, D))).then_inc(self.loaded, 16)

    def statistics(self, dve, ch, s):
        for h in range(2):
            ch(dve.bn_stats(self.stats[:, s, h, :], self.rows(s)[:, 512 * h:512 * h + 512]))
        ch.sync()
        ch.do(dve.bn_aggr(self.agg[:, s, 0:2], self.stats[:, s, :, :]))
        dve.tensor_scalar(self.agg[:, s, 2:3], self.agg[:, s, 1:2], LN_EPS, 0.0, ALU.add, ALU.add).then_inc(self.var, 1)

    def root_of(self, act, s):
        act.wait_ge(self.var, s + 1)
        act.activation(self.agg[:, s, 3:4], self.agg[:, s, 2:3], ACT.Sqrt).then_inc(self.root, 1)

    def scales(self, dve, ch, s):
        dve.wait_ge(self.root, s + 1)
        ch.do(dve.reciprocal(self.agg[:, s, 4:5], self.agg[:, s, 3:4]))
        dve.scalar_tensor_tensor(out=self.agg[:, s, 5:6], in0=self.agg[:, s, 0:1], scalar=-1.0, in1=self.agg[:, s, 4:5],
                                 op0=ALU.mult, op1=ALU.mult).then_inc(self.scale, 1)

    def normalise(self, act, s):
        act.wait_ge(self.scale, s + 1)
        act.activation(self.rows(s), self.rows(s), ACT.Identity, bias=self.agg[:, s, 5:6], scale=self.agg[:, s, 4:5]).then_inc(self.normal, 1)

    def times_gain(self, dve, s):
        dve.wait_ge(self.normal, s + 1)
        dve.tensor_tensor(self.rows(s), self.rows(s), self.gain[:, :], ALU.mult).then_inc(self.scaled, 1)

    def plus_shift(self, pool, s):
        pool.wait_ge(self.scaled, s + 1)
        pool.tensor_tensor(self.rows(s), self.rows(s), self.shift[:, :], ALU.add).then_inc(self.ready, 1)


def output_projection(nc, m, cst, io, merged, scr):
    with ExitStack() as stack:
        a = Memory(nc, stack)
        m_hi, m_lo = a.sb("m_hi", [P, KD, L], F32R), a.sb("m_lo", [P, KD, L], F32R)
        w_raw = a.sb("wo_raw", [P, 2, D])
        w_hi, w_lo = a.sb("wo_hi", [P, KD, D], F32R), a.sb("wo_lo", [P, KD, D], F32R)
        x_in = merged
        norm = LayerNorm(a, "ln1", lambda s: x_in[:, s, :])
        ps = a.ps("ps_wo", [P, 4, 2, 512])
        ld_w, ld_x = [a.sem("ld_wo0"), a.sem("ld_wo1")], a.sem("ld_wox")
        mh, ml, wh, wl = a.sem("m_hi_made"), a.sem("m_lo_made"), a.sem("wo_hi_made"), a.sem("wo_lo_made")
        done, read, stored, dve_sem = (a.sem("wo_" + n) for n in ("done", "read", "stored", "dve_ch"))
        x_d = io["x"][0].rearrange("(p s) d -> p s d", s=NT)
        x1_d = scr["x1"][0:L, 0:D].rearrange("(p s) d -> p s d", s=NT)
        w_d = io["w_out"][0].rearrange("(j p) n -> p j n", p=P)
        with nc.Block() as block:
            @block.sync
            def _(sp):
                for j in range(KD):
                    if j >= 2:
                        sp.wait_ge(wl, j - 1)
                    sp.dma_start(w_raw[:, j % 2, :], w_d[:, j, :]).then_inc(ld_w[j % 2], 16)
                norm.load(sp, io["ln1_g"], io["ln1_b"])
                sp.wait_ge(ml, KD)
                sp.dma_start(x_in[:, :, :], x_d).then_inc(ld_x, 16)
                for s in range(NT):
                    sp.wait_ge(norm.ready, s + 1)
                    sp.dma_start(x1_d[:, s, :], x_in[:, s, :]).then_inc(stored, 16)
                sp.wait_ge(stored, 16 * NT)

            @block.tensor
            def _(pe):
                def product(s, j):
                    for h in range(2):
                        ins = mm3(pe, ps[:, s % 4, h, :], m_hi[:, j, s:L:NT], m_lo[:, j, s:L:NT],
                                  w_hi[:, j, 512 * h:512 * h + 512], w_lo[:, j, 512 * h:512 * h + 512], j == 0, j == KD - 1)
                    if j == KD - 1:
                        ins.then_inc(done, 1)

                for j in range(KD):
                    pe.wait_ge(ml, j + 1)
                    pe.wait_ge(wl, j + 1)
                    for s in range(4):
                        product(s, j)
                for s in range(4, NT):
                    pe.wait_ge(read, s - 3)
                    for j in range(KD):
                        product(s, j)

            @block.scalar
            def _(act):
                for j in range(KD):
                    act.activation(m_hi[:, j, :], merged[:, j, :], ACT.Copy).then_inc(mh, 1)
                    act.wait_ge(ld_w[j % 2], 16 * (j // 2 + 1))
                    act.activation(w_hi[:, j, :], w_raw[:, j % 2, :], ACT.Copy).then_inc(wh, 1)
                for s in range(NT + 1):
                    if s < NT:
                        norm.root_of(act, s)
                    if s >= 1:
                        norm.normalise(act, s - 1)

            @block.vector
            def _(dve):
                ch = Chain(dve, dve_sem)
                for j in range(KD):
                    dve.wait_ge(mh, j + 1)
                    dve.tensor_tensor(m_lo[:, j, :], merged[:, j, :], m_hi[:, j, :].bitcast(F32), ALU.subtract).then_inc(ml, 1)
                    dve.wait_ge(wh, j + 1)
                    dve.tensor_tensor(w_lo[:, j, :], w_raw[:, j % 2, :], w_hi[:, j, :].bitcast(F32), ALU.subtract).then_inc(wl, 1)
                dve.wait_ge(ld_x, 16)
                dve.wait_ge(norm.loaded, 32)

                def residual(s):
                    dve.wait_ge(done, s + 1)
                    dve.scalar_tensor_tensor(out=x_in[:, s, :], in0=x_in[:, s, :], scalar=ALPHA,
                                             in1=ps[:, s % 4, :, :].rearrange("p h n -> p (h n)"), op0=ALU.mult, op1=ALU.add).then_inc(read, 1)

                for s in range(4):
                    residual(s)
                for s in range(NT + 2):
                    if s < NT:
                        if s >= 4:
                            residual(s)
                        dve.wait_ge(read, s + 1)
                        norm.statistics(dve, ch, s)
                    if 1 <= s <= NT:
                        norm.scales(dve, ch, s - 1)
                    if s >= 2:
                        norm.times_gain(dve, s - 2)

            @block.gpsimd
            def _(pool):
                pool.wait_ge(norm.loaded, 32)
                for s in range(NT):
                    norm.plus_shift(pool, s)


def route_and_share(nc, m, cst, io, scr, tab):
    with ExitStack() as stack:
        a = Memory(nc, stack)
        xT_hi, xT_lo = a.sb("x1T_hi", [P, KD, L], F32R), a.sb("x1T_lo", [P, KD, L], F32R)
        NB = 4
        x_in = a.sb("x1_in", [P, NB, D])
        NAMES = ("gate", "up")
        raw = [a.sb(f"sh_{n}_raw", [P, KD, EH]) for n in NAMES]
        hi = [a.sb(f"sh_{n}_hi", [P, KD, EH], F32R) for n in NAMES]
        lo = [a.sb(f"sh_{n}_lo", [P, KD, EH], F32R) for n in NAMES]
        d_hi, d_lo = a.sb("sh_down_hi", [P, 2, D], F32R), a.sb("sh_down_lo", [P, 2, D], F32R)
        r_raw, r_hi, r_lo = a.sb("router_raw", [P, KD, NE]), a.sb("router_hi", [P, KD, NE], F32R), a.sb("router_lo", [P, KD, NE], F32R)
        h = a.sb("sh_h", [P, L // 2])
        h_hi, h_lo = a.sb("sh_h_hi", [P, 2, L], F32R), a.sb("sh_h_lo", [P, 2, L], F32R)
        silu = a.sb("sh_silu", [P, L // 2])
        acc = x_in[:, 2:4, :]
        W = (P, NT, NE)
        score, sel, key, gates = (a.sb("rt_" + n, [P, NT, NE]) for n in ("score", "sel", "key", "gates"))
        t64 = a.sb("rt_t64", [P, 2, NT, NE])
        bias = a.sb("rt_bias", [P, NE])
        top2 = a.sb("rt_top2", [P, NT, 8, 8])
        grp = a.sb("rt_grp", [P, 4, NT, 8])
        top8 = a.sb("rt_top8", [P, NT, 8])
        low8 = a.sb("rt_low8", [P, 8, 8])
        tot = a.sb("rt_tot", [P, 2, NT])
        mask = a.sb("rt_mask", [P, NT, NE], BF16)
        tri = a.sb("rt_tri", [P, P], BF16)
        ones = a.sb("rt_ones", [P, P], BF16)
        onesf = a.sb("rt_onesf", [NE, P])
        trif = a.sb("rt_trif", [NE, NE])
        slot_n = a.sb("rt_slot", [P, P])
        ecol = a.sb("rt_ecol", [NE, P])
        cnt = a.sb("rt_cnt", [NE, 4])
        NX = (L - 1) // CAP
        over = a.sb("rt_over", [NE, NX])
        place = a.sb("rt_place", [NE, NX])
        onehot = a.sb("rt_onehot", [NE, NX + 1, P])
        base_w = a.sb("rt_base_w", [NE, NX, P])
        small = a.sb("rt_small", [P, 4])
        zero = a.sb("rt_zero", [P, D + NE])

        ps_t = a.ps("ps_rt", [P, 2, 512])
        ps_r = a.ps("ps_router", [P, NT, NE])
        ps_pos = a.ps("ps_pos", [P, 512])
        ps_s = a.ps("ps_share", [P, 4, 512])
        (ld_x0, ld_x1, ld_w, ld_dn, ld_r, ld_b, turned, x_hi_made, x_lo_made, w_hi_made, w_lo_made, zeros_ready, zeros_out,
         r_done, score_ready, mask_ready, pos_done, cnt_done, over_ready, tab_done, gates_ready, gu_done, silu_made, h_made,
         h_hi_made, h_lo_made, dn_done, acc_ready, gates_out, dve_sem, pool_sem, pat_ready, place_done, place_ready) = (
            a.sem("rs_" + n) for n in
            ("ld_x0", "ld_x1", "ld_w", "ld_dn", "ld_r", "ld_b", "turned", "x_hi", "x_lo", "w_hi", "w_lo", "zeros", "zeros_out",
             "r_done", "score", "mask", "pos_done", "cnt_done", "over", "tab_done", "gates", "gu_done", "silu", "h",
             "h_hi", "h_lo", "dn_done", "acc", "gates_out", "dve_ch", "pool_ch", "patterns", "place_done", "place_ready"))
        ld_x = (ld_x0, ld_x1, a.sem("rs_ld_x2"), a.sem("rs_ld_x3"))
        acc_out = (a.sem("rs_acc_out0"), a.sem("rs_acc_out1"))
        logits_T = acc[0:NE, 0, :]
        logits_done, logits_copied = a.sem("rs_logits_done"), a.sem("rs_logits_copied")
        x1_d = scr["x1"][0:L, 0:D].rearrange("(p s) d -> p s d", s=NT)
        acc_d = scr["acc"][0:L, :].rearrange("(p s) d -> p s d", s=NT)
        ident = cst["ident"]
        d_raw = raw[0][:, :, :].rearrange("p k n -> p (k n)").rearrange("p (c n) -> p c n", c=2)

        with nc.Block() as block:
            @block.sync
            def _(sp):
                for s in range(NT):
                    if s >= NB:
                        sp.wait_ge(turned, 2 * (s - NB + 1))
                    sp.dma_start(x_in[:, s % NB, :], x1_d[:, s, :]).then_inc(ld_x[s % NB], 16)
                    if s == 1:
                        sp.dma_start(r_raw[:, :, :], io["router_w"][0].rearrange("(q k) n -> q k n", k=KD)).then_inc(ld_r, 16)
                        sp.dma_start(bias[:, :], io["router_bias"].broadcast_to((P, NE))).then_inc(ld_b, 16)
                        for n, t in zip(NAMES, raw):
                            sp.dma_start(t[:, :, :], io[f"sh_w_{n}"][0].rearrange("(q k) n -> q k n", k=KD)).then_inc(ld_w, 16)
                sp.wait_ge(zeros_ready, 1)
                for lo_row, n in ((L, P), (L + P, REST)):
                    sp.dma_start(scr["x1"][lo_row:lo_row + n, :], zero[0:n, :]).then_inc(zeros_out, 16)
                    sp.dma_start(scr["acc"][lo_row:lo_row + n, :], zero[0:n, 0:D]).then_inc(zeros_out, 16)
                sp.wait_ge(w_lo_made, 2)
                sp.dma_start(d_raw, io["sh_w_down"][0].rearrange("(c p) n -> p c n", p=P)).then_inc(ld_dn, 16)
                for s in range(NT):
                    if s < 2:
                        sp.wait_ge(turned, 2 * NT)
                    else:
                        sp.wait_ge(acc_ready, s - 1)
                    sp.dma_start(x_in[:, s % 2, :], x1_d[:, s, :]).then_inc(ld_x[s % 2], 16)
                    if s == 0:
                        sp.wait_ge(gates_ready, 1)
                        sp.dma_start(scr["x1"][0:L, D:D + NE].rearrange("(p s) e -> p s e", s=NT), gates[:, :, :]).then_inc(gates_out, 16)
                    if s >= 1:
                        sp.wait_ge(acc_ready, s)
                        sp.dma_start(acc_d[:, s - 1, :], acc[:, (s - 1) % 2, :]).then_inc(acc_out[(s - 1) % 2], 16)
                sp.wait_ge(acc_ready, NT)
                sp.dma_start(acc_d[:, NT - 1, :], acc[:, 1, :]).then_inc(acc_out[1], 16)
                for j in range(2):
                    sp.wait_ge(acc_out[j], 16 * NT // 2)
                sp.wait_ge(zeros_out, 64)
                sp.wait_ge(gates_out, 16)

            @block.gpsimd
            def _(pool):
                ch = Chain(pool, pool_sem)
                ch(pool.memset(zero[:, :], 0.0))
                ch.sync()
                pool.sem_inc(zeros_ready, 1)
                ch(pool.memset(low8[:, :, :], 1.0))
                ch(pool.memset(tri[:, :], 1.0))
                ch(pool.memset(ones[:, :], 1.0))
                ch(pool.memset(onesf[:, :], 1.0))
                ch(pool.memset(trif[:, :], 1.0))
                ch(pool.iota(slot_n[:, :], pattern=[[1, P]], base=0, channel_multiplier=0, allow_small_or_imprecise_dtypes=True))
                ch(pool.iota(ecol[:, :], pattern=[[0, P]], base=0, channel_multiplier=1, allow_small_or_imprecise_dtypes=True))
                ch.sync()
                for j in range(NX):
                    ch.do(pool.memset(base_w[:, j, :], float(CAP * (j + 1))))
                ch.do(pool.affine_select(out=low8[:, :, :], in_=low8[:, :, :], compare_op=ALU.is_gt, fill=0.0, base=0,
                                         pattern=[[1, 8], [-1, 8]], channel_multiplier=0))
                ch.do(pool.affine_select(out=tri[:, :], in_=tri[:, :], compare_op=ALU.is_gt, fill=0.0, base=0,
                                         pattern=[[1, P]], channel_multiplier=-1))
                ch.do(pool.affine_select(out=trif[:, :], in_=trif[:, :], compare_op=ALU.is_gt, fill=0.0, base=0,
                                         pattern=[[1, NE]], channel_multiplier=-1))
                pool.sem_inc(pat_ready, 1)

            @block.tensor
            def _(pe):
                for s in range(NT):
                    pe.wait_ge(ld_x[s % NB], 16 * (s // NB + 1))
                    for half in range(2):
                        n = 2 * s + half
                        if n >= 2:
                            pe.wait_ge(x_lo_made, n - 1)
                        for j in range(4):
                            ins = pe.transpose(ps_t[:, n % 2, P * j:P * j + P], x_in[:, s % NB, 4 * half + j:D:KD], ident[:, :])
                        ins.then_inc(turned, 1)
                pe.wait_ge(x_lo_made, 2 * NT)
                pe.wait_ge(w_lo_made, 1)
                for half in range(2):
                    cols = slice(512 * half, 512 * half + 512)
                    for k in range(KD):
                        ins = mm3(pe, ps_s[0:NE, 2 + half, :], r_hi[:, k, :], r_lo[:, k, :], xT_hi[:, k, cols], xT_lo[:, k, cols],
                                  k == 0, k == KD - 1)
                    ins.then_inc(logits_done, 1)
                pe.wait_ge(logits_copied, 2)
                for s in range(NT):
                    ins = pe.transpose(ps_r[:, s, :], logits_T[:, s:L:NT], ident[0:NE, 0:NE])
                ins.then_inc(r_done, 1)
                for n in range(4):
                    c, half = n // 2, slice(512 * (n % 2), 512 * (n % 2) + 512)
                    if n >= 2:
                        pe.wait_ge(h_made, n - 1)
                    for w in range(2):
                        pe.wait_ge(w_lo_made, w + 2)
                        for k in range(KD):
                            ins = mm3(pe, ps_s[:, 2 * (n % 2) + w, :], hi[w][:, k, P * c:P * c + P], lo[w][:, k, P * c:P * c + P],
                                      xT_hi[:, k, half], xT_lo[:, k, half], k == 0, k == KD - 1)
                    ins.then_inc(gu_done, 1)
                pe.wait_ge(mask_ready, 1)
                pe.wait_ge(pat_ready, 1)
                for s in range(NT):
                    ins = pe.matmul(ps_pos[:, NE * s:NE * s + NE], tri[:, :], mask[:, s, :], start=(s == 0), stop=(s == NT - 1),
                                    skip_group_check=True)
                    if s + 1 < NT:
                        later = mask[:, s, :].unsqueeze(1).broadcast_to((P, NT - 1 - s, NE))
                        ins = pe.matmul(ps_pos[:, NE * (s + 1):NE * NT], ones[:, :], later, start=False, stop=False, skip_group_check=True)
                ins.then_inc(pos_done, 1)
                pe.wait_ge(x_lo_made, 2 * NT)
                for s in range(NT):
                    ins = pe.matmul(ps_t[0:NE, 0, 0:1], mask[:, s, :], ones[:, 0:1], start=(s == 0), stop=(s == NT - 1))
                ins.then_inc(cnt_done, 1)

                def down(s):
                    if s >= 2:
                        pe.wait_ge(acc_ready, s - 1)
                    for half in range(2):
                        for c in range(2):
                            ins = mm3(pe, ps_s[:, 2 * (s % 2) + half, :], h_hi[:, c, s:L:NT], h_lo[:, c, s:L:NT],
                                      d_hi[:, c, 512 * half:512 * half + 512], d_lo[:, c, 512 * half:512 * half + 512], c == 0, c == 1)
                    ins.then_inc(dn_done, 1)

                pe.wait_ge(h_lo_made, 4)
                pe.wait_ge(w_lo_made, 4)
                for s in range(2):
                    down(s)
                pe.wait_ge(over_ready, 1)
                pe.matmul(ps_t[0:NE, 0, 4:5], trif[:, :], cnt[:, 1:2], start=True, stop=True)
                pe.matmul(ps_t[:, 0, 8:9], onesf[:, :], cnt[:, 1:2], start=True, stop=True).then_inc(place_done, 1)
                pe.wait_ge(place_ready, 1)
                for n, w in ((0, None), (1, base_w)):
                    cols = slice(P * n, P * n + P)
                    js = range(NX + 1) if w is None else range(1, NX + 1)
                    for j in js:
                        ins = pe.matmul(ps_t[:, 1, cols], ecol[:, :] if w is None else base_w[:, j - 1, :], onehot[:, j, :],
                                        start=(j == js[0]), stop=(j == js[-1]))
                ins.then_inc(tab_done, 1)
                for s in range(2, NT):
                    down(s)

            @block.scalar
            def _(act):
                act.wait_ge(ld_r, 16)
                act.activation(r_hi[:, :, :], r_raw[:, :, :], ACT.Copy).then_inc(w_hi_made, 1)
                for n in range(2 * NT):
                    act.wait_ge(turned, n + 1)
                    s, half = n // 2, n % 2
                    act.activation(xT_hi[:, 4 * half:4 * half + 4, s:L:NT], ps_t[:, n % 2, :].rearrange("p (k t) -> p k t", k=4),
                                   ACT.Copy).then_inc(x_hi_made, 1)
                act.wait_ge(ld_w, 32)
                for w in range(2):
                    act.activation(hi[w][:, :, :], raw[w][:, :, :], ACT.Copy).then_inc(w_hi_made, 1)
                for half in range(2):
                    act.wait_ge(logits_done, half + 1)
                    act.activation(logits_T[:, 512 * half:512 * half + 512], ps_s[0:NE, 2 + half, :], ACT.Copy).then_inc(logits_copied, 1)
                act.wait_ge(r_done, 1)
                act.activation(score[:, :, :], ps_r[:, :, :], ACT.Sigmoid).then_inc(score_ready, 1)
                for n in range(4):
                    act.wait_ge(gu_done, n + 1)
                    if n:
                        act.wait_ge(h_made, n)
                    act.activation(silu[:, :], ps_s[:, 2 * (n % 2), :], ACT.Silu).then_inc(silu_made, 1)
                    act.wait_ge(h_made, n + 1)
                    act.activation(h_hi[:, n // 2, 512 * (n % 2):512 * (n % 2) + 512], h[:, :], ACT.Copy).then_inc(h_hi_made, 1)
                act.wait_ge(ld_dn, 16)
                act.activation(d_hi[:, :, :], d_raw, ACT.Copy).then_inc(w_hi_made, 1)

            @block.vector
            def _(dve):
                ch = Chain(dve, dve_sem)
                tt, ts = dve.tensor_tensor, dve.tensor_scalar

                def split_lo(o, r, hh, n):
                    dve.wait_ge(w_hi_made, n)
                    tt(o[:, :, :], r, hh[:, :, :].bitcast(F32), ALU.subtract).then_inc(w_lo_made, 1)

                split_lo(r_lo, r_raw[:, :, :], r_hi, 1)
                for n in range(2 * NT):
                    dve.wait_ge(x_hi_made, n + 1)
                    s, half = n // 2, n % 2
                    tt(xT_lo[:, 4 * half:4 * half + 4, s:L:NT], ps_t[:, n % 2, :].rearrange("p (k t) -> p k t", k=4),
                       xT_hi[:, 4 * half:4 * half + 4, s:L:NT].bitcast(F32), ALU.subtract).then_inc(x_lo_made, 1)
                for w in range(2):
                    split_lo(lo[w], raw[w][:, :, :], hi[w], w + 2)

                def share(n):
                    dve.wait_ge(silu_made, n + 1)
                    if n:
                        dve.wait_ge(h_hi_made, n)
                        dve.wait_ge(h_lo_made, n)
                    tt(h[:, :], silu[:, :], ps_s[:, 2 * (n % 2) + 1, :], ALU.mult).then_inc(h_made, 1)
                    dve.wait_ge(h_hi_made, n + 1)
                    cols = slice(512 * (n % 2), 512 * (n % 2) + 512)
                    tt(h_lo[:, n // 2, cols], h[:, :], h_hi[:, n // 2, cols].bitcast(F32), ALU.subtract).then_inc(h_lo_made, 1)

                dve.wait_ge(score_ready, 1)
                dve.wait_ge(ld_b, 16)
                dve.wait_ge(pat_ready, 1)
                ch.do(tt(sel[:, :, :], score[:, :, :], bias[:, :].unsqueeze(1).broadcast_to(W), ALU.add))
                for s in range(NT):
                    for g in range(8):
                        ch(dve.max(top2[:, s, g, :], sel[:, s, 8 * g:8 * g + 8]))
                ch.sync()
                gs, rank, gm, neg = (grp[:, j, :, :] for j in range(4))
                ch.do(tt(gs, top2[:, :, :, 0], top2[:, :, :, 1], ALU.add))
                G = (P, NT, 8, 8)
                mine, other = gs.unsqueeze(3).broadcast_to(G), gs.unsqueeze(2).broadcast_to(G)
                gt, eq = (t64[:, j, :, :].rearrange("p s (g h) -> p s g h", g=8) for j in range(2))
                ch(tt(gt, other, mine, ALU.is_gt))
                ch.do(tt(eq, other, mine, ALU.is_equal))
                ch.do(tt(eq, eq, low8[:, :, :].unsqueeze(1).broadcast_to(G), ALU.mult))
                ch.do(tt(gt, gt, eq, ALU.add))
                ch.do(dve.tensor_reduce(rank, gt, AX.X, ALU.add))
                ch.do(ts(gm, rank, 3.5, 0.0, ALU.is_lt, ALU.add))
                ch.do(ts(neg, gm, -1.0, -NEG, ALU.add, ALU.mult))
                view = lambda t: t[:, :, :].rearrange("p s (g e) -> p s g e", g=8)
                ch.do(tt(view(key), view(sel), gm.unsqueeze(3).broadcast_to(G), ALU.mult))
                ch.do(tt(view(key), view(key), neg.unsqueeze(3).broadcast_to(G), ALU.add))
                for s in range(NT):
                    ch(dve.max(top8[:, s, :], key[:, s, :]))
                ch.sync()
                for s in range(NT):
                    ch(dve.match_replace(sel[:, s, :], top8[:, s, :], key[:, s, :], 2 * NEG))
                ch.sync()
                chosen = t64[:, 0, :, :]
                ch.do(ts(chosen, sel[:, :, :], 1.5 * NEG, 0.0, ALU.is_lt, ALU.add))
                dve.tensor_copy(mask[:, :, :], chosen).then_inc(mask_ready, 1)
                ch.do(tt(gates[:, :, :], score[:, :, :], chosen, ALU.mult))
                ch.do(dve.tensor_reduce(tot[:, 0, :], gates[:, :, :], AX.X, ALU.add))
                ch.do(dve.reciprocal(tot[:, 1, :], tot[:, 0, :]))
                ch.do(ts(tot[:, 1, :], tot[:, 1, :], ROUTED_SCALE, 0.0, ALU.mult, ALU.add))
                tt(gates[:, :, :], gates[:, :, :], tot[:, 1, :].unsqueeze(2).broadcast_to(W), ALU.mult).then_inc(gates_ready, 1)
                for n in range(4):
                    share(n)
                split_lo(d_lo, d_raw, d_hi, 4)
                dve.wait_ge(pos_done, 1)
                ch.do(ts(t64[:, 1, :, :], ps_pos[:, :].rearrange("p (s e) -> p s e", s=NT), 1.0, 0.0, ALU.add, ALU.add))
                ch.do(tt(t64[:, 1, :, :], t64[:, 1, :, :], chosen, ALU.mult))
                ch.do(ts(tab["pos_m"][:, :, :], t64[:, 1, :, :], -1.0, 0.0, ALU.add, ALU.add))
                dve.wait_ge(cnt_done, 1)
                ch.do(dve.tensor_copy(cnt[:, 0:1], ps_t[0:NE, 0, 0:1]))
                for j in range(NX):
                    ch(ts(over[:, j:j + 1], cnt[:, 0:1], CAP * (j + 1) + 0.5, 0.0, ALU.is_gt, ALU.add))
                ch.sync()
                dve.tensor_reduce(cnt[:, 1:2], over[:, :], AX.X, ALU.add).then_inc(over_ready, 1)
                dve.wait_ge(place_done, 1)
                for j in range(NX):
                    ch(ts(place[:, j:j + 1], ps_t[0:NE, 0, 4:5], float(NE + j), 0.0, ALU.add, ALU.add))
                ch(ts(small[:, 0:1], ps_t[:, 0, 8:9], 0.5, 0.25, ALU.mult, ALU.add))
                ch(ts(small[:, 2:3], ps_t[:, 0, 8:9], float(NE), 0.0, ALU.add, ALU.add))
                ch.sync()
                ch.do(ts(small[:, 1:2], small[:, 0:1], ROUND, -ROUND, ALU.add, ALU.add))
                ch.do(ts(tab["loops"][0:1, :], small[0:1, 1:2], NE / 2 - 1, 0.0, ALU.add, ALU.add))
                ch(ts(onehot[:, 0, :], slot_n[0:NE, :], ecol[:, 0:1], None, ALU.is_equal))
                for j in range(NX):
                    ch(ts(onehot[:, j + 1, :], slot_n[0:NE, :], place[:, j:j + 1], over[:, j:j + 1], ALU.is_equal, ALU.mult))
                ch.sync()
                dve.sem_inc(place_ready, 1)
                dve.wait_ge(tab_done, 1)
                ch(dve.tensor_copy(tab["item_e"][:, :], ps_t[0:1, 1, 0:P]))
                ch.do(ts(tab["item_base"][:, :], slot_n[:, :], small[:, 2:3], 2048.0, ALU.is_ge, ALU.mult))
                ch.do(tt(tab["item_base"][:, :], tab["item_base"][:, :], ps_t[:, 1, P:2 * P], ALU.add))
                for s in range(NT):
                    dve.wait_ge(dn_done, s + 1)
                    dve.wait_ge(ld_x[s % 2], 16 * (NT // NB + s // 2 + 1))
                    if s >= 2:
                        dve.wait_ge(acc_out[s % 2], 16 * (s // 2))
                    dve.scalar_tensor_tensor(out=acc[:, s % 2, :], in0=x_in[:, s % 2, :], scalar=ALPHA,
                                             in1=ps_s[:, 2 * (s % 2):2 * (s % 2) + 2, :].rearrange("p h n -> p (h n)"),
                                             op0=ALU.mult, op1=ALU.add).then_inc(acc_ready, 1)


def experts(nc, m, cst, io, scr, tab):
    with ExitStack() as stack:
        a = Memory(nc, stack)
        XW = D + NE
        GATE, UP, DOWN = range(3)
        raw = [[a.sb(f"w_raw_{j}{w}", [P, 2048]) for w in range(3)] for j in range(2)]
        hi = [[a.sb(f"w_hi_{j}{w}", [P, 2048], F32R) for w in range(3)] for j in range(2)]
        lo = [[a.sb(f"w_lo_{j}{w}", [P, 2048], F32R) for w in range(3)] for j in range(2)]
        x_main = [a.sb(f"x_main_{j}", [P, XW]) for j in range(2)]
        x_rest = [a.sb(f"x_rest_{j}", [REST, XW]) for j in range(2)]
        xT = a.sb("xe", [P, KD, 2, CAP], F32R)
        cross = a.sb("e_cross", [P, 2, CAP])
        pre = a.sb("e_pre", [P, 2, CAP])
        silu, h = a.sb("e_silu", [P, 2, CAP]), a.sb("e_h", [P, 2, CAP])
        h_hi, h_lo = a.sb("e_h_hi", [P, 2, CAP], F32R), a.sb("e_h_lo", [P, 2, CAP], F32R)
        y_main = [a.sb(f"y_main_{j}", [P, D]) for j in range(2)]
        y_rest = [a.sb(f"y_rest_{j}", [REST, D]) for j in range(2)]
        g_main = [a.sb(f"g_main_{j}", [P, 1]) for j in range(2)]
        g_rest = [a.sb(f"g_rest_{j}", [REST, 1]) for j in range(2)]
        slots, here = a.sb("e_slots", [P, CAP]), a.sb("e_here", [P, CAP])
        sel = a.sb("e_sel", [P, NT, CAP], FP16)
        info = a.sb("e_info", [P, NT, 2], FP16)
        dummy = a.sb("e_dummy", [P, 2])
        neg_slot = a.sb("e_neg_slot", [P, 2])
        idx_f = a.sb("e_idx_f", [P, 2])
        idx_main = [a.sb(f"idx_main_{j}", [P, 1], I32) for j in range(2)]
        idx_rest = [a.sb(f"idx_rest_{j}", [REST, 1], I32) for j in range(2)]
        out_main = [a.sb(f"out_main_{j}", [P, 1], I32) for j in range(2)]
        out_rest = [a.sb(f"out_rest_{j}", [REST, 1], I32) for j in range(2)]
        ps_gu = a.ps("ps_gu", [P, 2, 512])
        ps_t = a.ps("ps_xt", [P, 3, 512])
        ps_y = a.ps("ps_ye", [P, 3, 512])
        IDX = 2 * CAP
        ld = [[a.sem(f"ld_e{j}{w}") for w in range(3)] for j in range(2)]
        (hi_made, lo_made, gu_done, cross_made, summed, silu_made, h_made, turned, xhi_made, xlo_made, y_done, y_evac, patterns,
         sel_ready, sums_done, idx_made, idx_kept, gate_kept, pool_sem, pool_held, dve_sem, dve_idx_sem) = (
            a.sem("ex_" + n) for n in
            ("hi", "lo", "gu", "cross", "summed", "silu", "h", "turned", "xhi", "xlo", "y_done", "y_evac", "patterns",
             "sel", "sums", "idx", "idx_kept", "gate_kept", "pool_ch", "pool_held", "dve_ch", "dve_idx"))
        gathered = [a.sem("gathered_0"), a.sem("gathered_1")]
        scattered = [a.sem("scattered_0"), a.sem("scattered_1")]
        ident = cst["ident"]
        src = [io["exp_w_gate"][0].rearrange("e (q k) n -> q e (k n)", k=KD),
               io["exp_w_up"][0].rearrange("e (q k) n -> q e (k n)", k=KD),
               io["exp_w_down"][0].rearrange("e (c p) n -> p e c n", p=P)]
        flat = lambda t: t[:, :]
        w3 = lambda t: t[:, :].rearrange("p (k n) -> p k n", k=KD)
        d3 = lambda t: t[:, :].rearrange("p (c n) -> p c n", c=2)

        with nc.Block() as block:
            @block.sync
            def _(sp):
                def load(n, j, wait=True):
                    e = sp.value_load(tab["item_e"][0:1, bass.ds(n, 1)], min_val=0, max_val=NE - 1)
                    for w in range(3):
                        if wait:
                            sp.wait_ge(lo_made, 6 * (n - 2) + 2 * w + 2)
                        if w == DOWN and not wait and j == 0:
                            sp.wait_ge(gathered[0], 32)
                        if w == DOWN:
                            sp.dma_start(d3(raw[j][w]).unsqueeze(1), src[w][:, bass.ds(e, 1), :, :]).then_inc(ld[j][w], 16)
                        else:
                            sp.dma_start(flat(raw[j][w]).unsqueeze(1), src[w][:, bass.ds(e, 1), :]).then_inc(ld[j][w], 16)

                load(0, 0, wait=False)
                load(1, 1, wait=False)
                loops = sp.value_load(tab["loops"][0:1, 0:1], min_val=NE // 2 - 1, max_val=57)
                with sp.Fori(1, loops + 1) as i:
                    for j in range(2):
                        load(2 * i + j, j)

            @block.gpsimd
            def _(pool):
                ch = Chain(pool, pool_sem)
                ch(pool.iota(slots[:, :], pattern=[[1, CAP]], base=0, channel_multiplier=0, allow_small_or_imprecise_dtypes=True))
                ch(pool.iota(info[:, :, 0], pattern=[[1, NT]], base=-L, channel_multiplier=NT, allow_small_or_imprecise_dtypes=True))
                ch(pool.iota(dummy[:, :], pattern=[[P, 2]], base=L, channel_multiplier=1, allow_small_or_imprecise_dtypes=True))
                ch(pool.iota(neg_slot[:, :], pattern=[[-P, 2]], base=0, channel_multiplier=-1, allow_small_or_imprecise_dtypes=True))
                ch.do(pool.memset(info[:, :, 1], 1.0))
                pool.sem_inc(patterns, 1)

                def hold(sem, value):
                    pool.wait_ge(sem, value)
                    pool.sem_inc(pool_held, 1)

                def gather(n, j, first=False):
                    hold(idx_made, n + 1)
                    if not first:
                        hold(turned, 3 * (n - 1))
                    for x, ix in ((x_main[j], idx_main[j]), (x_rest[j], idx_rest[j])):
                        pool.indirect_dma_start(out=x[:, :], out_offset=None, in_=scr["x1"][:, :],
                                                in_offset=bass.IndirectOffsetOnAxis(ap=ix[:, 0:1], axis=0)).then_inc(gathered[j], 16)

                def keep_gate(n, j, uses):
                    e = pool.value_load(tab["item_e"][0:1, bass.ds(n, 1)], min_val=0, max_val=NE - 1)
                    hold(gathered[j], 32 * uses)
                    pool.tensor_copy(g_main[j][:, :], x_main[j][:, bass.ds(e + D, 1)]).then_inc(gate_kept, 1)
                    pool.tensor_copy(g_rest[j][:, :], x_rest[j][:, bass.ds(e + D, 1)]).then_inc(gate_kept, 1)

                def keep_indices(j):
                    pool.tensor_copy(out_main[j][:, :], idx_main[j][:, :]).then_inc(idx_kept, 1)
                    pool.tensor_copy(out_rest[j][:, :], idx_rest[j][:, :]).then_inc(idx_kept, 1)

                def turn(n, j, ahead1, ahead2, pair):
                    keep_indices(j)
                    if ahead1:
                        keep_gate(n + 1, 1 - j, pair + 1 + (1 if j else 0))
                    if ahead2:
                        gather(n + 2, j)
                    hold(y_evac, 4 * n + 4)
                    hold(idx_kept, 2 * n + 2)
                    hold(scattered[1 - j], 32 * (pair + j))
                    for y, ix in ((y_main[j], out_main[j]), (y_rest[j], out_rest[j])):
                        pool.indirect_dma_start(out=scr["acc"][:, :], out_offset=bass.IndirectOffsetOnAxis(ap=ix[:, 0:1], axis=0),
                                                in_=y[:, :], in_offset=None, compute_op=ALU.add).then_inc(scattered[j], 16)

                for n in range(2):
                    gather(n, n, first=True)
                keep_gate(0, 0, 1)
                loops = pool.value_load(tab["loops"][0:1, 0:1], min_val=NE // 2 - 1, max_val=57)
                with pool.Fori(0, loops) as i:
                    for j in range(2):
                        turn(2 * i + j, j, True, True, i)
                turn(2 * loops, 0, True, False, loops)
                turn(2 * loops + 1, 1, False, False, loops)
                for j in range(2):
                    pool.wait_ge(scattered[j], 32 * (loops + 1))

            @block.tensor
            def _(pe):
                pe.wait_ge(patterns, 1)

                def sums(n):
                    pe.wait_ge(sel_ready, n + 1)
                    pe.wait_ge(idx_made, n)
                    for s in range(NT):
                        pe.matmul(ps_gu[:, 0, IDX:IDX + 2], sel[:, s, 0:P], info[:, s, :], start=(s == 0), stop=(s == NT - 1))
                    for s in range(NT):
                        ins = pe.matmul(ps_gu[0:REST, 0, IDX + 4:IDX + 6], sel[:, s, P:CAP], info[:, s, :], start=(s == 0), stop=(s == NT - 1))
                    ins.then_inc(sums_done, 1)

                def turn_rows(j, uses):
                    pe.wait_ge(gathered[j], 32 * uses)
                    for b in range(2):
                        for k in range(4):
                            ins = pe.transpose(ps_t[:, b, P * k:P * k + P], x_main[j][:, 4 * b + k:D:KD], ident[:, :])
                        ins.then_inc(turned, 1)
                    for k in range(KD):
                        ins = pe.transpose(ps_t[:, 2, REST * k:REST * k + REST], x_rest[j][:, k:D:KD], ident[0:REST, 0:REST])
                    ins.then_inc(turned, 1)

                def turn(n, j, ahead1, ahead2, pair):
                    pe.wait_ge(xlo_made, 3 * n + 3)
                    pe.wait_ge(lo_made, 6 * n + 4)
                    pe.wait_ge(idx_made, n + 2 if ahead1 else n + 1)
                    for c in range(2):
                        for w in (GATE, UP):
                            if c:
                                pe.wait_ge(summed, 4 * n + w + 1)
                            for k in range(KD):
                                cols = slice(P * c, P * c + P)
                                pe.matmul(ps_gu[:, w, 0:2 * CAP], w3(hi[j][w])[:, k, cols], xT[:, k, :, :],
                                          start=(k == 0), stop=False, skip_group_check=True)
                                ins = pe.matmul(ps_gu[:, w, 0:CAP], w3(lo[j][w])[:, k, cols], xT[:, k, 0, :],
                                                start=False, stop=(k == KD - 1), skip_group_check=True)
                            ins.then_inc(gu_done, 1)
                    if ahead1:
                        turn_rows(1 - j, pair + 1 + j)
                    if ahead2:
                        pe.wait_ge(summed, 4 * n + 3)
                        sums(n + 2)
                    pe.wait_ge(h_made, 2 * n + 2)
                    pe.wait_ge(lo_made, 6 * n + 6)
                    pe.wait_ge(y_evac, 4 * n)
                    for seg in range(4):
                        tok, rows = (slice(0, P), P) if seg < 2 else (slice(P, CAP), REST)
                        cols = slice(512 * (seg % 2), 512 * (seg % 2) + 512)
                        if seg == 3:
                            pe.wait_ge(y_evac, 4 * n + 1)
                        for c in range(2):
                            ins = mm3(pe, ps_y[0:rows, seg % 3, :], h_hi[:, c, tok], h_lo[:, c, tok],
                                      d3(hi[j][DOWN])[:, c, cols], d3(lo[j][DOWN])[:, c, cols], c == 0, c == 1)
                        ins.then_inc(y_done, 1)

                sums(0)
                sums(1)
                turn_rows(0, 1)
                loops = pe.value_load(tab["loops"][0:1, 0:1], min_val=NE // 2 - 1, max_val=57)
                with pe.Fori(0, loops) as i:
                    for j in range(2):
                        turn(2 * i + j, j, True, True, i)
                turn(2 * loops, 0, True, False, loops)
                turn(2 * loops + 1, 1, False, False, loops)

            @block.scalar
            def _(act):
                def split_hi(w, j, uses, piece):
                    if piece == 0:
                        act.wait_ge(ld[j][w], 16 * uses)
                    cols = slice(1024 * piece, 1024 * piece + 1024)
                    act.activation(hi[j][w][:, cols], raw[j][w][:, cols], ACT.Copy).then_inc(hi_made, 1)

                def rows_hi(n):
                    for b in range(3):
                        act.wait_ge(turned, 3 * n + b + 1)
                        if b < 2:
                            out, in_ = xT[:, 4 * b:4 * b + 4, 0, 0:P], ps_t[:, b, :].rearrange("p (k t) -> p k t", k=4)
                        else:
                            out, in_ = xT[:, :, 0, P:CAP], ps_t[:, 2, 0:KD * REST].rearrange("p (k t) -> p k t", k=KD)
                        act.activation(out, in_, ACT.Copy).then_inc(xhi_made, 1)

                def turn(n, j, ahead1, ahead2, pair):
                    uses = pair + 1 + j
                    def low_products(g):
                        act.wait_ge(gu_done, 4 * n + g + 1)
                        act.activation(cross[:, g % 2, :], ps_gu[:, g % 2, CAP:2 * CAP], ACT.Copy).then_inc(cross_made, 1)

                    def gated(c):
                        act.wait_ge(summed, 4 * n + 2 * c + 1)
                        act.activation(silu[:, c, :], pre[:, GATE, :], ACT.Silu).then_inc(silu_made, 1)

                    if ahead1:
                        split_hi(GATE, 1 - j, uses, 0)
                        split_hi(GATE, 1 - j, uses, 1)
                    low_products(0)
                    if ahead1:
                        split_hi(UP, 1 - j, uses, 0)
                    gated(0)
                    low_products(1)
                    if ahead1:
                        split_hi(UP, 1 - j, uses, 1)
                    low_products(2)
                    gated(1)
                    low_products(3)
                    if ahead1:
                        rows_hi(n + 1)
                    act.wait_ge(gate_kept, 2 * n + 2)
                    act.wait_ge(scattered[j], 32 * pair)
                    for seg in range(4):
                        if ahead1 and seg < 2:
                            split_hi(DOWN, 1 - j, uses, seg)
                        act.wait_ge(y_done, 4 * n + seg + 1)
                        cols = slice(512 * (seg % 2), 512 * (seg % 2) + 512)
                        y, g, rows = (y_main, g_main, P) if seg < 2 else (y_rest, g_rest, REST)
                        act.activation(y[j][:, cols], ps_y[0:rows, seg % 3, :], ACT.Copy, scale=g[j][:, 0:1]).then_inc(y_evac, 1)

                for w in range(3):
                    if w == DOWN:
                        rows_hi(0)
                    for piece in range(2):
                        split_hi(w, 0, 1, piece)
                loops = act.value_load(tab["loops"][0:1, 0:1], min_val=NE // 2 - 1, max_val=57)
                with act.Fori(0, loops) as i:
                    for j in range(2):
                        turn(2 * i + j, j, True, True, i)
                turn(2 * loops, 0, True, False, loops)
                turn(2 * loops + 1, 1, False, False, loops)

            @block.vector
            def _(dve):
                tt = dve.tensor_tensor
                ch, chi = Chain(dve, dve_sem), Chain(dve, dve_idx_sem)
                dve.wait_ge(patterns, 1)

                def split_lo(n, w, j, piece):
                    dve.wait_ge(hi_made, 6 * n + 2 * w + piece + 1)
                    cols = slice(1024 * piece, 1024 * piece + 1024)
                    tt(lo[j][w][:, cols], raw[j][w][:, cols], hi[j][w][:, cols].bitcast(F32), ALU.subtract).then_inc(lo_made, 1)

                def rows_lo(n):
                    for b in range(3):
                        dve.wait_ge(xhi_made, 3 * n + b + 1)
                        if b < 2:
                            view, in_ = (lambda part: xT[:, 4 * b:4 * b + 4, part, 0:P]), ps_t[:, b, :].rearrange("p (k t) -> p k t", k=4)
                        else:
                            view, in_ = (lambda part: xT[:, :, part, P:CAP]), ps_t[:, 2, 0:KD * REST].rearrange("p (k t) -> p k t", k=KD)
                        tt(view(1), in_, view(0).bitcast(F32), ALU.subtract).then_inc(xlo_made, 1)

                def select(n):
                    e = dve.value_load(tab["item_e"][0:1, bass.ds(n, 1)], min_val=0, max_val=NE - 1)
                    chi.do(tt(here[:, :], slots[:, :], tab["item_base"][:, bass.ds(n, 1)].broadcast_to((P, CAP)), ALU.add))
                    tt(sel[:, :, :], tab["pos_m"][:, :, bass.ds(e, 1)].broadcast_to((P, NT, CAP)),
                       here[:, :].unsqueeze(1).broadcast_to((P, NT, CAP)), ALU.is_equal).then_inc(sel_ready, 1)

                def indices(n, j):
                    dve.wait_ge(sums_done, n + 1)
                    for c, (rows, out) in enumerate(((P, idx_main[j]), (REST, idx_rest[j]))):
                        number, taken = (ps_gu[0:rows, 0, IDX + 4 * c + i:IDX + 4 * c + i + 1] for i in range(2))
                        chi.do(dve.tensor_scalar(idx_f[0:rows, c:c + 1], taken, neg_slot[0:rows, c:c + 1], dummy[0:rows, c:c + 1],
                                                 ALU.mult, ALU.add))
                        ins = tt(out[:, :], idx_f[0:rows, c:c + 1], number, ALU.add)
                        if c == 0:
                            chi(ins)
                        else:
                            chi.sync()
                            ins.then_inc(idx_made, 1)

                def add_cross(n, g):
                    dve.wait_ge(cross_made, 4 * n + g + 1)
                    tt(pre[:, g % 2, :], ps_gu[:, g % 2, 0:CAP], cross[:, g % 2, :], ALU.add).then_inc(summed, 1)

                def hidden(n, c):
                    dve.wait_ge(summed, 4 * n + 2 * c + 2)
                    dve.wait_ge(silu_made, 2 * n + c + 1)
                    ch.do(tt(h[:, c, :], silu[:, c, :], pre[:, UP, :], ALU.mult))
                    ch.do(dve.tensor_copy(h_hi[:, c, :], h[:, c, :]))
                    tt(h_lo[:, c, :], h[:, c, :], h_hi[:, c, :].bitcast(F32), ALU.subtract).then_inc(h_made, 1)

                def turn(n, j, ahead1, ahead2):
                    if ahead2:
                        select(n + 2)
                    for g in range(4):
                        if ahead1 and g < 3:
                            split_lo(n + 1, g // 2, 1 - j, g % 2)
                        add_cross(n, g)
                        if g % 2:
                            hidden(n, g // 2)
                    if ahead1:
                        rows_lo(n + 1)
                    if ahead2:
                        dve.wait_ge(idx_kept, 2 * n + 2)
                        indices(n + 2, j)
                    if ahead1:
                        split_lo(n + 1, UP, 1 - j, 1)
                        for piece in range(2):
                            split_lo(n + 1, DOWN, 1 - j, piece)

                for n in range(2):
                    select(n)
                    indices(n, n)
                for w in range(3):
                    if w == DOWN:
                        rows_lo(0)
                    for piece in range(2):
                        split_lo(0, w, 0, piece)
                loops = dve.value_load(tab["loops"][0:1, 0:1], min_val=NE // 2 - 1, max_val=57)
                with dve.Fori(0, loops) as i:
                    ch.loop(i, 8)
                    chi.loop(i, 8)
                    for j in range(2):
                        turn(2 * i + j, j, True, True)
                ch.end_loop(loops)
                chi.end_loop(loops)
                turn(2 * loops, 0, True, False)
                turn(2 * loops + 1, 1, False, False)


def output_norm(nc, m, io, scr, out):
    with ExitStack() as stack:
        a = Memory(nc, stack)
        rows = a.sb("ln2_rows", [P, NT, D])
        norm = LayerNorm(a, "ln2", lambda s: rows[:, s, :])
        ld = [a.sem(f"ld_acc{s}") for s in range(NT)]
        stored, dve_sem = a.sem("ln2_stored"), a.sem("ln2_dve_ch")
        acc_d = scr["acc"][0:L, :].rearrange("(p s) d -> p s d", s=NT)
        out_d = out[0].rearrange("(p s) d -> p s d", s=NT)
        with nc.Block() as block:
            @block.sync
            def _(sp):
                for s in range(NT):
                    sp.dma_start(rows[:, s, :], acc_d[:, s, :]).then_inc(ld[s], 16)
                    if s == 1:
                        norm.load(sp, io["ln2_g"], io["ln2_b"])
                for s in range(NT):
                    sp.wait_ge(norm.ready, s + 1)
                    sp.dma_start(out_d[:, s, :], rows[:, s, :]).then_inc(stored, 16)
                sp.wait_ge(stored, 16 * NT)

            @block.scalar
            def _(act):
                for s in range(NT + 1):
                    if s < NT:
                        norm.root_of(act, s)
                    if s >= 1:
                        norm.normalise(act, s - 1)

            @block.vector
            def _(dve):
                ch = Chain(dve, dve_sem)
                for s in range(NT + 2):
                    if s < NT:
                        dve.wait_ge(ld[s], 16)
                        norm.statistics(dve, ch, s)
                    if 1 <= s <= NT:
                        norm.scales(dve, ch, s - 1)
                    if s >= 2:
                        if s == 2:
                            dve.wait_ge(norm.loaded, 32)
                        norm.times_gain(dve, s - 2)

            @block.gpsimd
            def _(pool):
                pool.wait_ge(norm.loaded, 32)
                for s in range(NT):
                    norm.plus_shift(pool, s)


def hybrid_layer(nc, io, scr, out):
    with ExitStack() as stack:
        m = Memory(nc, stack)
        cst, cst["write"] = constants(nc, m)
        with ExitStack() as mixer:
            a = Memory(nc, mixer)
            merged = a.sb("merged", [P, KD, L])
            keep = {"bias_T": a.sb("bias_T", [P, NB_COL]), "ut_all": merged[:, 0:4, :].rearrange("p a b -> p (a b)")}
            y_T = merged[:, 0:4, :]
            y_tok = merged[:, 4:8, :].rearrange("p a (b c) -> p (a b) c", b=2)
            keep["u_tok"] = y_tok
            with ExitStack() as branches:
                b = Memory(nc, branches)
                xT_hi, xT_lo = b.sb("xT_hi", [P, KD, L], F32R), b.sb("xT_lo", [P, KD, L], F32R)
                keep["states"] = b.sb("states", [P, 2, PAIRS, NCH + 1])
                keep["scan_fac"] = b.sb("scan_fac", [P, 2, 2 * PAIRS])
                mixer_input(nc, b, cst, io, xT_hi, xT_lo, keep, scr)
                attention(nc, b, cst, io, xT_hi, xT_lo, keep, scr)
                ya = [b.sb("ya_" + n, [P, 4, L], F32R) for n in ("hi", "lo")]
                branch_outputs(nc, b, cst, io, keep, scr, ya[0], ya[1], y_tok)
                y2 = [b.sb("y2_" + n, [P, 4, L], F32R) for n in ("hi", "lo")]
                gated_ssm(nc, b, cst, io, y_tok, y_T, y2[0], y2[1])
                merge(nc, b, cst, io, xT_hi, xT_lo, y2, ya, keep, merged)
            output_projection(nc, a, cst, io, merged, scr)
        tab = {"pos_m": m.sb("pos_m", [P, NT, NE]), "item_e": m.sb("item_e", [1, P], I32),
               "item_base": m.sb("item_base", [P, P]), "loops": m.sb("loops", [1, 1], I32)}
        route_and_share(nc, m, cst, io, scr, tab)
        experts(nc, m, cst, io, scr, tab)
        output_norm(nc, m, io, scr, out)


def kernel(**inputs):
    import concourse.bacc as _bacc
    from concourse.bass_utils import run_bass_kernel_spmd as _run

    nc = _bacc.Bacc("TRN2", target_bir_lowering=False, num_devices=1)
    arrays, io = {}, {}
    for name, value in inputs.items():
        arr = np.ascontiguousarray(value)
        arrays["in_" + name] = arr
        io[name] = nc.dram_tensor("in_" + name, arr.shape, mybir.dt.from_np(arr.dtype), kind="ExternalInput").ap()
    out = nc.dram_tensor("out_0", (1, L, D), F32, kind="ExternalOutput").ap()
    scr = {"c_pow": nc.dram_tensor("scr_c_pow", (P, 2 * PAIRS * (T + 1) * SSM_C), F32).ap(),
           "k_pad": nc.dram_tensor("scr_k_pad", (SSM_C, SSM_G, KP0 + P), F32).ap(),
           "att": nc.dram_tensor("scr_att", (NG, L, NH * ROW), F32).ap(),
           "x1": nc.dram_tensor("scr_x1", (L + CAP, D + NE), F32).ap(),
           "acc": nc.dram_tensor("scr_acc", (L + CAP, D), F32).ap()}
    hybrid_layer(nc, io, scr, out)
    r = _run(nc, [arrays], core_ids=[0])
    return r.results[0]["out_0"]
```
